# Optimizing a Trainium2 kernel written in Bass

```python
import math
import jax, jax.numpy as jnp
from jax import lax
import numpy as np

D_MODEL = 1024
BATCH = 1
SEQ = 256
DEPTH = 2

N_MIXERS = 2
N_A_LAYERS = (DEPTH + 1) // 2
N_B_LAYERS = DEPTH // 2
DA_HEADS = 8
DA_HEAD_DIM = 64
DA_V_DIM = 2 * DA_HEAD_DIM
Q_BLOCK = 128
REL_BUCKETS = 32
REL_MAX_EXACT = REL_BUCKETS // 2
REL_MAX_DIST = 128
SGU_CHUNK = 128
SGU_WIDTH = D_MODEL
SGU_GROUPS = 8
SGU_GROUP_DIM = SGU_WIDTH // SGU_GROUPS
D_FF = 2816
N_MOD = 9
EPS = 1e-6
NEG_INF = -1e30


def rms_norm(x, g):
    x32 = x.astype(jnp.float32)
    y = x32 * lax.rsqrt(jnp.mean(x32 * x32, axis=-1, keepdims=True) + EPS)
    return (y * g.astype(jnp.float32)).astype(x.dtype)

def layer_norm(x, g, b):
    x32 = x.astype(jnp.float32)
    mu = jnp.mean(x32, axis=-1, keepdims=True)
    xc = x32 - mu
    y = xc * lax.rsqrt(jnp.mean(xc * xc, axis=-1, keepdims=True) + EPS)
    return (y * g.astype(jnp.float32) + b.astype(jnp.float32)).astype(x.dtype)

def modulate(h, shift, scale):
    return h * (1.0 + scale[:, None, :]) + shift[:, None, :]

def swiglu(h, wg, wu, wd):
    return (jax.nn.silu(h @ wg) * (h @ wu)) @ wd

def t5_bucket(rel):
    n = jnp.maximum(rel, 0)
    nf = jnp.maximum(n, 1).astype(jnp.float32)
    large = REL_MAX_EXACT + (jnp.log(nf / REL_MAX_EXACT) / math.log(REL_MAX_DIST / REL_MAX_EXACT)
                             * (REL_BUCKETS - REL_MAX_EXACT)).astype(jnp.int32)
    large = jnp.minimum(large, REL_BUCKETS - 1)
    return jnp.where(n < REL_MAX_EXACT, n, large)

def diff_attention(h, w_qkv, q_g, k_g, lq1, lk1, lq2, lk2, subln_g, w_o, rel_bias, lambda_init):
    B, S, _ = h.shape
    q, k, v = jnp.split(h @ w_qkv, 3, axis=-1)
    q = rms_norm(q.reshape(B, S, DA_HEADS, 2, DA_HEAD_DIM), q_g)
    k = rms_norm(k.reshape(B, S, DA_HEADS, 2, DA_HEAD_DIM), k_g)
    v32 = v.reshape(B, S, DA_HEADS, DA_V_DIM).astype(jnp.float32)
    k32 = k.astype(jnp.float32)
    f32 = jnp.float32
    lam = (jnp.exp(jnp.sum(lq1.astype(f32) * lk1.astype(f32)))
           - jnp.exp(jnp.sum(lq2.astype(f32) * lk2.astype(f32))) + lambda_init)
    scale = 1.0 / math.sqrt(DA_HEAD_DIM)
    nb = S // Q_BLOCK
    qb = q.reshape(B, nb, Q_BLOCK, DA_HEADS, 2, DA_HEAD_DIM).transpose(1, 0, 2, 3, 4, 5)
    k_pos = jnp.arange(S, dtype=jnp.int32)
    table = rel_bias.astype(f32)

    def block(args):
        q_blk, bi = args
        q_pos = bi * Q_BLOCK + jnp.arange(Q_BLOCK, dtype=jnp.int32)
        rel = q_pos[:, None] - k_pos[None, :]
        bias = jnp.where((rel >= 0)[..., None], table[t5_bucket(rel)], NEG_INF)
        bias = bias.transpose(2, 0, 1)
        logits = jnp.einsum('bqhcd,bkhcd->bhcqk', q_blk.astype(f32), k32) * scale + bias[None, :, None]
        p = jax.nn.softmax(logits, axis=-1)
        attn = p[:, :, 0] - lam * p[:, :, 1]
        o = jnp.einsum('bhqk,bkhe->bqhe', attn, v32)
        o = rms_norm(o, subln_g) * (1.0 - lambda_init)
        return o.reshape(B, Q_BLOCK, DA_HEADS * DA_V_DIM).astype(h.dtype)

    out = lax.map(block, (qb, jnp.arange(nb, dtype=jnp.int32)))
    out = out.transpose(1, 0, 2, 3).reshape(B, S, DA_HEADS * DA_V_DIM)
    return out @ w_o

def spatial_gating(h, w_in, ln_g, ln_b, w_s, b_s, w_out):
    B, S, _ = h.shape
    z = jax.nn.gelu(h @ w_in, approximate=False)
    u, v = jnp.split(z, 2, axis=-1)
    v = layer_norm(v, ln_g, ln_b)
    nc = S // SGU_CHUNK
    v = v.reshape(B, nc, SGU_CHUNK, SGU_GROUPS, SGU_GROUP_DIM)
    causal = jnp.tril(jnp.ones((SGU_CHUNK, SGU_CHUNK), dtype=w_s.dtype))
    mixed = jnp.einsum('gts,bnsgc->bntgc', w_s * causal, v) + b_s.T[:, :, None]
    gated = u * mixed.reshape(B, S, SGU_WIDTH)
    return gated @ w_out

def _normal(k, shape, std):
    return jax.random.normal(k, shape, jnp.float32) * std

def first_inputs(seed: int = 0) -> dict:
    key = jax.random.key(seed)
    ks = jax.random.split(key, 32)
    D, F = D_MODEL, D_FF
    gain = lambda k, shape: 1.0 + _normal(k, shape, 0.1)
    return {
        'x': _normal(ks[0], (BATCH, SEQ, D), 1.0),
        'c': _normal(ks[1], (BATCH, D), 1.0),
        'rel_bias': _normal(ks[2], (REL_BUCKETS, DA_HEADS), 0.5),
        'ada_w': _normal(ks[3], (DEPTH, D, N_MOD * D), 0.5 * D ** -0.5),
        'ada_b': _normal(ks[4], (DEPTH, N_MOD * D), 0.02),
        'ln_ffn1': gain(ks[5], (DEPTH, D)),
        'ffn1_wg': _normal(ks[6], (DEPTH, D, F), D ** -0.5),
        'ffn1_wu': _normal(ks[7], (DEPTH, D, F), D ** -0.5),
        'ffn1_wd': _normal(ks[8], (DEPTH, F, D), F ** -0.5),
        'ln_mix': gain(ks[9], (DEPTH, D)),
        'ln_ffn2': gain(ks[10], (DEPTH, D)),
        'ffn2_wg': _normal(ks[11], (DEPTH, D, F), D ** -0.5),
        'ffn2_wu': _normal(ks[12], (DEPTH, D, F), D ** -0.5),
        'ffn2_wd': _normal(ks[13], (DEPTH, F, D), F ** -0.5),
        'ln_out': gain(ks[14], (DEPTH, D)),
        'attn_w_qkv': _normal(ks[15], (N_A_LAYERS, D, 3 * D), D ** -0.5),
        'attn_q_norm': gain(ks[16], (N_A_LAYERS, DA_HEAD_DIM)),
        'attn_k_norm': gain(ks[17], (N_A_LAYERS, DA_HEAD_DIM)),
        'attn_lq1': _normal(ks[18], (N_A_LAYERS, DA_HEAD_DIM), 0.1),
        'attn_lk1': _normal(ks[19], (N_A_LAYERS, DA_HEAD_DIM), 0.1),
        'attn_lq2': _normal(ks[20], (N_A_LAYERS, DA_HEAD_DIM), 0.1),
        'attn_lk2': _normal(ks[21], (N_A_LAYERS, DA_HEAD_DIM), 0.1),
        'attn_subln': gain(ks[22], (N_A_LAYERS, DA_V_DIM)),
        'attn_w_o': _normal(ks[23], (N_A_LAYERS, D, D), D ** -0.5),
        'sgu_w_in': _normal(ks[24], (N_B_LAYERS, D, 2 * SGU_WIDTH), D ** -0.5),
        'sgu_ln_g': gain(ks[25], (N_B_LAYERS, SGU_WIDTH)),
        'sgu_ln_b': _normal(ks[26], (N_B_LAYERS, SGU_WIDTH), 0.02),
        'sgu_w_s': _normal(ks[27], (N_B_LAYERS, SGU_GROUPS, SGU_CHUNK, SGU_CHUNK), SGU_CHUNK ** -0.5),
        'sgu_b_s': gain(ks[28], (N_B_LAYERS, SGU_GROUPS, SGU_CHUNK)),
        'sgu_w_out': _normal(ks[29], (N_B_LAYERS, SGU_WIDTH, D), SGU_WIDTH ** -0.5),
    }

def first_block(x, c, rel_bias, ada_w, ada_b, ln_ffn1, ffn1_wg, ffn1_wu, ffn1_wd, ln_mix,
              ln_ffn2, ffn2_wg, ffn2_wu, ffn2_wd, ln_out, attn_w_qkv, attn_q_norm, attn_k_norm,
              attn_lq1, attn_lk1, attn_lq2, attn_lk2, attn_subln, attn_w_o, sgu_w_in, sgu_ln_g,
              sgu_ln_b, sgu_w_s, sgu_b_s, sgu_w_out):
    c_act = jax.nn.silu(c)
    for i in range(DEPTH):
        mod = c_act @ ada_w[i] + ada_b[i]
        sh1, sc1, g1, sh2, sc2, g2, sh3, sc3, g3 = jnp.split(mod, N_MOD, axis=-1)
        h = modulate(rms_norm(x, ln_ffn1[i]), sh1, sc1)
        x = x + 0.5 * g1[:, None, :] * swiglu(h, ffn1_wg[i], ffn1_wu[i], ffn1_wd[i])
        h = modulate(rms_norm(x, ln_mix[i]), sh2, sc2)
        j = i // N_MIXERS
        if i % N_MIXERS == 0:
            lambda_init = 0.8 - 0.6 * math.exp(-0.3 * i)
            mix = diff_attention(h, attn_w_qkv[j], attn_q_norm[j], attn_k_norm[j], attn_lq1[j],
                                 attn_lk1[j], attn_lq2[j], attn_lk2[j], attn_subln[j], attn_w_o[j],
                                 rel_bias, lambda_init)
        else:
            mix = spatial_gating(h, sgu_w_in[j], sgu_ln_g[j], sgu_ln_b[j], sgu_w_s[j], sgu_b_s[j],
                                 sgu_w_out[j])
        x = x + g2[:, None, :] * mix
        h = modulate(rms_norm(x, ln_ffn2[i]), sh3, sc3)
        x = x + 0.5 * g3[:, None, :] * swiglu(h, ffn2_wg[i], ffn2_wu[i], ffn2_wd[i])
        x = rms_norm(x, ln_out[i])
    return x


NEG_INF_2 = -1e30
HG_HEADS = 8
HG_DK = 128
HG_DV = D_MODEL // HG_HEADS
HG_CHUNK = 64
NSA_HEADS = 16
NSA_KV = 4
NSA_GROUP = NSA_HEADS // NSA_KV
NSA_HD = D_MODEL // NSA_HEADS
CMP_LEN = 32
CMP_STRIDE = 16
SEL_LEN = 64
SEL_TOPK = 16
WINDOW = 512
Q_BLOCK_2 = 32
FORCED_SCORE = 1e4
CONV_W = 3


def rmsnorm(x, g):
    xf = x.astype(jnp.float32)
    y = xf * lax.rsqrt(jnp.mean(xf * xf, axis=-1, keepdims=True) + EPS)
    return (y * g).astype(x.dtype)

def alibi_slopes(n):
    return jnp.asarray([2.0 ** (-8.0 * (h + 1) / n) for h in range(n)], jnp.float32)

def hgrn2_mixer(h, w_in, w_out, g_norm, lb):
    B, S, _ = h.shape
    fd = HG_HEADS * HG_DK
    proj = h @ w_in
    q, f_pre, i_in, g = jnp.split(proj, [fd, 2 * fd, 2 * fd + D_MODEL], axis=-1)
    f_pre = f_pre.astype(jnp.float32)
    log_f = jnp.log(lb + (1.0 - lb) * jax.nn.sigmoid(f_pre))
    k = (1.0 - lb) * jax.nn.sigmoid(-f_pre)
    n = S // HG_CHUNK

    def chunks(t, d):
        return t.astype(jnp.float32).reshape(B, n, HG_CHUNK, HG_HEADS, d).transpose(1, 0, 3, 2, 4)

    xs = (chunks(q, HG_DK), chunks(k, HG_DK), chunks(i_in, HG_DV), chunks(log_f, HG_DK))
    causal = jnp.tril(jnp.ones((HG_CHUNK, HG_CHUNK), bool))[:, :, None]

    def step(state, inp):
        qc, kc, vc, lfc = inp
        b = jnp.cumsum(lfc, axis=2)
        o_inter = jnp.einsum('bhtk,bhkv->bhtv', qc * jnp.exp(b), state)
        diff = b[:, :, :, None, :] - b[:, :, None, :, :]
        decay = jnp.exp(jnp.where(causal, diff, NEG_INF_2))
        scores = jnp.einsum('bhtk,bhsk,bhtsk->bhts', qc, kc, decay)
        o_intra = jnp.einsum('bhts,bhsv->bhtv', scores, vc)
        b_last = b[:, :, -1:, :]
        state = state * jnp.exp(b_last[:, :, 0, :, None]) + jnp.einsum(
            'bhsk,bhsv->bhkv', kc * jnp.exp(b_last - b), vc)
        return state, o_inter + o_intra

    s0 = jnp.zeros((B, HG_HEADS, HG_DK, HG_DV), jnp.float32)
    _, o = lax.scan(step, s0, xs)
    o = o.transpose(1, 0, 3, 2, 4).reshape(B, S, HG_HEADS, HG_DV)
    o = rmsnorm(o, g_norm).reshape(B, S, D_MODEL)
    o = o * jax.nn.silu(g.astype(jnp.float32))
    return o.astype(h.dtype) @ w_out

def nsa_mixer(h, w_in, w_out, cmp_pe, cmp_w1, cmp_w2):
    B, S, _ = h.shape
    G, HPG, HD = NSA_KV, NSA_GROUP, NSA_HD
    nc = (S - CMP_LEN) // CMP_STRIDE + 1
    ns = S // SEL_LEN
    k_sel_n = min(SEL_TOPK, ns)
    kvd = G * HD
    split_at = [D_MODEL + j * kvd for j in range(7)]
    q, k_c, v_c, k_s, v_s, k_w, v_w, gate = jnp.split(h @ w_in, split_at, axis=-1)
    q = q.reshape(B, S, G, HPG, HD)
    gate = jax.nn.sigmoid(gate.astype(jnp.float32)).reshape(B, S, G, HPG, 3)

    def kv(t):
        return t.reshape(B, S, G, HD)

    cidx = (np.arange(nc) * CMP_STRIDE)[:, None] + np.arange(CMP_LEN)[None, :]

    def compress(t, pe, w1, w2):
        blocks = kv(t)[:, cidx] + pe[None, None, :, None, :]
        blocks = blocks.transpose(0, 1, 3, 2, 4).reshape(B, nc, G, CMP_LEN * HD)
        return jax.nn.silu(blocks @ w1) @ w2

    kc = compress(k_c, cmp_pe[0], cmp_w1[0], cmp_w2[0])
    vc = compress(v_c, cmp_pe[1], cmp_w1[1], cmp_w2[1])
    cmp_end = jnp.asarray(np.arange(nc) * CMP_STRIDE + CMP_LEN - 1, jnp.int32)
    cmp_mid = jnp.asarray(np.arange(nc) * CMP_STRIDE + (CMP_LEN - 1) / 2.0, jnp.float32)
    ci = np.arange(nc)[:, None] * CMP_STRIDE
    sj = np.arange(ns)[None, :] * SEL_LEN
    overlap = jnp.asarray((ci <= sj + SEL_LEN - 1) & (ci + CMP_LEN - 1 >= sj), jnp.float32)

    ks_blk = kv(k_s).reshape(B, ns, SEL_LEN, G, HD).transpose(0, 3, 1, 2, 4)
    vs_blk = kv(v_s).reshape(B, ns, SEL_LEN, G, HD).transpose(0, 3, 1, 2, 4)
    pad = ((0, 0), (WINDOW, 0), (0, 0), (0, 0))
    kw_pad = jnp.pad(kv(k_w), pad)
    vw_pad = jnp.pad(kv(v_w), pad)

    slopes = alibi_slopes(NSA_HEADS).reshape(G, HPG)
    scale = HD ** -0.5
    blk_ids = jnp.arange(ns)
    bi = jnp.arange(B)[:, None, None, None]
    gi = jnp.arange(G)[None, :, None, None]

    def block(i):
        q0 = i * Q_BLOCK_2
        t = q0 + jnp.arange(Q_BLOCK_2)
        qb = lax.dynamic_slice_in_dim(q, q0, Q_BLOCK_2, axis=1)
        gb = lax.dynamic_slice_in_dim(gate, q0, Q_BLOCK_2, axis=1)
        s_c = jnp.einsum('bqghd,bngd->bghqn', qb, kc, preferred_element_type=jnp.float32) * scale
        dist_c = t[:, None].astype(jnp.float32) - cmp_mid[None, :]
        s_c = s_c - slopes[None, :, :, None, None] * dist_c
        valid_c = cmp_end[None, :] <= t[:, None]
        p_c = jax.nn.softmax(jnp.where(valid_c, s_c, NEG_INF_2), axis=-1)
        p_c = p_c * (t >= CMP_LEN - 1).astype(jnp.float32)[None, None, None, :, None]
        o_c = jnp.einsum('bghqn,bngd->bqghd', p_c, vc)
        imp = jnp.einsum('bghqn,nj->bgqj', p_c, overlap)
        cur = t // SEL_LEN
        valid_s = blk_ids[None, :] * SEL_LEN <= t[:, None]
        forced = ((blk_ids[None, :] == 0) | (blk_ids[None, :] == cur[:, None])
                  | (blk_ids[None, :] == cur[:, None] - 1)) & valid_s
        score = jnp.where(forced, FORCED_SCORE, jnp.where(valid_s, imp, -1.0))
        _, idx = lax.top_k(score, k_sel_n)
        k_sel = ks_blk[bi, gi, idx]
        v_sel = vs_blk[bi, gi, idx].reshape(B, G, Q_BLOCK_2, k_sel_n * SEL_LEN, HD)
        pos = idx[..., None] * SEL_LEN + jnp.arange(SEL_LEN)
        s_s = jnp.einsum('bqghd,bgqkld->bghqkl', qb, k_sel, preferred_element_type=jnp.float32) * scale
        dist_s = (t[None, None, :, None, None] - pos).astype(jnp.float32)
        s_s = s_s - slopes[None, :, :, None, None, None] * dist_s[:, :, None]
        mask_s = (pos <= t[None, None, :, None, None])[:, :, None]
        s_s = jnp.where(mask_s, s_s, NEG_INF_2).reshape(B, G, HPG, Q_BLOCK_2, k_sel_n * SEL_LEN)
        o_s = jnp.einsum('bghqm,bgqmd->bqghd', jax.nn.softmax(s_s, axis=-1), v_sel)
        kw = lax.dynamic_slice_in_dim(kw_pad, q0, Q_BLOCK_2 + WINDOW, axis=1)
        vw = lax.dynamic_slice_in_dim(vw_pad, q0, Q_BLOCK_2 + WINDOW, axis=1)
        s_pos = q0 - WINDOW + jnp.arange(Q_BLOCK_2 + WINDOW)
        s_w = jnp.einsum('bqghd,bsgd->bghqs', qb, kw, preferred_element_type=jnp.float32) * scale
        s_w = s_w - slopes[None, :, :, None, None] * (t[:, None] - s_pos[None, :]).astype(jnp.float32)
        mask_w = (s_pos[None, :] <= t[:, None]) & (s_pos[None, :] > t[:, None] - WINDOW) & (s_pos[None, :] >= 0)
        o_w = jnp.einsum('bghqs,bsgd->bqghd', jax.nn.softmax(jnp.where(mask_w, s_w, NEG_INF_2), axis=-1), vw)
        return gb[..., 0, None] * o_c + gb[..., 1, None] * o_s + gb[..., 2, None] * o_w

    o = lax.map(block, jnp.arange(S // Q_BLOCK_2))
    o = o.transpose(1, 0, 2, 3, 4, 5).reshape(B, S, D_MODEL)
    return o.astype(h.dtype) @ w_out

def conv_ffn(h, w_up, conv_w, conv_b, w_down):
    a, v = jnp.split(h @ w_up, 2, axis=-1)
    a = lax.conv_general_dilated(a, conv_w[:, None, :].astype(a.dtype), window_strides=(1,),
                                 padding=[(CONV_W - 1, 0)], dimension_numbers=('NWC', 'WIO', 'NWC'),
                                 feature_group_count=D_FF) + conv_b
    return (jax.nn.silu(a) * v) @ w_down

def second_inputs(seed: int = 0) -> dict:
    key = jax.random.key(seed)
    ks = jax.random.split(key, 24)
    n_a = (DEPTH + 1) // 2
    n_b = DEPTH // 2
    D = D_MODEL
    nsa_in = D + 6 * NSA_KV * NSA_HD + 3 * NSA_HEADS

    def nrm(k, shape, s):
        return jax.random.normal(k, shape, jnp.float32) * s

    return {
        'x': nrm(ks[0], (BATCH, SEQ, D), 1.0),
        'c': nrm(ks[1], (BATCH, D), 1.0),
        'ada_w': nrm(ks[2], (DEPTH, D, 6 * D), 0.5 * D ** -0.5),
        'ada_b': nrm(ks[3], (DEPTH, 6 * D), 0.02),
        'norm_mix': 1.0 + nrm(ks[4], (DEPTH, D), 0.02),
        'norm_ffn': 1.0 + nrm(ks[5], (DEPTH, D), 0.02),
        'final_norm': 1.0 + nrm(ks[6], (D,), 0.02),
        'hg_w_in': nrm(ks[7], (n_a, D, 2 * HG_HEADS * HG_DK + 2 * D), D ** -0.5),
        'hg_w_out': nrm(ks[8], (n_a, D, D), D ** -0.5),
        'hg_gnorm': 1.0 + nrm(ks[9], (n_a, HG_DV), 0.02),
        'hg_lb': nrm(ks[10], (n_a + 1, HG_HEADS * HG_DK), 0.5),
        'nsa_w_in': nrm(ks[11], (n_b, D, nsa_in), D ** -0.5),
        'nsa_w_out': nrm(ks[12], (n_b, D, D), D ** -0.5),
        'nsa_cmp_pe': nrm(ks[13], (n_b, 2, CMP_LEN, NSA_HD), 0.1),
        'nsa_cmp_w1': nrm(ks[14], (n_b, 2, CMP_LEN * NSA_HD, NSA_HD), (CMP_LEN * NSA_HD) ** -0.5),
        'nsa_cmp_w2': nrm(ks[15], (n_b, 2, NSA_HD, NSA_HD), NSA_HD ** -0.5),
        'ffn_w_up': nrm(ks[16], (DEPTH, D, 2 * D_FF), D ** -0.5),
        'ffn_conv_w': nrm(ks[17], (DEPTH, CONV_W, D_FF), CONV_W ** -0.5),
        'ffn_conv_b': nrm(ks[18], (DEPTH, D_FF), 0.02),
        'ffn_w_down': nrm(ks[19], (DEPTH, D_FF, D), D_FF ** -0.5),
    }

def second_block(x, c, ada_w, ada_b, norm_mix, norm_ffn, final_norm, hg_w_in, hg_w_out, hg_gnorm, hg_lb,
              nsa_w_in, nsa_w_out, nsa_cmp_pe, nsa_cmp_w1, nsa_cmp_w2, ffn_w_up, ffn_conv_w, ffn_conv_b,
              ffn_w_down):
    lb_all = jnp.cumsum(jax.nn.softmax(hg_lb.astype(jnp.float32), axis=0), axis=0)
    c_act = jax.nn.silu(c)
    for layer in range(DEPTH):
        mod = c_act @ ada_w[layer] + ada_b[layer]
        sh1, sc1, g1, sh2, sc2, g2 = [m[:, None, :] for m in jnp.split(mod, 6, axis=-1)]
        hmix = rmsnorm(x, norm_mix[layer]) * (1.0 + sc1) + sh1
        j = layer // N_MIXERS
        if layer % N_MIXERS == 0:
            y = hgrn2_mixer(hmix, hg_w_in[j], hg_w_out[j], hg_gnorm[j], lb_all[j])
        else:
            y = nsa_mixer(hmix, nsa_w_in[j], nsa_w_out[j], nsa_cmp_pe[j], nsa_cmp_w1[j], nsa_cmp_w2[j])
        x = x + g1 * y
        hffn = rmsnorm(x, norm_ffn[layer]) * (1.0 + sc2) + sh2
        x = x + g2 * conv_ffn(hffn, ffn_w_up[layer], ffn_conv_w[layer], ffn_conv_b[layer], ffn_w_down[layer])
    return rmsnorm(x, final_norm)


def setup_inputs(seed=0):
    out = dict(first_inputs(seed))
    for name, value in second_inputs(seed + 1).items():
        if name != "x":
            out[name + "_2"] = value
    return out


def reference(
    x, c, rel_bias, ada_w, ada_b, ln_ffn1, ffn1_wg, ffn1_wu, ffn1_wd, ln_mix, ln_ffn2, ffn2_wg,
    ffn2_wu, ffn2_wd, ln_out, attn_w_qkv, attn_q_norm, attn_k_norm, attn_lq1, attn_lk1,
    attn_lq2, attn_lk2, attn_subln, attn_w_o, sgu_w_in, sgu_ln_g, sgu_ln_b, sgu_w_s, sgu_b_s,
    sgu_w_out, c_2, ada_w_2, ada_b_2, norm_mix_2, norm_ffn_2, final_norm_2, hg_w_in_2,
    hg_w_out_2, hg_gnorm_2, hg_lb_2, nsa_w_in_2, nsa_w_out_2, nsa_cmp_pe_2, nsa_cmp_w1_2,
    nsa_cmp_w2_2, ffn_w_up_2, ffn_conv_w_2, ffn_conv_b_2, ffn_w_down_2,
):
    x = first_block(
        x, c, rel_bias, ada_w, ada_b, ln_ffn1, ffn1_wg, ffn1_wu, ffn1_wd, ln_mix, ln_ffn2,
        ffn2_wg, ffn2_wu, ffn2_wd, ln_out, attn_w_qkv, attn_q_norm, attn_k_norm, attn_lq1,
        attn_lk1, attn_lq2, attn_lk2, attn_subln, attn_w_o, sgu_w_in, sgu_ln_g, sgu_ln_b,
        sgu_w_s, sgu_b_s, sgu_w_out,
    )
    return second_block(
        x, c_2, ada_w_2, ada_b_2, norm_mix_2, norm_ffn_2, final_norm_2, hg_w_in_2, hg_w_out_2,
        hg_gnorm_2, hg_lb_2, nsa_w_in_2, nsa_w_out_2, nsa_cmp_pe_2, nsa_cmp_w1_2, nsa_cmp_w2_2,
        ffn_w_up_2, ffn_conv_w_2, ffn_conv_b_2, ffn_w_down_2,
    )


_drawn_inputs = setup_inputs


def setup_inputs(seed=0):
    import zlib

    import numpy as np

    out = dict(_drawn_inputs(seed))
    spreads = {}
    factors = {'attn_q_norm': 3.136,
     'attn_k_norm': 3.774,
     'attn_lq2': 7.289,
     'attn_lk2': 5.095,
     'sgu_ln_g': 3.271,
     'sgu_ln_b': 8.0,
     'norm_mix_2': 4.391,
     'norm_ffn_2': 6.942,
     'final_norm_2': 8.887,
     'hg_gnorm_2': 8.0,
     'nsa_cmp_pe_2': 35.663,
     'ffn_conv_b_2': 8.0}
    for name, (base, spread) in spreads.items():
        noise = np.random.default_rng([zlib.crc32(name.encode()), seed]).standard_normal(out[name].shape)
        drawn = base * np.exp(spread * noise) if base else spread * noise
        out[name] = __import__('jax').numpy.asarray(drawn.astype(out[name].dtype))
    for name, factor in factors.items():
        out[name] = (out[name] * factor).astype(out[name].dtype)
    return out
```

```python
import math
from contextlib import ExitStack

import numpy as np
import concourse.bass as bass
from concourse import mybir

F32 = mybir.dt.float32
F32R = mybir.dt.float32r
U32 = mybir.dt.uint32
I32 = mybir.dt.int32
ALU = mybir.AluOpType
ACT = mybir.ActivationFunctionType
AX = mybir.AxisListType.X

P = 128
SEQ = 256
NT = SEQ // P
D = 1024
KB = D // P
DFF = 2816
FI = DFF // 256
EPS = 1e-6
SLAB = 2048
RAW = 6
SPL = 3
ATILES = 4
N_MOD = 9
N_MOD_2 = 6
HEADS = 8
REL_BUCKETS = 32
REL_MAX_DIST = 128
REL_W = 3 * P
LAMBDA_INIT = 0.8 - 0.6 * math.exp(-0.3 * 0)
NSA_HEADS = 16
NSA_KV = 4
NSA_HPG = NSA_HEADS // NSA_KV
NSA_HD = 64
CMP_LEN = 32
CMP_STRIDE = 16
NC = (SEQ - CMP_LEN) // CMP_STRIDE + 1
FAR = 1e32

FFN_SLABS = 3 * FI
PHASES = ["F0", "A", "F1", "F2", "G", "F3", "H", "C0", "N", "C1"]
SLABS_OF = {"A": 16, "G": 12, "H": 20, "N": 15}
BASE = {}
_n = 0
for _p in PHASES:
    BASE[_p] = _n
    _n += SLABS_OF.get(_p, FFN_SLABS)
FFNS = [p for p in PHASES if p[0] in "FC"]

V2 = 2 * N_MOD
MODS = {"F0": (0, 1, 2), "A": (3, 4, 5), "F1": (6, 7, 8), "F2": (9, 10, 11), "G": (12, 13, 14),
        "F3": (15, 16, 17), "H": (V2, V2 + 1, V2 + 2), "C0": (V2 + 3, V2 + 4, V2 + 5),
        "N": (V2 + 6, V2 + 7, V2 + 8), "C1": (V2 + 9, V2 + 10, V2 + 11)}
NV = V2 + 2 * N_MOD_2
FIRST_VEC = {"F0": 2, "A": 7, "F1": 8, "F2": 13, "F3": 18, "H": 23, "C0": 24, "N": 29}
OPND = {}
for _p in PHASES:
    OPND[_p] = len(OPND)
    if _p in SLABS_OF:
        OPND[_p + "o"] = len(OPND)


def bucket_starts():
    exact = REL_BUCKETS // 2
    n = np.arange(SEQ)
    nf = np.maximum(n, 1).astype(np.float32)
    large = exact + (np.log(nf / np.float32(exact)) / np.float32(math.log(REL_MAX_DIST / exact))
                     * (REL_BUCKETS - exact)).astype(np.int32)
    b = np.where(n < exact, n, np.minimum(large, REL_BUCKETS - 1))
    return [int(np.searchsorted(b, k)) for k in range(REL_BUCKETS)] + [SEQ]


def build(nc, T, out, upto=99):
    phases = PHASES[:upto]
    nslabs = sum(SLABS_OF.get(p, FFN_SLABS) for p in phases)
    with ExitStack() as ctx:
        def sb(name, cols, dt=F32):
            return ctx.enter_context(nc.sbuf_tensor(name, [P, cols], dt))

        def sem(name):
            return ctx.enter_context(nc.semaphore(name))

        raw = sb("raw", RAW * SLAB)
        hi = sb("hi", SPL * SLAB, F32R)
        lo = sb("lo", SPL * SLAB, F32R)
        ada = sb("ada", ATILES * D)
        ada_acc = sb("ada_acc", D)
        operand_hi = sb("operand_hi", KB * SEQ, F32R)
        operand_lo = sb("operand_lo", KB * SEQ, F32R)
        x = sb("x", NT * D)
        gate_row = sb("gate_row", D)
        cols = sb("cols", 6 * P)
        modcol = sb("modcol", NV * KB)
        ident = sb("ident", P)
        ones = sb("ones", P)
        pair_ones = sb("pair_ones", P)
        act_hi = sb("act_hi", 2 * 2 * SEQ, F32R)
        act_lo = sb("act_lo", 2 * 2 * SEQ, F32R)
        small = sb("small", 160)
        work = sb("work", 12500)

        def view(a, b):
            return work[:, a:b]

        def slab(t, s, n):
            return t[:, (s % n) * SLAB:(s % n + 1) * SLAB]

        def op_k(t, k):
            return t[:, k * SEQ:(k + 1) * SEQ]

        sumsq = small[:, 0:2]
        rstd = small[:, 2:4]
        eps_col = small[:, 4:5]
        a_col = small[:, 8:16]
        c_col = small[:, 16:32]
        neg_lam = small[:, 32:33]
        lam_s = small[:, 33:37]
        qk_gain = small[:, 38:40]
        head_gain = small[:, 40:41]
        nmax = small[:, 128:140]
        sums = small[:, 140:152]
        coef = small[:, 44:56]
        lb_col = small[:, 68:76]
        oml_col = small[:, 76:84]
        lb_tmp = small[:, 84:108]
        bn = small[:, 108:120]
        bn_out = small[:, 120:124]
        table_col = small[:, 124:125]

        dacc = ctx.enter_context(nc.psum_tensor("dacc", [P, NT * D], F32))
        up = ctx.enter_context(nc.psum_tensor("up", [P, 2 * 512], F32))
        misc = ctx.enter_context(nc.psum_tensor("misc", [P, 2 * 512], F32))

        def bank(t, j):
            return t[:, j * 512:(j + 1) * 512]

        rel_dram = nc.dram_tensor("rel_scratch", [HEADS, P, REL_W], F32, kind="Internal").ap()

        raw_full = [sem(f"raw_full{i}") for i in range(RAW)]
        ada_full = [sem(f"ada_full{i}") for i in range(ATILES)]
        ada_first = [sem(f"ada_first{i}") for i in range(ATILES)]
        FIRST_ROUNDS = 2 * KB // ATILES
        names = """hi_done lo_done slab_used x_loaded rows_loaded const_done c_in c_psum cols_psum c_ready
            ada_step ada_summed mod_done diag_done gate_psum gate_done
            sumsq_done sqrt_done normed_ready turned shifted_a shifted_d operand_hi_done operand_ready x_done tile_done
            silu_done prod_done acthi_done actlo_done tap_a tap_d
            sq_done ss_done rs_done qk_done v_done qk_logits biased maxed expd attn_done turned_p p_done
            pv_done o_done lam_in lam_exp lam_done rel_rows rel_done rel_out rel_in
            hn_sq hn_ss hn_rs hn_hi out_row row_in row_free
            gelu_done ln_sqrt ln_done ws_in ws_masked ws_turned ws_done mixed bs_in
            ln_stats gated gated_hi level_diff level_exp level_w level_s level_done pt_zero ho_psum ho_done hq_done hk_done sg_done
            own_done own_kept f_done scanned logf_done lb_a lb_d mask_done g_taken hv_done silu_g
            dist_done nq_done nk_done w1_in hid_pe hid_act kc_pe kc_done nv_done ngate_done cl_done cs_done
            cexp_done cp_done npt_pe npt_done no_done windows_done nqk_pe nb_done nmax_done nexp_done nscaled npv_pe no_hi act_chain dve_chain pool_chain stored""".split()
        S = {n: sem(n) for n in names}
        hi_done, lo_done, slab_used = S["hi_done"], S["lo_done"], S["slab_used"]

        block = ctx.enter_context(nc.Block())

        def chain(eng, s):
            count = [0]

            def link(ins):
                count[0] += 1
                ins.then_inc(s, 1)
                eng.wait_ge(s, count[0])
            return link

        col_at = {"ada": 0}
        rows_plan = []
        for li, name in enumerate(["ln_ffn1", "ln_mix", "ln_ffn2", "norm_mix_2", "norm_ffn_2"]):
            rows_plan.append((2, 16 * li, T[name].rearrange("l (k p) -> (l k) p", p=P), 0))
            col_at[name] = 2 * P + 16 * li
        rows_plan += [(2, 80, T["hg_lb_2"].rearrange("l (k p) -> (l k) p", p=P), 0),
                      (2, 96, T["attn_subln"], 0), (2, 97, T["hg_gnorm_2"], 0)]
        for o in (0, 64):
            rows_plan += [(2, 98, T["attn_q_norm"], o), (2, 99, T["attn_k_norm"], o),
                          (3, 0, T["nsa_cmp_pe_2"].rearrange("a b l d -> (a b l) d"), o)]
        rows_plan += [(0, 0, T["ada_b"].rearrange("l (k p) -> (l k) p", p=P)[0:P, :], 0),
                      (1, 0, T["ada_b"].rearrange("l (k p) -> (l k) p", p=P)[P:144, :], 0),
                      (1, 16, T["ada_b_2"].rearrange("l (k p) -> (l k) p", p=P), 0)]
        for l in range(2):
            rows_plan += [(4 + l, 0, T["ffn_conv_w_2"][l].rearrange("w (k p) -> (w k) p", p=P), 0),
                          (4 + l, 66, T["ffn_conv_b_2"][l:l + 1].rearrange("l (k p) -> (l k) p", p=P), 0)]
        tile_rows = [128, 112, 100, 64, 88, 88]

        def gain_cols(name, layer):
            return cols[:, col_at[name] + 8 * layer:col_at[name] + 8 * layer + 8]

        GAIN = {"F0": ("ln_ffn1", 0), "A": ("ln_mix", 0), "F1": ("ln_ffn2", 0), "F2": ("ln_ffn1", 1),
                "G": ("ln_mix", 1), "F3": ("ln_ffn2", 1), "H": ("norm_mix_2", 0), "C0": ("norm_ffn_2", 0),
                "N": ("norm_mix_2", 1), "C1": ("norm_ffn_2", 1)}
        ffn_w = {"F0": ("ffn1_wg", "ffn1_wu", "ffn1_wd", 0), "F1": ("ffn2_wg", "ffn2_wu", "ffn2_wd", 0),
                 "F2": ("ffn1_wg", "ffn1_wu", "ffn1_wd", 1), "F3": ("ffn2_wg", "ffn2_wu", "ffn2_wd", 1)}

        def ffn_sources(p):
            if p in ffn_w:
                g, u, d, l = ffn_w[p]
                return T[g][l], T[u][l], T[d][l]
            l = int(p[1])
            return T["ffn_w_up_2"][l][:, 0:DFF], T["ffn_w_up_2"][l][:, DFF:2 * DFF], T["ffn_w_down_2"][l]

        OUT_ROW = {"F1": T["ln_out"][0:1, :], "F3": T["ln_out"][1:2, :]}
        if upto >= len(PHASES):
            OUT_ROW["C1"] = T["final_norm_2"].rearrange("(a d) -> a d", a=1)
        out_norms = [p for p in phases if p in OUT_ROW]
        norm_list = []
        for p in phases:
            norm_list.append(p)
            if p in OUT_ROW:
                norm_list.append(p + "x")

        def x_count(p):
            n = 0
            for q in phases:
                n += 2
                if q == p:
                    return n
                if q in OUT_ROW:
                    n += 2

        def x_before(norm):
            if norm.endswith("x"):
                return x_count(norm[:-1])
            i = phases.index(norm)
            if i == 0:
                return 0
            return x_count(phases[i - 1]) + (2 if phases[i - 1] in OUT_ROW else 0)

        def count_up(p, i, j):
            return FFNS.index(p) * 2 * FI + 2 * i + j

        def tap(p, w, i, j, it=0):
            o = (4 + int(p[1])) * P + 22 * w + 2 * i + j
            return cols[:, o:o + 1] if isinstance(it, int) else cols[:, bass.ds(it * 4 + o, 1)]

        normed = view(0, 2048)
        turned32 = view(2048, 4096)
        silu_sb = [view(4096 + 256 * j, 4352 + 256 * j) for j in range(2)]
        act32 = [view(4608 + 256 * j, 4864 + 256 * j) for j in range(2)]
        rows_sb = view(6144, 6144 + 6 * P)
        out_row = view(10900, 11924)
        resid_tmp = view(0, 2048)
        qT = view(0, 2048)
        kT = view(2048, 4096)

        v_sb = view(4096, 6144)
        rel_bias = view(6144, 9216).rearrange("p (h k) -> p h k", h=HEADS)
        sq_sb = [view(9216 + 512 * j, 9728 + 512 * j) for j in range(2)]
        rs_sb = [view(10240 + 512 * j, 10752 + 512 * j) for j in range(2)]
        prob = [view(9216 + 768 * j, 9984 + 768 * j) for j in range(3)]
        attn = [view(11520, 11904), view(11904, 12288), ada_acc[:, 0:3 * P]]
        rel_rows = view(6912, 6912 + REL_W)
        rel_tab = view(7424, 7456)
        lam_in = view(11264, 11520)
        c_rows = view(7712, 7840)
        vg_sb = view(2048, 4096)
        ws_raw = view(4096, 5120)
        ws_t = view(5120, 6144)
        ln_g_row, ln_b_row = view(6144, 7168), view(7168, 8192)
        bs_row = view(8192, 9216)
        b_sb = view(4096, 6144)
        hv_sb = view(6144, 8192)
        wlev = [view(8192 + 512 * j, 8704 + 512 * j) for j in range(2)]
        pt_sb = [view(9216 + 768 * j, 9984 + 768 * j) for j in range(2)]
        masks = view(10752, 11648)
        restart = view(11648, 11904)
        hn_sq_sb = [view(9216 + 512 * j, 9728 + 512 * j) for j in range(2)]
        hn_rs_sb = [view(10240 + 512 * j, 10752 + 512 * j) for j in range(2)]
        ks_t, kw_t, kc_t, vc_t = (view(2048 + 512 * j, 2560 + 512 * j) for j in range(4))
        vs_sb, vw_sb = view(4096, 4608), view(4608, 5120)
        w1_sb = [view(5120 + 2048 * j, 7168 + 2048 * j) for j in range(2)]
        w2_sb = [view(9216 + 64 * j, 9280 + 64 * j) for j in range(2)]
        n_prob = [view(5120 + 768 * j, 5888 + 768 * j) for j in range(3)]
        n_pt = [view(7424 + 768 * j, 8192 + 768 * j) for j in range(2)]
        gates = view(9344, 9440)
        kc2 = view(9440, 9500)
        vc_sb = view(9504, 9760)
        hid = [view(9760 + 60 * j, 9820 + 60 * j) for j in range(2)]
        dist = view(9888, 10272)
        cbias = view(10272, 10752)
        windows = view(10752, 11712)
        c_prob = view(10752, 11232)
        c_pt = [view(11232 + 256 * j, 11488 + 256 * j) for j in range(2)]
        n_small = view(11712, 11988)
        diag = view(11988, 12500)

        def col_slab(w, c0):
            v = w[:, c0:c0 + 256].rearrange("(k p) n -> p k n", p=P)
            return [(lambda t, a=a: t.rearrange("p (k n) -> p k n", k=KB)[:, 4 * a:4 * a + 4, :],
                     v[:, 4 * a:4 * a + 4, :]) for a in range(2)]

        def row_slab(w, m):
            return [(lambda t, a=a: t[:, a * D:(a + 1) * D], w[(2 * m + a) * P:(2 * m + a + 1) * P, :])
                    for a in range(2)]

        def mixer_slabs(p):
            if p == "A":
                w = T["attn_w_qkv"][0]
                return ([col_slab(w, 256 * m) for m in range(8)] + [row_slab(w[:, 2048:3072], m) for m in range(4)]
                        + [row_slab(T["attn_w_o"][0], m) for m in range(4)])
            if p == "G":
                w = T["sgu_w_in"][0]
                return ([col_slab(w, 256 * m) for m in range(4)] + [row_slab(w[:, 1024:2048], m) for m in range(4)]
                        + [row_slab(T["sgu_w_out"][0], m) for m in range(4)])
            if p == "H":
                w = T["hg_w_in_2"][0]
                return ([col_slab(w, 256 * m) for m in range(8)] + [row_slab(w[:, 2048:3072], m) for m in range(4)]
                        + [col_slab(w, 3072 + 256 * m) for m in range(4)]
                        + [row_slab(T["hg_w_out_2"][0], m) for m in range(4)])
            w = T["nsa_w_in_2"][0]
            wo = T["nsa_w_out_2"][0]
            res = [col_slab(w, D)]
            for m in range(4):
                src = []
                for g in range(2):
                    c0 = ((m // 2) * 2 * NSA_HPG + g * NSA_HPG + 2 * (m % 2)) * NSA_HD
                    src.append((lambda t, g=g: t.rearrange("p (k n) -> p k n", k=KB)[:, :, g * P:(g + 1) * P],
                                w[:, c0:c0 + P].rearrange("(k p) n -> p k n", p=P)))
                res.append(src)
            for c0 in (1280, 1536, 2048, 1792, 2304, 2608 - 256):
                res.append(col_slab(w, c0))
            for m in range(4):
                src = []
                for g in range(2):
                    r0 = ((m // 2) * 2 * NSA_HPG + g * NSA_HPG + 2 * (m % 2)) * NSA_HD
                    src.append((lambda t, g=g: t[g * 64:(g + 1) * 64, :].rearrange("p (b n) -> p b n", b=2),
                                wo[r0:r0 + P, :].rearrange("(b r) n -> r b n", b=2)))
                res.append(src)
            return res

        def split_views(s):
            if not BASE["N"] < s <= BASE["N"] + 4:
                return [(lambda t: t, lambda t: t)]
            return [(lambda t, c=c: t.rearrange("p (k g n) -> p k g n", k=KB, g=2)[:, :, :, c * 64:(c + 1) * 64],
                     lambda t, c=c: t.rearrange("p (k c g n) -> p k c g n", k=KB, c=2, g=2)[:, :, c]) for c in range(2)]

        PE_MIX, ACT_MIX, DVE_MIX = {}, {}, {}
        ab_banks = [bank(up, 0), bank(up, 1)] + [bank(dacc, j) for j in range(4)]
        sgu_banks = [bank(up, 0), bank(up, 1), bank(misc, 0), bank(misc, 1)]
        nsa_banks = sgu_banks + [bank(dacc, j) for j in range(4)]

        def pe_out(p, pe, slab_ready, row_product, operand_stat):
            b = BASE[p] + SLABS_OF[p] - 4
            for m in range(4):
                slab_ready(b + m)
                pe.wait_ge(S["operand_ready"], 4 * OPND[p + "o"] + m + 1)
                row_product(b + m, operand_stat(m), m == 0, m == 3, last_of_phase=(m == 3))

        def pe_head_sums(pe, inst, c):
            pe.wait_ge(S["hn_sq"], 4 * inst + c + 1)
            if c >= 2:
                pe.wait_ge(S["hn_rs"], 4 * inst + c - 1)
            pe.matmul(bank(misc, c % 2), ones[:, :], hn_sq_sb[c % 2], start=True, stop=True).then_inc(S["hn_ss"], 1)

        def pe_attention(pe, slab_ready, col_product, row_product, operand_stat, ada_sum, gate_spread, three):
            b = BASE["A"]

            def square_sum(m):
                pe.wait_ge(S["sq_done"], m + 1)
                if m == 0:
                    pe.wait_ge(S["gate_done"], phases.index("A") + 1)
                if m >= 2:
                    pe.wait_ge(S["rs_done"], m - 1)
                pe.matmul(bank(misc, m % 2), pair_ones[:, :], sq_sb[m % 2], start=True, stop=True).then_inc(S["ss_done"], 1)

            for m in range(8):
                slab_ready(b + m)
                if m >= 6:
                    pe.wait_ge(S["qk_done"], m - 5)
                col_product(b + m, ab_banks[m % 6], "A" if m == 0 else None)
                if m == 0:
                    pe.wait_ge(S["operand_ready"], 4 * OPND["A"] + 4)
                    gate_spread("A")
                if m:
                    square_sum(m - 1)
            pe.wait_ge(S["qk_done"], 6)
            for m in range(4):
                slab_ready(b + 8 + m)
                row_product(b + 8 + m, operand_stat(m), m == 0, m == 3)
                if m == 0:
                    square_sum(7)
            pe.wait_ge(S["rs_done"], 8)
            ada_sum(7)

            def logits(h):
                if h >= 2:
                    pe.wait_ge(S["biased"], 2 * (h - 1))
                else:
                    pe.wait_ge(S["qk_done"], 8)
                    pe.wait_ge(S["mod_done"], 8)
                for c in range(2):
                    q = qT[64 * c:64 * c + 64, h * SEQ:(h + 1) * SEQ]
                    k = kT[64 * c:64 * c + 64, h * SEQ:(h + 1) * SEQ]
                    o = bank((up, misc)[c], h % 2)
                    pe.matmul(o[:, 0:SEQ], q[:, P:SEQ], k, start=True, stop=True, skip_group_check=True)
                    last = pe.matmul(o[:, SEQ:3 * P], q[:, 0:P], k[:, 0:P], start=True, stop=True,
                                     skip_group_check=True)
                last.then_inc(S["qk_logits"], 1)

            def turn_probs(h):
                pe.wait_ge(S["attn_done"], h + 1)
                if h == 0:
                    pe.wait_ge(S["v_done"], 1)
                if h >= 2:
                    pe.wait_ge(S["p_done"], h - 1)
                for j in range(3):
                    last = pe.transpose(bank(dacc, h % 2)[:, j * P:(j + 1) * P], attn[h % 3][:, j * P:(j + 1) * P],
                                        ident[:, :])
                last.then_inc(S["turned_p"], 1)

            def values(h):
                pe.wait_ge(S["p_done"], h + 1)
                if h >= 2:
                    pe.wait_ge(S["o_done"], h - 1)
                o = bank(dacc, 2 + h % 2)
                v = [v_sb[:, t * D + h * P:t * D + (h + 1) * P] for t in range(NT)]
                pt = attn[h % 3]
                pe.matmul(o[:, P:SEQ], v[0], pt[:, 0:P], start=True, stop=False, skip_group_check=True)
                pe.matmul(o[:, P:SEQ], v[1], pt[:, P:2 * P], start=False, stop=True, skip_group_check=True)
                pe.matmul(o[:, 0:P], v[0], pt[:, 2 * P:3 * P], start=False, stop=True,
                          skip_group_check=True).then_inc(S["pv_done"], 1)

            for h in range(HEADS + 3):
                if h < HEADS:
                    logits(h)
                if 2 <= h < HEADS + 2:
                    turn_probs(h - 2)
                if h >= 3:
                    values(h - 3)
            for c in range(4):
                pe_head_sums(pe, 0, c)
            pe_out("A", pe, slab_ready, row_product, operand_stat)

        def act_attention(act, link, split_hi, gate, head_norm):
            b = BASE["A"]
            gate("A")
            split_hi(b + 2)
            act.wait_ge(S["lam_done"], 1)
            act.activation(lam_s[:, 2:4], lam_s[:, 0:2], ACT.Exp).then_inc(S["lam_exp"], 1)

            def square(m):
                act.wait_ge(slab_used, b + m + 1)
                act.activation(sq_sb[m % 2], ab_banks[m % 6], ACT.Square).then_inc(S["sq_done"], 1)

            def root(m):
                act.wait_ge(S["ss_done"], m + 1)
                if m >= 2:
                    act.wait_ge(S["qk_done"], m - 1)
                act.activation(rs_sb[m % 2], bank(misc, m % 2), ACT.Sqrt, scale=1.0 / NSA_HD,
                               bias=eps_col).then_inc(S["rs_done"], 1)

            for m in range(12):
                if m:
                    split_hi(b + m + 2)
                if 1 <= m <= 8:
                    square(m - 1)
                if 2 <= m <= 9:
                    root(m - 2)
            act.wait_ge(slab_used, b + 12)
            act.copy(v_sb, dacc[:, :]).then_inc(S["v_done"], 1)
            split_hi(b + 14)

            def exps(h):
                act.wait_ge(S["maxed"], h + 1)
                for j, (o, n) in enumerate(((0, SEQ), (3 * P, SEQ), (SEQ, P), (3 * P + SEQ, P))):
                    s = prob[h % 3][:, o:o + n]
                    last = act.activation(s, s, ACT.Exp, bias=nmax[:, 4 * (h % 3) + j:4 * (h % 3) + j + 1],
                                          accum_out=sums[:, 4 * (h % 3) + j:4 * (h % 3) + j + 1])
                    last.then_inc(S["expd"], 1)

            def probs_back(h):
                act.wait_ge(S["turned_p"], h + 1)
                act.copy(attn[h % 3], bank(dacc, h % 2)[:, 0:3 * P]).then_inc(S["p_done"], 1)

            def result(h):
                act.wait_ge(S["pv_done"], h + 1)
                act.copy(qT[:, h * SEQ:(h + 1) * SEQ], bank(dacc, 2 + h % 2)[:, 0:SEQ]).then_inc(S["o_done"], 1)

            for h in range(HEADS + 3):
                if h < HEADS:
                    exps(h)
                if 2 <= h < HEADS + 2:
                    probs_back(h - 2)
                if h >= 3:
                    result(h - 3)
            act.wait_ge(S["o_done"], HEADS)
            head_norm(0, qT)
            for m in range(1, 4):
                split_hi(b + 12 + m + 2)

        def dve_attention(dve, link, split_lo, ada_tile, mod_vector, residual, head_norm):
            b = BASE["A"]

            dve.wait_ge(S["lam_in"], 64)
            for i in range(2):
                a = lam_in[:, P * i:P * i + 64]
                link(dve.tensor_tensor(a, a, lam_in[:, P * i + 64:P * i + P], ALU.mult))
                ins = dve.tensor_reduce(lam_s[:, i:i + 1], a, AX, ALU.add)
                if i == 0:
                    link(ins)
            ins.then_inc(S["lam_done"], 1)

            def scale_qk(m):
                dve.wait_ge(S["rs_done"], m + 1)
                link(dve.reciprocal(rs_sb[m % 2], rs_sb[m % 2]))
                dst = (qT, kT)[m // 4][:, (m % 4) * 512:(m % 4 + 1) * 512]
                dve.scalar_tensor_tensor(dst, ab_banks[m % 6], qk_gain[:, m // 4:m // 4 + 1], rs_sb[m % 2],
                                         ALU.mult, ALU.mult).then_inc(S["qk_done"], 1)

            for m in range(12):
                split_lo(b + m + 2)
                if 2 <= m <= 9:
                    scale_qk(m - 2)
                if m < KB:
                    ada_tile(7, m)
            dve.wait_ge(S["lam_exp"], 1)
            link(dve.tensor_tensor(neg_lam, lam_s[:, 3:4], lam_s[:, 2:3], ALU.subtract))
            link(dve.tensor_scalar(neg_lam, neg_lam, -LAMBDA_INIT, None, ALU.add))
            mod_vector(7)
            split_lo(b + 14)
            dve.wait_ge(S["rel_in"], 32)
            dve.wait_ge(S["qk_done"], 8)

            def bias_and_max(h):
                dve.wait_ge(S["qk_logits"], h + 1)
                for c in range(2):
                    dve.tensor_tensor(prob[h % 3][:, c * 3 * P:(c + 1) * 3 * P], bank((up, misc)[c], h % 2)[:, 0:3 * P],
                                      rel_bias[:, h, :], ALU.add).then_inc(S["biased"], 1)
                dve.wait_ge(S["biased"], 2 * h + 2)
                s = prob[h % 3].rearrange("p (c k) -> p c k", c=2)
                link(dve.tensor_reduce(nmax[:, 4 * (h % 3):4 * (h % 3) + 2], s[:, :, 0:SEQ], AX, ALU.max, negate=True))
                dve.tensor_reduce(nmax[:, 4 * (h % 3) + 2:4 * (h % 3) + 4], s[:, :, SEQ:3 * P], AX, ALU.max,
                                  negate=True).then_inc(S["maxed"], 1)

            def combine(h):
                dve.wait_ge(S["expd"], 4 * (h + 1))
                c = coef[:, 4 * (h % 3):4 * (h % 3) + 4]
                link(dve.reciprocal(c, sums[:, 4 * (h % 3):4 * (h % 3) + 4]))
                odd = c.rearrange("p (t c) -> p t c", c=2)[:, :, 1]
                link(dve.tensor_scalar(odd, odd, neg_lam, None, ALU.mult))
                if h >= 3:
                    dve.wait_ge(S["pv_done"], h - 2)
                pr, at = prob[h % 3], attn[h % 3]
                link(dve.tensor_scalar(at[:, 0:SEQ], pr[:, 0:SEQ], c[:, 0:1], None, ALU.mult))
                link(dve.tensor_scalar(at[:, SEQ:3 * P], pr[:, SEQ:3 * P], c[:, 2:3], None, ALU.mult))
                link(dve.scalar_tensor_tensor(at[:, 0:SEQ], pr[:, 3 * P:3 * P + SEQ], c[:, 1:2], at[:, 0:SEQ],
                                              ALU.mult, ALU.add))
                dve.scalar_tensor_tensor(at[:, SEQ:3 * P], pr[:, 3 * P + SEQ:6 * P], c[:, 3:4], at[:, SEQ:3 * P],
                                         ALU.mult, ALU.add).then_inc(S["attn_done"], 1)

            for h in range(HEADS + 1):
                if h < HEADS:
                    bias_and_max(h)
                if h:
                    combine(h - 1)
            dve.wait_ge(S["o_done"], HEADS)
            head_norm(0, qT, head_gain)
            for m in range(1, 4):
                split_lo(b + 12 + m + 2)
            residual("A")

        PE_MIX["A"], ACT_MIX["A"], DVE_MIX["A"] = pe_attention, act_attention, dve_attention

        def pe_gating(pe, slab_ready, col_product, row_product, operand_stat, ada_sum, gate_spread, three):
            b = BASE["G"]
            for m in range(4):
                slab_ready(b + m)
                if m == 2:
                    pe.wait_ge(S["gate_done"], phases.index("G") + 1)
                col_product(b + m, sgu_banks[m], "G" if m == 0 else None)
                if m == 0:
                    pe.wait_ge(S["operand_ready"], 4 * OPND["G"] + 4)
                    gate_spread("G")
            for m in range(4):
                slab_ready(b + 4 + m)
                row_product(b + 4 + m, operand_stat(m), m == 0, m == 3)
            pe.wait_ge(S["gelu_done"], 4)
            pe.wait_ge(S["ws_masked"], 1)
            for g in range(8):
                last = pe.transpose(misc[:, g * P:(g + 1) * P], ws_raw[:, g * P:(g + 1) * P], ident[:, :])
            last.then_inc(S["ws_turned"], 1)
            pe.wait_ge(S["bs_in"], 48)
            pe.wait_ge(S["ws_done"], 1)
            pe.wait_ge(S["ln_done"], 2)
            for c in range(4):
                for gg in range(2):
                    g = 2 * c + gg
                    for t in range(NT):
                        o = bank(dacc, c)[:, gg * SEQ + t * P:gg * SEQ + (t + 1) * P]
                        pe.matmul(o, vg_sb[:, t * D + g * P:t * D + (g + 1) * P], ws_t[:, g * P:(g + 1) * P],
                                  start=(gg == 0 and t == 0), stop=False, skip_group_check=True)
                        last = pe.matmul(o, ones[0:1, :], bs_row[0:1, g * P:(g + 1) * P], start=False, stop=True,
                                         skip_group_check=True)
                last.then_inc(S["mixed"], 1)
            pe.wait_ge(S["operand_ready"], 4 * OPND["Go"] + 4)
            pe_out("G", pe, slab_ready, row_product, operand_stat)

        def act_gating(act, link, split_hi, gate, head_norm):
            b = BASE["G"]
            gate("G")
            for m in range(8):
                split_hi(b + m + 2)
                if 1 <= m <= 4:
                    act.wait_ge(slab_used, b + m)
                    act.activation(qT[:, (m - 1) * 512:m * 512], sgu_banks[m - 1], ACT.Gelu).then_inc(S["gelu_done"], 1)
            act.wait_ge(slab_used, b + 8)
            for t in range(NT):
                act.activation(vg_sb[:, t * D:(t + 1) * D], dacc[:, t * D:(t + 1) * D],
                               ACT.Gelu).then_inc(S["gelu_done"], 1)
            split_hi(b + 10)
            act.wait_ge(S["ln_stats"], 1)
            var = bn_out.rearrange("p (t s) -> p t s", s=2)[:, :, 1]
            act.activation(var, var, ACT.Sqrt, bias=eps_col).then_inc(S["ln_sqrt"], 1)
            for c in range(4):
                act.wait_ge(S["gated"], c + 1)
                act.copy(operand_hi[:, c * 512:(c + 1) * 512], qT[:, c * 512:(c + 1) * 512]).then_inc(S["gated_hi"], 1)
            for m in range(1, 4):
                split_hi(b + 8 + m + 2)

        def dve_gating(dve, link, split_lo, ada_tile, mod_vector, residual, head_norm):
            b = BASE["G"]
            for m in range(9):
                split_lo(b + m + 2)
            for t in range(NT):
                dve.wait_ge(S["gelu_done"], 5 + t)
                for h in range(2):
                    link(dve.bn_stats(bn[:, 6 * h:6 * h + 6], vg_sb[:, t * D + 512 * h:t * D + 512 * (h + 1)]))
                ins = dve.bn_aggr(bn_out[:, 2 * t:2 * t + 2], bn[:, 0:12].rearrange("p (a b) -> p a b", b=6))
                if t == 0:
                    link(ins)
            ins.then_inc(S["ln_stats"], 1)
            dve.wait_ge(S["ws_turned"], 1)
            dve.tensor_copy(ws_t, misc[:, :]).then_inc(S["ws_done"], 1)
            dve.wait_ge(S["ln_sqrt"], 1)
            var = bn_out.rearrange("p (t s) -> p t s", s=2)[:, :, 1]
            link(dve.reciprocal(var, var))
            dve.wait_ge(S["bs_in"], 48)
            for t in range(NT):
                v = vg_sb[:, t * D:(t + 1) * D]
                link(dve.tensor_scalar(v, v, bn_out[:, 2 * t:2 * t + 1], bn_out[:, 2 * t + 1:2 * t + 2],
                                       ALU.subtract, ALU.mult))
                link(dve.tensor_tensor(v, v, ln_g_row, ALU.mult))
                dve.tensor_tensor(v, v, ln_b_row, ALU.add).then_inc(S["ln_done"], 1)
            for c in range(4):
                o = slice(c * 512, (c + 1) * 512)
                dve.wait_ge(S["mixed"], c + 1)
                dve.tensor_tensor(qT[:, o], qT[:, o], bank(dacc, c), ALU.mult).then_inc(S["gated"], 1)
                dve.wait_ge(S["gated_hi"], c + 1)
                dve.tensor_tensor(operand_lo[:, o], qT[:, o], operand_hi[:, o].bitcast(F32),
                                  ALU.subtract).then_inc(S["operand_ready"], 1)
            for m in range(1, 4):
                split_lo(b + 8 + m + 2)
            residual("G")

        PE_MIX["G"], ACT_MIX["G"], DVE_MIX["G"] = pe_gating, act_gating, dve_gating

        LEVELS = [1, 2, 4, 8, 16, 32, 64, P]

        def hgrn_pool_masks(pool, link):
            pool.wait_ge(S["x_done"], x_before("H"))
            link(pool.memset(masks, 0.0))
            for w, m in enumerate(LEVELS[:-1]):
                v = masks[:, w * P:(w + 1) * P].rearrange("p (g h m) -> p g h m", h=2, m=m)[:, :, 1, :]
                n = P // (2 * m)
                link(pool.memset(v, 1.0))
                link(pool.affine_select(out=v, in_=v, compare_op=ALU.is_ge, fill=0.0, base=0,
                                        pattern=[[-2 * m, n], [0, m]], channel_multiplier=1))
                link(pool.affine_select(out=v, in_=v, compare_op=ALU.is_ge, fill=0.0, base=m - 1,
                                        pattern=[[2 * m, n], [0, m]], channel_multiplier=-1))
            link(pool.memset(restart, 1.0))
            pool.memset(restart.rearrange("p (t s) -> p t s", t=NT)[:, :, 0:1], 0.0).then_inc(S["mask_done"], 1)

        def level_halves(n):
            a, w = n // len(LEVELS), n % len(LEVELS)
            m = LEVELS[w]
            f = lambda t, h: t.rearrange("p (g h m) -> p g h m", h=2, m=m)[:, :, h, :]
            return a, w, m, f

        def hgrn_pool_levels(pool):
            for n in range(4 * len(LEVELS)):
                a, w, m, f = level_halves(n)
                o = slice(a * 512, (a + 1) * 512)
                for h, t in ((0, kT), (1, qT)):
                    pool.wait_ge(S["level_exp"], 2 * n + h + 1)
                    pool.tensor_tensor(f(wlev[n % 2], h), f(wlev[n % 2], h), f(t[:, o], h),
                                       ALU.mult).then_inc(S["level_w"], 1)

        def pe_hgrn(pe, slab_ready, col_product, row_product, operand_stat, ada_sum, gate_spread, three):
            b = BASE["H"]
            for m in range(8):
                slab_ready(b + m)
                if m >= 6:
                    pe.wait_ge(S["hq_done"], m - 5)
                col_product(b + m, ab_banks[m % 6], "H" if m == 0 else None)
                if m == 0:
                    pe.wait_ge(S["operand_ready"], 4 * OPND["H"] + 4)
                    gate_spread("H")
            pe.wait_ge(S["hq_done"], 4)
            pe.wait_ge(S["hk_done"], 4)
            for m in range(4):
                slab_ready(b + 8 + m)
                row_product(b + 8 + m, operand_stat(m), m == 0, m == 3)
            pe.wait_ge(S["gate_done"], phases.index("H") + 1)
            ada_sum(23)

            def own(a):
                if a == 0:
                    pe.wait_ge(S["hv_done"], 1)
                for j in range(4):
                    o = a * 512 + j * P
                    last = pe.matmul(bank(dacc, a % 2)[:, j * P:(j + 1) * P], kT[:, o:o + P], qT[:, o:o + P],
                                     start=True, stop=True, skip_group_check=True)
                last.then_inc(S["own_done"], 1)

            def level(n):
                pe.wait_ge(S["level_w"], 2 * n + 2)
                if n >= 2:
                    pe.wait_ge(S["level_done"], n - 1)
                w = wlev[n % 2]
                cross = n % len(LEVELS) == len(LEVELS) - 1
                for j in range(2 if cross else 4):
                    l = w[:, j * SEQ:j * SEQ + P] if cross else w[:, j * P:(j + 1) * P]
                    r = w[:, j * SEQ + P:(j + 1) * SEQ] if cross else l
                    last = pe.matmul(bank(up, n % 2)[:, j * P:(j + 1) * P], l, r, start=True, stop=True,
                                     skip_group_check=True)
                last.then_inc(S["level_s"], 1)

            def values(a):
                pe.wait_ge(S["level_done"], len(LEVELS) * (a + 1))
                pe.wait_ge(S["own_kept"], a + 1)
                if a >= 2:
                    pe.wait_ge(S["ho_done"], a - 1)
                o = bank(dacc, 2 + a % 2)
                pt = pt_sb[a % 2]
                for j in range(2):
                    v = [hv_sb[:, t * D + (2 * a + j) * P:t * D + (2 * a + j + 1) * P] for t in range(NT)]
                    q = j * SEQ
                    pe.matmul(o[:, q:q + P], v[0], pt[:, j * 3 * P:j * 3 * P + P], start=(j == 0), stop=True,
                              skip_group_check=True)
                    pe.matmul(o[:, q + P:q + SEQ], v[1], pt[:, j * 3 * P + P:j * 3 * P + 2 * P], start=False,
                              stop=False, skip_group_check=True)
                    last = pe.matmul(o[:, q + P:q + SEQ], v[0], pt[:, j * 3 * P + 2 * P:j * 3 * P + 3 * P],
                                     start=False, stop=True, skip_group_check=True)
                last.then_inc(S["ho_psum"], 1)

            def output_gate(c):
                slab_ready(b + 12 + c)
                if c >= 2:
                    pe.wait_ge(S["g_taken"], c - 1)
                col_product(b + 12 + c, bank(misc, c % 2))

            pe.wait_ge(S["mod_done"], 24)
            for a in range(4):
                own(a)
                for w in range(len(LEVELS)):
                    level(a * len(LEVELS) + w)
                    if w == 1 and a:
                        values(a - 1)
                    if w == 3 and a:
                        output_gate(a - 1)
            output_gate(3)
            values(3)
            pe.wait_ge(S["g_taken"], 4)
            for c in range(4):
                pe_head_sums(pe, 1, c)
            pe_out("H", pe, slab_ready, row_product, operand_stat)

        def act_hgrn(act, link, split_hi, gate, head_norm):
            b = BASE["H"]
            gate("H")
            act.wait_ge(S["lb_d"], 1)
            act.activation(lb_tmp[:, 0:16], lb_tmp[:, 0:16], ACT.Exp).then_inc(S["lb_a"], 1)

            def take(m):
                act.wait_ge(slab_used, b + m + 1)
                if m < 4:
                    act.copy(qT[:, m * 512:(m + 1) * 512], ab_banks[m % 6]).then_inc(S["hq_done"], 1)
                    return
                if m >= 6:
                    act.wait_ge(S["hk_done"], m - 5)
                act.activation(wlev[m % 2], ab_banks[m % 6], ACT.Sigmoid).then_inc(S["sg_done"], 1)
                act.activation(pt_sb[m % 2][:, 0:512], ab_banks[m % 6], ACT.Sigmoid,
                               scale=-1.0).then_inc(S["sg_done"], 1)

            for m in range(12):
                split_hi(b + m + 2)
                if 1 <= m <= 8:
                    take(m - 1)
                if m == 10:
                    act.wait_ge(S["hk_done"], 4)
                    act.activation(b_sb, b_sb, ACT.Ln).then_inc(S["logf_done"], 1)
            act.wait_ge(slab_used, b + 12)
            act.copy(hv_sb, dacc[:, :]).then_inc(S["hv_done"], 1)
            split_hi(b + 14)

            def result(a):
                act.wait_ge(S["ho_psum"], a + 1)
                act.copy(qT[:, a * 512:(a + 1) * 512], bank(dacc, 2 + a % 2)).then_inc(S["ho_done"], 1)

            def take_gate(c):
                act.wait_ge(slab_used, b + 13 + c)
                act.wait_ge(S["level_w"], 2 * len(LEVELS) * (c + 1))
                act.copy(kT[:, c * 512:(c + 1) * 512], bank(misc, c % 2)).then_inc(S["g_taken"], 1)
                split_hi(b + 15 + c)

            for n in range(4 * len(LEVELS)):
                a, w, m, f = level_halves(n)
                act.wait_ge(S["level_diff"], n + 1)
                t = wlev[n % 2]
                act.activation(f(t, 0), f(t, 0), ACT.Exp, scale=-1.0).then_inc(S["level_exp"], 1)
                src = f(b_sb[:, a * 512:(a + 1) * 512], 1) if m == P else f(t, 1)
                act.activation(f(t, 1), src, ACT.Exp).then_inc(S["level_exp"], 1)
                if w == 4 and a:
                    result(a - 1)
                if w == 6 and a:
                    take_gate(a - 1)
            take_gate(3)
            result(3)
            act.wait_ge(S["ho_done"], 4)
            act.wait_ge(S["g_taken"], 4)
            act.activation(kT, kT, ACT.Silu).then_inc(S["silu_g"], 1)
            head_norm(1, qT)
            for m in range(1, 4):
                split_hi(b + 16 + m + 2)

        def dve_hgrn(dve, link, split_lo, ada_tile, mod_vector, residual, head_norm):
            b = BASE["H"]
            l0, l1 = cols[:, 2 * P + 80:2 * P + 88], cols[:, 2 * P + 88:2 * P + 96]
            link(dve.tensor_tensor(lb_tmp[:, 16:24], l0, l1, ALU.max))
            link(dve.tensor_tensor(lb_tmp[:, 0:8], l0, lb_tmp[:, 16:24], ALU.subtract))
            dve.tensor_tensor(lb_tmp[:, 8:16], l1, lb_tmp[:, 16:24], ALU.subtract).then_inc(S["lb_d"], 1)
            dve.wait_ge(S["lb_a"], 1)
            link(dve.tensor_tensor(lb_tmp[:, 16:24], lb_tmp[:, 0:8], lb_tmp[:, 8:16], ALU.add))
            link(dve.reciprocal(lb_tmp[:, 16:24], lb_tmp[:, 16:24]))
            link(dve.tensor_tensor(lb_col, lb_tmp[:, 0:8], lb_tmp[:, 16:24], ALU.mult))
            link(dve.tensor_scalar(oml_col, lb_col, -1.0, 1.0, ALU.mult, ALU.add))

            def forget(c):
                dve.wait_ge(S["sg_done"], 2 * c + 2)
                for j in range(2):
                    h = 2 * c + j
                    o = slice(h * SEQ, (h + 1) * SEQ)
                    dve.tensor_scalar(b_sb[:, o], wlev[c % 2][:, j * SEQ:(j + 1) * SEQ], oml_col[:, h:h + 1],
                                      lb_col[:, h:h + 1], ALU.mult, ALU.add).then_inc(S["f_done"], 1)
                    ins = dve.tensor_scalar(kT[:, o], pt_sb[c % 2][:, j * SEQ:(j + 1) * SEQ], oml_col[:, h:h + 1],
                                            None, ALU.mult)
                    if j == 0:
                        link(ins)
                dve.wait_ge(S["f_done"], 2 * c + 2)
                ins.then_inc(S["hk_done"], 1)

            for m in range(12):
                split_lo(b + m + 2)
                if 5 <= m <= 8:
                    forget(m - 5)
                if m < KB:
                    ada_tile(23, m)
            dve.wait_ge(S["logf_done"], 1)
            dve.wait_ge(S["mask_done"], 1)
            for h in range(HEADS):
                o = slice(h * SEQ, (h + 1) * SEQ)
                dve.tensor_tensor_scan(b_sb[:, o], restart, b_sb[:, o], 0.0, ALU.mult,
                                       ALU.add).then_inc(S["scanned"], 1)
            dve.wait_ge(S["scanned"], HEADS)
            mod_vector(23)
            split_lo(b + 14)
            n_levels = 4 * len(LEVELS)

            def difference(n):
                a, w, m, f = level_halves(n)
                if n >= 2:
                    dve.wait_ge(S["level_s"], n - 1)
                src = b_sb[:, a * 512:(a + 1) * 512].rearrange("p (g m) -> p g m", m=2 * m)
                dst = wlev[n % 2].rearrange("p (g m) -> p g m", m=2 * m)
                k = m if m == P else 2 * m
                dve.tensor_tensor(dst[:, :, 0:k], src[:, :, 0:k],
                                  src[:, :, m - 1:m].to_broadcast([P, 512 // (2 * m), k]),
                                  ALU.subtract).then_inc(S["level_diff"], 1)

            def keep(n):
                a, w, m, f = level_halves(n)
                dve.wait_ge(S["level_s"], n + 1)
                pt = pt_sb[a % 2].rearrange("p (h j q) -> p h j q", h=2, j=3)
                sc = bank(up, n % 2)
                if m == P:
                    dve.tensor_copy(pt[:, :, 2, :], sc[:, 0:SEQ].rearrange("p (h q) -> p h q", h=2)).then_inc(S["level_done"], 1)
                    return
                for j in range(2):
                    ins = dve.copy_predicated(pt[:, j, 0:2, :],
                                              masks[:, w * P:(w + 1) * P].bitcast(U32).unsqueeze(1).to_broadcast([P, 2, P]),
                                              sc[:, j * SEQ:(j + 1) * SEQ].rearrange("p (t q) -> p t q", t=2))
                    if j == 0:
                        link(ins)
                    else:
                        ins.then_inc(S["level_done"], 1)

            def keep_own(a):
                if a >= 2:
                    dve.wait_ge(S["ho_psum"], a - 1)
                link(dve.memset(pt_sb[a % 2], 0.0))
                dve.wait_ge(S["own_done"], a + 1)
                pt = pt_sb[a % 2].rearrange("p (h j q) -> p h j q", h=2, j=3)
                for j in range(2):
                    ins = dve.copy_predicated(pt[:, j, 0:2, :], ident[:, :].bitcast(U32).unsqueeze(1).to_broadcast([P, 2, P]),
                                              bank(dacc, a % 2)[:, j * SEQ:(j + 1) * SEQ].rearrange("p (t q) -> p t q", t=2))
                    if j == 0:
                        link(ins)
                ins.then_inc(S["own_kept"], 1)
                dve.wait_ge(S["own_kept"], a + 1)

            difference(0)
            difference(1)
            for n in range(n_levels):
                if n % len(LEVELS) == 0:
                    keep_own(n // len(LEVELS))
                if n:
                    dve.wait_ge(S["level_done"], n)
                keep(n)
                if n + 2 < n_levels:
                    difference(n + 2)
                if n % len(LEVELS) == 6 and n > len(LEVELS):
                    split_lo(b + 14 + n // len(LEVELS))
            split_lo(b + 18)
            dve.wait_ge(S["ho_done"], 4)
            head_norm(1, qT, cols[:, 2 * P + 97:2 * P + 98], gate=kT)
            for m in range(1, 4):
                split_lo(b + 16 + m + 2)
            residual("H")

        PE_MIX["H"], ACT_MIX["H"], DVE_MIX["H"] = pe_hgrn, act_hgrn, dve_hgrn

        def nsa_head(n):
            bb, f = n // 2, n % 2
            h = (bb // NSA_HPG) * 2 * NSA_HPG + f * NSA_HPG + bb % NSA_HPG
            return bb, f, bb // NSA_HPG, h, float(np.float32(2.0 ** (-8.0 * (h + 1) / NSA_HEADS)))

        c_max, c_sum = n_small[:, 0:32], n_small[:, 32:64]
        n_nmax, n_sums, n_coef = n_small[:, 64:76], n_small[:, 76:88], n_small[:, 88:100]
        late_row = n_small[:, 100:101]
        c_dist = n_small[:, 104:104 + NT * NC]
        c_prob4 = c_prob.rearrange("p (f t b n) -> p f t b n", f=2, t=NT, n=NC)

        def nsa_pool_tables(pool, link):
            pool.wait_ge(S["x_done"], x_before("N"))
            for o, n, base in ((0, SEQ, P), (SEQ, P, 0)):
                d = dist[:, o:o + n]
                link(pool.iota(d, pattern=[[-1, n]], base=base, channel_multiplier=1,
                               allow_small_or_imprecise_dtypes=True))
                link(pool.affine_select(out=d, in_=d, compare_op=ALU.is_ge, fill=FAR, base=base,
                                        pattern=[[-1, n]], channel_multiplier=1))
            cd = c_dist.rearrange("p (t n) -> p t n", t=NT)
            link(pool.iota(cd, pattern=[[P, NT], [-CMP_STRIDE, NC]], base=0, channel_multiplier=1,
                           allow_small_or_imprecise_dtypes=True))
            link(pool.tensor_scalar(cd, cd, -(CMP_LEN - 1) / 2.0, None, ALU.add))
            link(pool.affine_select(out=cd, in_=cd, compare_op=ALU.is_ge, fill=FAR, base=-(CMP_LEN - 1),
                                    pattern=[[P, NT], [-CMP_STRIDE, NC]], channel_multiplier=1))
            cb = cbias.rearrange("p (f t b n) -> p f t b n", f=2, t=NT, n=NC)
            for n in range(NSA_HEADS):
                bb, f, _, _, slope = nsa_head(n)
                link(pool.tensor_scalar(cb[:, f, :, bb, :], cd, -slope, None, ALU.mult))
            link(pool.memset(late_row, 1.0))
            pool.affine_select(out=late_row, in_=late_row, compare_op=ALU.is_ge, fill=0.0, base=-(CMP_LEN - 1),
                               pattern=[[0, 1]], channel_multiplier=1).then_inc(S["dist_done"], 1)

        def pe_nsa(pe, slab_ready, col_product, row_product, operand_stat, ada_sum, gate_spread, three):
            b = BASE["N"]

            def token_product(s, dst, c0, w):
                for t in range(NT):
                    for k in range(KB):
                        last = three(dst[:, t * w:(t + 1) * w],
                                     [op_k(o, k)[:, t * P:(t + 1) * P] for o in (operand_hi, operand_lo)],
                                     [slab(o, s, SPL)[:, k * SEQ + c0:k * SEQ + c0 + w] for o in (hi, lo)],
                                     k == 0, k == KB - 1)
                last.then_inc(slab_used, 1)

            for m in range(11):
                slab_ready(b + m)
                if m == 1:
                    pe.wait_ge(S["operand_ready"], 4 * OPND["N"] + 4)
                    gate_spread("N")
                if m == 3:
                    pe.wait_ge(S["gate_done"], phases.index("N") + 1)
                if m < 8:
                    col_product(b + m, nsa_banks[m - 1 if 1 <= m <= 4 else max(m, 4)], "N" if m == 0 else None)
                else:
                    pe.wait_ge(S["nq_done"], m - 7)
                    token_product(b + m, nsa_banks[m - 8], *((0, SEQ) if m < 10 else (SEQ - 3 * NSA_HEADS, 3 * NSA_HEADS)))
            pe.wait_ge(S["nq_done"], 4)
            ada_sum(29)

            pe.wait_ge(S["w1_in"], 96)
            pe.wait_ge(S["nv_done"], 2)
            for a in range(2):
                if a == 1:
                    pe.wait_ge(S["ngate_done"], 1)
                    pe.wait_ge(S["mod_done"], 30)
                pe.wait_ge(S["windows_done"], a + 1)
                for l in range(CMP_LEN):
                    for f in range(2):
                        r = slice(64 * f, 64 * f + 64)
                        last = pe.matmul(bank((up, misc)[a], f)[0:64, 0:2 * NC],
                                         w1_sb[a][r, l * 64:(l + 1) * 64], windows[r, l * 2 * NC:(l + 1) * 2 * NC],
                                         start=(l == 0), stop=(l == CMP_LEN - 1), skip_group_check=True)
                last.then_inc(S["hid_pe"], 1)
            pe.wait_ge(S["hid_act"], 2)
            pe.wait_ge(S["nk_done"], 4)
            pe.matmul(bank(dacc, 2)[0:64, 0:NSA_KV * NC], w2_sb[0][0:64, :], hid[0][0:64, :], start=True,
                      stop=True).then_inc(S["kc_pe"], 1)
            pe.wait_ge(S["hid_act"], 4)
            for g in range(NSA_KV):
                last = pe.matmul(bank(dacc, 3)[0:NC, g * 64:(g + 1) * 64], hid[1][0:64, g * NC:(g + 1) * NC],
                                 w2_sb[1][0:64, :], start=True, stop=True, skip_group_check=True)
            last.then_inc(S["kc_pe"], 1)

            def compressed_scores():
                pe.wait_ge(S["kc_done"], 1)
                for t in range(NT):
                    for n in range(NSA_HEADS):
                        bb, f, p, _, _ = nsa_head(n)
                        r = slice(64 * f, 64 * f + 64)
                        o = (t * KB + bb) * NC
                        g = 2 * p + f
                        last = pe.matmul(bank(dacc, f)[:, o:o + NC], qT[r, bb * SEQ + t * P:bb * SEQ + (t + 1) * P],
                                         kc2[r, g * NC:(g + 1) * NC], start=True, stop=True, skip_group_check=True)
                last.then_inc(S["cs_done"], 1)

            def scores(n):
                bb, f, p, _, _ = nsa_head(n)
                r = slice(64 * f, 64 * f + 64)
                if n >= 2:
                    pe.wait_ge(S["nb_done"], n - 1)
                q = qT[r, bb * SEQ:(bb + 1) * SEQ]
                k = work[r, 2048:3072].rearrange("p (r b s) -> p r b s", r=2, b=2)[:, :, p, :]
                pe.matmul(bank(up, n % 2), q[:, P:SEQ], k, start=True, stop=True, skip_group_check=True)
                pe.matmul(bank(misc, n % 2)[:, 0:SEQ], q[:, 0:P], k[:, :, 0:P], start=True, stop=True,
                          skip_group_check=True).then_inc(S["nqk_pe"], 1)

            def turn_probs(n):
                bb, f, _, _, _ = nsa_head(n)
                pe.wait_ge(S["nscaled"], n + 1)
                if n == 0:
                    pe.wait_ge(S["cp_done"], 1)
                if n:
                    pe.wait_ge(S["npt_done"], n)
                pr = n_prob[n % 3]
                for br in range(2):
                    for j, c in enumerate((512 + br * P, br * SEQ, br * SEQ + P)):
                        w = (br * 3 + j) * P
                        pe.transpose(dacc[:, w:w + P], pr[:, c:c + P], ident[:, :])
                for t in range(NT):
                    w = (6 + t) * P
                    last = pe.transpose(dacc[0:NC, w:w + P], c_prob4[:, f, t, bb, :], ident[:, :])
                last.then_inc(S["npt_pe"], 1)

            def values(n):
                _, _, p, _, _ = nsa_head(n)
                pe.wait_ge(S["npt_done"], n + 1)
                if n >= 2:
                    pe.wait_ge(S["no_done"], n - 1)
                o = bank(dacc, 2 + n % 2)[:, 0:SEQ]
                pe.matmul(o, vc_sb[0:NC, p * P:(p + 1) * P], c_pt[n % 2][0:NC, :], start=True, stop=False,
                          skip_group_check=True)
                for br, v in enumerate((vs_sb, vw_sb)):
                    pt = n_pt[n % 2][:, br * 3 * P:(br + 1) * 3 * P]
                    pe.matmul(o, v[:, p * P:(p + 1) * P], pt[:, 0:SEQ], start=False, stop=False, skip_group_check=True)
                    last = pe.matmul(o[:, P:SEQ], v[:, SEQ + p * P:SEQ + (p + 1) * P], pt[:, SEQ:3 * P], start=False,
                                     stop=(br == 1), skip_group_check=True)
                last.then_inc(S["npv_pe"], 1)

            compressed_scores()
            pe.wait_ge(S["kc_done"], 2)
            for n in range(NSA_HEADS + 3):
                if n < NSA_HEADS:
                    scores(n)
                if 2 <= n < NSA_HEADS + 2:
                    turn_probs(n - 2)
                if n >= 3:
                    values(n - 3)
            pe.wait_ge(S["no_done"], NSA_HEADS)
            pe_out("N", pe, slab_ready, row_product, operand_stat)

        def act_nsa(act, link, split_hi, gate, head_norm):
            b = BASE["N"]
            gate("N")
            for m in range(12):
                split_hi(b + m + 2)
                if 2 <= m <= 5:
                    act.activation(qT[:, (m - 2) * 512:(m - 1) * 512], nsa_banks[m - 2], ACT.Copy,
                                   scale=float(NSA_HD) ** -0.5).then_inc(S["nq_done"], 1)
                elif m == 1 or 6 <= m <= 8:
                    act.copy((kc_t, vc_t, ks_t, kw_t)[max(m - 5, 0)], nsa_banks[max(m - 1, 4)]).then_inc(S["nk_done"], 1)
                elif 9 <= m <= 10:
                    act.copy((vs_sb, vw_sb)[m - 9], nsa_banks[m - 9]).then_inc(S["nv_done"], 1)
            act.activation(gates, bank(misc, 0)[:, 0:NT * 3 * NSA_HEADS], ACT.Sigmoid).then_inc(S["ngate_done"], 1)
            for a in range(2):
                act.wait_ge(S["hid_pe"], a + 1)
                h = hid[a][0:64, :].rearrange("p (b f n) -> p f b n", f=2, n=NC)
                for f in range(2):
                    act.activation(h[:, f], bank((up, misc)[a], f)[0:64, 0:2 * NC]
                                   .rearrange("p (b n) -> p b n", n=NC), ACT.Silu).then_inc(S["hid_act"], 1)
            act.wait_ge(S["kc_pe"], 1)
            act.copy(kc2[0:64, :], bank(dacc, 2)[0:64, 0:NSA_KV * NC])
            act.copy(kc2[64:P, :], bank(dacc, 2)[0:64, 0:NSA_KV * NC]).then_inc(S["kc_done"], 1)
            act.wait_ge(S["kc_pe"], 2)
            act.copy(vc_sb[0:NC, :], bank(dacc, 3)[0:NC, 0:SEQ]).then_inc(S["kc_done"], 1)

            def exps(n):
                act.wait_ge(S["nmax_done"], n + 1)
                for j, (o, w) in enumerate(((512, P), (512 + P, P), (0, SEQ), (SEQ, SEQ))):
                    s = n_prob[n % 3][:, o:o + w]
                    i = 4 * (n % 3) + j
                    act.activation(s, s, ACT.Exp, bias=n_nmax[:, i:i + 1],
                                   accum_out=n_sums[:, i:i + 1]).then_inc(S["nexp_done"], 1)

            def probs_back(n):
                act.wait_ge(S["npt_pe"], n + 1)
                if n >= 2:
                    act.wait_ge(S["npv_pe"], n - 1)
                act.copy(n_pt[n % 2], dacc[:, 0:768])
                act.copy(c_pt[n % 2][0:NC, :], dacc[0:NC, 768:1024]).then_inc(S["npt_done"], 1)

            def result(n):
                bb, f, _, _, _ = nsa_head(n)
                r = slice(64 * f, 64 * f + 64)
                act.wait_ge(S["npv_pe"], n + 1)
                act.copy(qT[r, bb * SEQ:(bb + 1) * SEQ],
                         bank(dacc, 2 + n % 2)[r, 0:SEQ]).then_inc(S["no_done"], 1)
                if n % 4 == 3:
                    o = slice(n // 4 * 512, (n // 4 + 1) * 512)
                    act.wait_ge(S["no_done"], n + 1)
                    act.copy(operand_hi[:, o], qT[:, o]).then_inc(S["no_hi"], 1)

            act.wait_ge(S["cl_done"], 1)
            act.activation(c_prob, c_prob, ACT.Exp).then_inc(S["cexp_done"], 1)
            for n in range(NSA_HEADS + 3):
                if n < NSA_HEADS:
                    exps(n)
                if 2 <= n < NSA_HEADS + 2:
                    probs_back(n - 2)
                if n >= 3:
                    result(n - 3)
            for m in range(1, 4):
                split_hi(b + 11 + m + 2)

        def dve_nsa(dve, link, split_lo, ada_tile, mod_vector, residual, head_norm):
            b = BASE["N"]

            def make_windows(a):
                src = (kc_t, vc_t)[a].rearrange("p (b c s) -> p b c s", b=2, s=CMP_STRIDE)
                w = windows.rearrange("p (l b n) -> p l b n", l=CMP_LEN, b=2)
                pos = cols[:, 3 * P + a * CMP_LEN:3 * P + (a + 1) * CMP_LEN]
                dve.wait_ge(S["nk_done"], a + 1)
                for j in range(CMP_LEN // CMP_STRIDE):
                    o = slice(j * CMP_STRIDE, (j + 1) * CMP_STRIDE)
                    for blk in range(2):
                        ins = dve.tensor_tensor(w[:, o, blk, :], src[:, blk, j:j + NC, :].rearrange("p n s -> p s n"),
                                                pos[:, o].unsqueeze(2).to_broadcast([P, CMP_STRIDE, NC]), ALU.add)
                ins.then_inc(S["windows_done"], 1)

            for m in range(12):
                split_lo(b + m + 2)
                if m < KB:
                    ada_tile(29, m)
                if m == 5:
                    make_windows(0)
            mod_vector(29)
            dve.wait_ge(S["hid_pe"], 1)
            make_windows(1)

            dve.wait_ge(S["dist_done"], 1)
            dve.wait_ge(S["cs_done"], 1)
            rows = c_prob.rearrange("p (r n) -> p r n", n=NC)
            link(dve.tensor_tensor(c_prob.rearrange("p (f c) -> p f c", f=2),
                                   dacc[:, 0:1024].rearrange("p (f c) -> p f c", f=2)[:, :, 0:NT * KB * NC],
                                   cbias.rearrange("p (f c) -> p f c", f=2), ALU.add))
            link(dve.tensor_reduce(c_max, rows, AX, ALU.max))
            dve.tensor_tensor(rows, rows, c_max.unsqueeze(2).to_broadcast([P, 32, NC]),
                              ALU.subtract).then_inc(S["cl_done"], 1)

            def compressed_probs():
                dve.wait_ge(S["cexp_done"], 1)
                link(dve.tensor_reduce(c_sum, rows, AX, ALU.add))
                link(dve.reciprocal(c_sum, c_sum))
                for f in range(2):
                    for t in range(NT):
                        c = c_sum[:, (f * NT + t) * KB:(f * NT + t + 1) * KB].rearrange("p (g h) -> p g h", g=2)
                        g0 = gates.rearrange("p (t g f h r) -> p t g f h r", t=NT, g=2, f=2, r=3)[:, t, :, f, :, 0]
                        link(dve.tensor_tensor(c, c, g0, ALU.mult))
                early = c_sum.rearrange("p (f t b) -> p f t b", f=2, t=NT)[:, :, 0, :]
                link(dve.tensor_scalar(early, early, late_row, None, ALU.mult))
                dve.tensor_tensor(rows, rows, c_sum.unsqueeze(2).to_broadcast([P, 32, NC]),
                                  ALU.mult).then_inc(S["cp_done"], 1)

            def bias_and_max(n):
                _, _, _, _, slope = nsa_head(n)
                dve.wait_ge(S["nqk_pe"], n + 1)
                if n >= 3:
                    dve.wait_ge(S["npt_pe"], n - 2)
                pr = n_prob[n % 3]
                m = n_nmax[:, 4 * (n % 3):4 * (n % 3) + 4]
                late = pr[:, 0:512].rearrange("p (r k) -> p r k", r=2)
                early = pr[:, 512:768].rearrange("p (r k) -> p r k", r=2)
                link(dve.scalar_tensor_tensor(late, dist[:, 0:SEQ].unsqueeze(1).to_broadcast([P, 2, SEQ]), -slope,
                                              bank(up, n % 2).rearrange("p (r k) -> p r k", r=2), ALU.mult, ALU.add))
                dve.scalar_tensor_tensor(early, dist[:, SEQ:3 * P].unsqueeze(1).to_broadcast([P, 2, P]), -slope,
                                         bank(misc, n % 2)[:, 0:SEQ].rearrange("p (r k) -> p r k", r=2), ALU.mult,
                                         ALU.add).then_inc(S["nb_done"], 1)
                dve.wait_ge(S["nb_done"], n + 1)
                link(dve.tensor_reduce(m[:, 0:2], early, AX, ALU.max, negate=True))
                dve.tensor_reduce(m[:, 2:4], late, AX, ALU.max, negate=True).then_inc(S["nmax_done"], 1)

            def scale(n):
                _, _, _, h, _ = nsa_head(n)
                dve.wait_ge(S["nexp_done"], 4 * n + 4)
                i = 4 * (n % 3)
                c = n_coef[:, i:i + 4]
                link(dve.reciprocal(c, n_sums[:, i:i + 4]))
                link(dve.tensor_tensor(c.rearrange("p (t r) -> p t r", t=NT), c.rearrange("p (t r) -> p t r", t=NT),
                                       gates.rearrange("p (t c) -> p t c", t=NT)[:, :, 3 * h + 1:3 * h + 3], ALU.mult))
                pr = n_prob[n % 3]
                late = pr[:, 0:512].rearrange("p (r k) -> p r k", r=2)
                early = pr[:, 512:768].rearrange("p (r k) -> p r k", r=2)
                link(dve.tensor_tensor(late, late, c[:, 2:4].unsqueeze(2).to_broadcast([P, 2, SEQ]), ALU.mult))
                dve.tensor_tensor(early, early, c[:, 0:2].unsqueeze(2).to_broadcast([P, 2, P]),
                                  ALU.mult).then_inc(S["nscaled"], 1)

            def operand_rest(c):
                o = slice(c * 512, (c + 1) * 512)
                dve.wait_ge(S["no_hi"], c + 1)
                dve.tensor_tensor(operand_lo[:, o], qT[:, o], operand_hi[:, o].bitcast(F32),
                                  ALU.subtract).then_inc(S["operand_ready"], 1)

            for n in range(NSA_HEADS + 1):
                if n < NSA_HEADS:
                    bias_and_max(n)
                if n == 0:
                    compressed_probs()
                if n:
                    scale(n - 1)
                if n >= 8 and n % 4 == 0:
                    operand_rest(n // 4 - 2)
            operand_rest(3)
            for m in range(1, 4):
                split_lo(b + 11 + m + 2)
            residual("N")

        PE_MIX["N"], ACT_MIX["N"], DVE_MIX["N"] = pe_nsa, act_nsa, dve_nsa
        def ada_source(v, k):
            if v < V2:
                return T["ada_w"][v // N_MOD][k * P:(k + 1) * P, (v % N_MOD) * D:(v % N_MOD + 1) * D]
            u = v - V2
            return T["ada_w_2"][u // N_MOD_2][k * P:(k + 1) * P, (u % N_MOD_2) * D:(u % N_MOD_2 + 1) * D]

        def ada_load(eng, v, k, it=0, source=None):
            m = v * KB + k
            if m >= ATILES:
                eng.wait_ge(S["ada_step"], m - ATILES + 1 + KB * it)
            eng.dma_start(ada[:, (m % ATILES) * D:(m % ATILES + 1) * D],
                          ada_source(v, k) if source is None else source).then_inc(
                              (ada_first if v < 2 else ada_full)[m % ATILES], 16)

        @block.sync
        def _(sp):
            early_slabs = []
            def load(s, it, sources):
                if s >= RAW:
                    sp.wait_ge(lo_done, s - RAW + 1 + RAW * it)
                for place, src in sources:
                    sp.dma_start(place(slab(raw, s, RAW)), src).then_inc(raw_full[s % RAW], 16)

            def up_src(p, i, j):
                wg, wu, _ = ffn_sources(p)
                return [(lambda t, a=a: t.rearrange("p (k n) -> p k n", k=KB)[:, :, a * P:(a + 1) * P],
                         w.rearrange("(k p) n -> p k n", p=P)[:, :, bass.ds(i * 256 + j * P, P)])
                        for a, w in enumerate((wg, wu))]

            def down_src(p, i):
                wd = ffn_sources(p)[2].rearrange("(k p) n -> p k n", p=P)
                return [(lambda t, a=a: t[:, a * D:(a + 1) * D].unsqueeze(1), wd[:, bass.ds(i * 2 + a, 1), :])
                        for a in range(2)]

            def ffn(p):
                b = BASE[p]
                for j in range(2):
                    if b + j not in early_slabs:
                        load(b + j, 0, up_src(p, 0, j))
                for i in (1, 2):
                    for j in range(2):
                        load(b + 3 * i - 1 + j, 0, up_src(p, i, j))
                    load(b + 3 * i + 1, 0, down_src(p, i - 1))
                if p in OUT_ROW:
                    sp.wait_ge(S["x_done"], x_before(p))
                    sp.dma_start(out_row, OUT_ROW[p].to_broadcast([P, D])).then_inc(S["row_in"], 16)
                with sp.Fori(0, (FI - 3) // 2) as it:
                    for i in (3, 4):
                        for j in range(2):
                            load(b + 3 * i - 1 + j, it, up_src(p, it * 2 + i, j))
                        load(b + 3 * i + 1, it, down_src(p, it * 2 + i - 1))
                load(b + FFN_SLABS - 1, 0, down_src(p, FI - 1))

            for r0, name in ((0, "c"), (KB, "c_2")):
                sp.dma_start(c_rows[r0:r0 + KB, :], T[name].rearrange("b (k p) -> (b k) p", p=P)).then_inc(S["c_in"], 16)
            first_tiles = [(v, k) for v in range(2) for k in range(KB)]

            def first_ada():
                v, k = first_tiles.pop(0)
                ada_load(sp, v, k)

            for _ in range(ATILES):
                first_ada()
            sp.dma_start(x[:, :].rearrange("p (t d) -> p t d", t=NT),
                         T["x"][0].rearrange("(t p) d -> p t d", p=P)).then_inc(S["x_loaded"], 16)
            for i, (tile, r0, src, o) in enumerate(rows_plan):
                sp.dma_start(rows_sb[r0:r0 + src.shape[0], tile * P + o:tile * P + o + src.shape[1]],
                             src).then_inc(S["rows_loaded"], 16)
                if i % 4 == 3 and len(first_tiles) > KB + 2:
                    first_ada()
            while first_tiles:
                for _ in range(min(5, len(first_tiles))):
                    first_ada()
                if len(first_tiles) < KB:
                    early_slabs.append(len(early_slabs))
                    load(early_slabs[-1], 0, up_src(phases[0], 0, early_slabs[-1]))
            for i, name in enumerate(("attn_lq1", "attn_lk1", "attn_lq2", "attn_lk2")):
                sp.dma_start(lam_in[:, 64 * i:64 * i + 64], T[name].to_broadcast([P, 64])).then_inc(S["lam_in"], 16)
            sp.dma_start(rel_tab[0:HEADS, :], T["rel_bias"].rearrange("b h -> h b"),
                         allow_slow_non_contiguous=True).then_inc(S["rel_rows"], 16)

            def mixer_parameters(p):
                sp.wait_ge(S["operand_ready"], 4 * OPND[p] + 4)
                if p == "A":
                    sp.wait_ge(S["rel_out"], 16)
                    for o, n, dst in ((P - 1, SEQ, rel_bias[:, :, 0:SEQ]), (2 * P - 1, P, rel_bias[:, :, SEQ:3 * P])):
                        sp.dma_start(dst, bass.AP(tensor=rel_dram.tensor, offset=rel_dram.offset + o,
                                                  ap=[[REL_W - 1, P], [P * REL_W, HEADS], [1, n]])).then_inc(S["rel_in"], 16)
                if p == "G":
                    sp.dma_start(ws_raw.rearrange("p (g s) -> p g s", g=8),
                                 T["sgu_w_s"][0].rearrange("g t s -> t g s")).then_inc(S["ws_in"], 16)
                    sp.dma_start(bs_row[0:1, :], T["sgu_b_s"][0:1].rearrange("a g t -> a (g t)")).then_inc(S["bs_in"], 16)
                    for dst, src in ((ln_g_row, T["sgu_ln_g"]), (ln_b_row, T["sgu_ln_b"])):
                        sp.dma_start(dst, src.to_broadcast([P, D])).then_inc(S["bs_in"], 16)
                if p == "N":
                    for a in range(2):
                        for g in range(2):
                            sp.dma_start(w1_sb[a][64 * g:64 * g + 64, :].rearrange("p (l f) -> p l f", f=64),
                                         T["nsa_cmp_w1_2"][0][a].rearrange("(l d) f -> d l f", d=64)).then_inc(S["w1_in"], 16)
                        sp.dma_start(w2_sb[a][0:64, :], T["nsa_cmp_w2_2"][0][a]).then_inc(S["w1_in"], 16)

            for p in phases:
                if p in FFNS:
                    ffn(p)
                    continue
                for m, src in enumerate(mixer_slabs(p)):
                    load(BASE[p] + m, 0, src)
                    if m == RAW - 1:
                        mixer_parameters(p)
            if phases[-1] in FFNS:
                load(nslabs, 0, down_src(phases[-1], FI - 1))
                sp.wait_ge(hi_done, nslabs + 1)
            sp.wait_ge(S["x_done"], x_count(phases[-1]) + (2 if phases[-1] in OUT_ROW else 0))
            sp.dma_start(out[0].rearrange("(t p) d -> p t d", p=P),
                         x[:, :].rearrange("p (t d) -> p t d", t=NT)).then_inc(S["stored"], 16)
            sp.wait_ge(S["stored"], 16)

        @block.gpsimd
        def _(pool):
            link = chain(pool, S["pool_chain"])
            const = S["const_done"]

            link(pool.memset(ones[:, :], 1.0))
            link(pool.memset(ident[:, :], 0.0))
            link(pool.affine_select(out=ident[:, :], in_=ident[:, :], compare_op=ALU.not_equal, fill=1.0, base=0,
                                    pattern=[[-1, P]], channel_multiplier=1))
            link(pool.memset(pair_ones[:, :], 0.0))
            link(pool.memset(pair_ones[0:64, 0:64], 1.0))
            link(pool.memset(pair_ones[64:P, 64:P], 1.0))
            pool.memset(eps_col, EPS).then_inc(const, 1)
            pool.wait_ge(const, 1)

            def gate_diag(p):
                g = phases.index(p)
                v = MODS[p][2]
                pool.wait_ge(S["mod_done"], v + 1)
                for h in range(2):
                    if g or h:
                        pool.wait_ge(S["gate_psum"], 2 * g + h)
                    pool.tensor_tensor(diag.rearrange("p (b f) -> p b f", b=4),
                                       ident[:, :].unsqueeze(1).to_broadcast([P, 4, P]),
                                       modcol[:, v * KB + 4 * h:v * KB + 4 * h + 4].unsqueeze(2).to_broadcast([P, 4, P]),
                                       ALU.mult).then_inc(S["diag_done"], 1)

            if "A" in phases:
                link(pool.memset(rel_rows[0:HEADS, :], -1e30))
                pool.wait_ge(S["rel_rows"], 16)
                starts = bucket_starts()
                for b in range(REL_BUCKETS):
                    n = starts[b + 1] - starts[b]
                    e = SEQ - starts[b]
                    ins = pool.tensor_copy(rel_rows[0:HEADS, e - n:e],
                                           rel_tab[0:HEADS, b:b + 1].to_broadcast([HEADS, n]))
                    link(ins)
                pool.dma_start(rel_dram, rel_rows[0:HEADS, :].unsqueeze(1).to_broadcast([HEADS, P, REL_W])).then_inc(S["rel_out"], 16)
                pool.wait_ge(S["rel_out"], 16)

            for p in phases:
                if p in FFNS:
                    if p in FIRST_VEC:
                        v = FIRST_VEC[p]
                        for k in range(KB):
                            ada_load(pool, v, k)
                        w = T["ada_w"] if v + 1 < V2 else T["ada_w_2"]
                        u, n = (v + 1, N_MOD) if v + 1 < V2 else (v + 1 - V2, N_MOD_2)
                        with pool.Fori(0, (FI - 3) // 2) as it:
                            for k in range(KB):
                                ada_load(pool, v + 1, k, it, w[u // n][k * P:(k + 1) * P, bass.ds(it * D + (u % n) * D, D)])
                    gate_diag(p)
                    continue
                gate_diag(p)
                if p in FIRST_VEC:
                    for k in range(KB):
                        ada_load(pool, FIRST_VEC[p], k)
                if p == "H":
                    hgrn_pool_masks(pool, link)
                if p == "N":
                    nsa_pool_tables(pool, link)
                if p == "G":
                    pool.wait_ge(S["ws_in"], 16)
                    v = ws_raw.rearrange("p (g s) -> p g s", g=8)
                    pool.affine_select(out=v, in_=v, compare_op=ALU.is_ge, fill=0.0, base=0,
                                       pattern=[[0, 8], [-1, P]], channel_multiplier=1).then_inc(S["ws_masked"], 1)
                if p == "H":
                    hgrn_pool_levels(pool)

        @block.tensor
        def _(pe):
            def slab_ready(s, it=0):
                pe.wait_ge(lo_done, s + 1 + RAW * it)

            def three(o, stat, mov, start, stop):
                pe.matmul(o, stat[0], mov[0], start=start, stop=False, skip_group_check=True)
                pe.matmul(o, stat[0], mov[1], start=False, stop=False, skip_group_check=True)
                return pe.matmul(o, stat[1], mov[0], start=False, stop=stop, skip_group_check=True)

            def col_product(s, dst, first_of=None):
                sl = (slab(hi, s, SPL), slab(lo, s, SPL))
                for k in range(KB):
                    if first_of is not None and k % 2 == 0:
                        pe.wait_ge(S["operand_ready"], 4 * OPND[first_of] + k // 2 + 1)
                    for b in range(2):
                        last = three(dst[:, b * SEQ:(b + 1) * SEQ], [t[:, k * SEQ + b * P:k * SEQ + (b + 1) * P] for t in sl],
                                     [op_k(t, k) for t in (operand_hi, operand_lo)], k == 0 and b == 0, k == KB - 1)
                last.then_inc(slab_used, 1)

            def row_product(s, stat, start, stop, last_of_phase=False):
                sl = (slab(hi, s, SPL), slab(lo, s, SPL))
                order = [(kk, t) for kk in range(2) for t in range(NT)]
                if last_of_phase:
                    order = [(kk, t) for t in range(NT) for kk in range(2)]
                for kk, t in order:
                    for part, parts in ((0, (0, 1)), (1, (0,))):
                        for q in parts:
                            for h in range(2):
                                last = pe.matmul(bank(dacc, 2 * t + h), stat(part, kk, t),
                                                 sl[q][:, kk * D + h * 512:kk * D + (h + 1) * 512],
                                                 start=(start and kk == 0 and part == 0 and q == 0),
                                                 stop=(stop and kk == 1 and part == 1), skip_group_check=True)
                    if last_of_phase and (kk, t) == (1, 0):
                        last.then_inc(S["tile_done"], 1)
                last.then_inc(slab_used, 1)

            def operand_stat(m):
                return lambda part, kk, t: op_k((operand_hi, operand_lo)[part], 2 * m + kk)[:, t * P:(t + 1) * P]

            def act_stat(i):
                def f(part, kk, t):
                    o = ((i % 2) * 2 + kk) * SEQ + t * P
                    return (act_hi, act_lo)[part][:, o:o + P]
                return f

            def ada_sum(v, it=0):
                pe.wait_ge(S["ada_step"], KB * (v + 1) + KB * it)
                if v >= 1:
                    pe.wait_ge(S["mod_done"], v + it)
                for k in range(KB):
                    last = pe.matmul(bank(misc, 1)[:, k:k + 1], ada_acc[:, k * P:(k + 1) * P], ones[:, 0:1],
                                     start=True, stop=True, skip_group_check=True)
                last.then_inc(S["ada_summed"], 1)

            def gate_spread(p):
                g = phases.index(p)
                for h in range(2):
                    pe.wait_ge(S["diag_done"], 2 * g + h + 1)
                    pe.matmul(bank(misc, h), ones[:, :], diag, start=True, stop=True).then_inc(S["gate_psum"], 1)

            def turn(norm):
                n = norms_feat.index(norm)
                for t in range(NT):
                    pe.wait_ge(S["normed_ready"], NT * n + t + 1)
                    for k in range(KB):
                        b = (bank(up, 0), bank(up, 1), bank(misc, 0), bank(misc, 1))[k // 2]
                        o = (k % 2) * SEQ + t * P
                        last = pe.transpose(b[:, o:o + P], normed[:, t * D + k * P:t * D + (k + 1) * P], ident[:, :])
                last.then_inc(S["turned"], 1)

            def ffn(p):
                b = BASE[p]
                u = lambda i, j: count_up(p, i, j)

                def ups(i, it=0):
                    for j in range(2):
                        s = b + (3 * i - 1 if i else 0) + j
                        slab_ready(s, it)
                        if u(i, j) >= 2:
                            pe.wait_ge(S["prod_done"], u(i, j) - 1 + 4 * it)
                        col_product(s, bank(up, j), p if (i, j) == (0, 0) else None)

                def down(i, it=0, start=False, stop=False):
                    s = b + (3 * i + 4 if i < FI - 1 else FFN_SLABS - 1)
                    slab_ready(s, it)
                    pe.wait_ge(S["actlo_done"], u(i, 1) + 1 + 4 * it)
                    row_product(s, act_stat(i), start, stop, last_of_phase=stop)

                v = FIRST_VEC.get(p)
                ups(0)
                ups(1)
                down(0, start=True)
                ups(2)
                down(1)
                with pe.Fori(0, (FI - 3) // 2) as it:
                    for i in (3, 4):
                        ups(i, it)
                        if v is not None and i == 3:
                            ada_sum(v, it)
                        down(i - 1, it)
                if v is not None:
                    ada_sum(v + 4)
                    pe.wait_ge(S["mod_done"], v + 5)
                gate_spread(p)
                down(FI - 1, stop=True)

            norms_feat = [p for p in phases]
            pe.wait_ge(S["c_in"], 32)
            pe.wait_ge(S["const_done"], 1)
            pe.transpose(bank(misc, 0)[:, 0:2 * KB], c_rows[0:2 * KB, :], ident[0:2 * KB, 0:2 * KB]).then_inc(S["c_psum"], 1)
            pe.wait_ge(S["rows_loaded"], 16 * len(rows_plan))
            for n, r in enumerate(tile_rows):
                last = pe.transpose(bank(up, 0)[:, n * P:n * P + r] if n < 4 else bank(up, 1)[:, (n - 4) * P:(n - 4) * P + r],
                                    rows_sb[0:r, n * P:(n + 1) * P], ident[0:r, 0:r])
            last.then_inc(S["cols_psum"], 1)
            for v in range(2):
                ada_sum(v)
            for p in phases:
                turn(p)
                if p in FFNS:
                    ffn(p)
                else:
                    PE_MIX[p](pe, slab_ready, col_product, row_product, operand_stat, ada_sum, gate_spread, three)

        @block.scalar
        def _(act):
            link = chain(act, S["act_chain"])

            def split_hi(s, it=0):
                if s >= nslabs:
                    return
                act.wait_ge(raw_full[s % RAW], 32 * (s // RAW + 1) + 32 * it)
                if s >= SPL:
                    act.wait_ge(slab_used, s - SPL + 1 + RAW * it)
                for take, put in split_views(s):
                    last = act.copy(put(slab(hi, s, SPL)), take(slab(raw, s, RAW)))
                last.then_inc(hi_done, 1)

            def norm(name):
                n = norm_list.index(name)
                act.activation(table_col, eps_col, ACT.Sqrt)
                for t in range(NT):
                    if n:
                        act.wait_ge(S["x_done"], x_before(name) - NT + t + 1)
                    elif t == 0:
                        act.wait_ge(S["x_loaded"], 16)
                    act.activation(normed[:, t * D:(t + 1) * D], x[:, t * D:(t + 1) * D], ACT.Square,
                                   accum_out=sumsq[:, t:t + 1]).then_inc(S["sumsq_done"], 1)
                    act.wait_ge(S["sumsq_done"], NT * n + t + 1)
                    act.activation(rstd[:, t:t + 1], sumsq[:, t:t + 1], ACT.Sqrt, scale=1.0 / D,
                                   bias=eps_col).then_inc(S["sqrt_done"], 1)
                if name.endswith("x"):
                    return
                if n == 0:
                    split_hi(0)
                    split_hi(1)
                f = phases.index(name)
                act.wait_ge(S["turned"], f + 1)
                act.wait_ge(S["shifted_d"], 5 * f + 1)
                v = MODS[name]

                def round_chunk(c):
                    act.copy(operand_hi[:, c * 512:(c + 1) * 512],
                             turned32[:, c * 512:(c + 1) * 512]).then_inc(S["operand_hi_done"], 1)

                for h in range(2):
                    ps = (bank(up, 0), bank(misc, 0))[h]
                    for k in (4 * h, 4 * h + 1):
                        act.activation(op_k(turned32, k), ps[:, (k % 2) * SEQ:(k % 2 + 1) * SEQ], ACT.Identity,
                                       scale=a_col[:, k:k + 1],
                                       bias=modcol[:, v[0] * KB + k:v[0] * KB + k + 1]).then_inc(S["shifted_a"], 1)
                    act.wait_ge(S["shifted_a"], 4 * f + 2 * h + 2)
                    round_chunk(2 * h)
                    act.wait_ge(S["shifted_d"], 5 * f + 2 * h + 3)
                    round_chunk(2 * h + 1)

            def gate(p):
                g = phases.index(p)
                act.wait_ge(S["gate_psum"], 2 * g + 2)
                if g:
                    act.wait_ge(S["x_done"], x_count(phases[g - 1]))
                act.activation(gate_row[:, :], misc[:, :], ACT.Copy,
                               scale=0.5 if p[0] == "F" else 1.0).then_inc(S["gate_done"], 1)

            def ffn(p):
                b = BASE[p]
                conv = p[0] == "C"

                def silu(s, i, j, it=0):
                    u = count_up(p, i, j)
                    act.wait_ge(slab_used, s + 1 + RAW * it)
                    if u >= 2:
                        act.wait_ge(S["prod_done"], u - 1 + 4 * it)
                    if conv:
                        act.activation(silu_sb[j], bank(up, j)[:, 0:SEQ], ACT.Identity, scale=tap(p, 2, i, j, it),
                                       bias=tap(p, 3, i, j, it)).then_inc(S["tap_a"], 1)
                        act.wait_ge(S["tap_d"], 2 * (u - 8 * FI) + 2 + 8 * it)
                        act.activation(silu_sb[j], silu_sb[j], ACT.Silu).then_inc(S["silu_done"], 1)
                    else:
                        act.activation(silu_sb[j], bank(up, j)[:, 0:SEQ], ACT.Silu).then_inc(S["silu_done"], 1)

                def hidden_hi(i, j, it=0):
                    act.wait_ge(S["prod_done"], count_up(p, i, j) + 1 + 4 * it)
                    o = ((i % 2) * 2 + j) * SEQ
                    act.copy(act_hi[:, o:o + SEQ], act32[j]).then_inc(S["acthi_done"], 1)

                def iteration(i, it=0):
                    a = b + 3 * i - 1
                    hidden_hi(i - 1, 1, it)
                    split_hi(a + 2, it)
                    split_hi(a + 3, it)
                    silu(a, i, 0, it)
                    split_hi(a + 4, it)
                    silu(a + 1, i, 1, it)
                    hidden_hi(i, 0, it)

                split_hi(b + 2)
                split_hi(b + 3)
                silu(b, 0, 0)
                silu(b + 1, 0, 1)
                hidden_hi(0, 0)
                iteration(1)
                iteration(2)
                with act.Fori(0, (FI - 3) // 2) as it:
                    iteration(3, it)
                    iteration(4, it)
                hidden_hi(FI - 1, 1)
                split_hi(b + FFN_SLABS + 1)
                gate(p)

            def head_norm(inst, src):
                for c in range(4):
                    act.activation(hn_sq_sb[c % 2], src[:, c * 512:(c + 1) * 512], ACT.Square).then_inc(S["hn_sq"], 1)
                    act.wait_ge(S["hn_ss"], 4 * inst + c + 1)
                    if c >= 2:
                        act.wait_ge(S["row_free"], 4 * inst + c - 1)
                    act.activation(hn_rs_sb[c % 2], bank(misc, c % 2), ACT.Sqrt, scale=1.0 / P,
                                   bias=eps_col).then_inc(S["hn_rs"], 1)
                    act.wait_ge(S["row_free"], 4 * inst + c + 1)
                    act.copy(operand_hi[:, c * 512:(c + 1) * 512], src[:, c * 512:(c + 1) * 512]).then_inc(S["hn_hi"], 1)

            act.wait_ge(S["c_psum"], 1)
            act.activation(c_col, bank(misc, 0)[:, 0:2 * KB], ACT.Silu).then_inc(S["c_ready"], 1)
            for p in phases:
                norm(p)
                if p in FFNS:
                    ffn(p)
                else:
                    ACT_MIX[p](act, link, split_hi, gate, head_norm)
                if p in OUT_ROW:
                    norm(p + "x")

        @block.vector
        def _(dve):
            link = chain(dve, S["dve_chain"])

            def split_lo(s, it=0):
                if s >= nslabs:
                    return
                dve.wait_ge(hi_done, s + 1 + RAW * it)
                for take, put in split_views(s):
                    last = dve.tensor_tensor(put(slab(lo, s, SPL)), take(slab(raw, s, RAW)),
                                             put(slab(hi, s, SPL)).bitcast(F32), ALU.subtract)
                last.then_inc(lo_done, 1)

            def ada_tile(v, k, it=0):
                m = v * KB + k
                t = ada[:, (m % ATILES) * D:(m % ATILES + 1) * D]
                c = c_col[:, (8 if v >= V2 else 0) + k:(8 if v >= V2 else 0) + k + 1]
                if v < 2:
                    dve.wait_ge(ada_first[m % ATILES], 16 * (m // ATILES + 1))
                else:
                    dve.wait_ge(ada_full[m % ATILES], 16 * (m // ATILES + 1 - FIRST_ROUNDS) + 32 * it)
                if k == 0:
                    if v:
                        dve.wait_ge(S["ada_summed"], v + it)
                    dve.tensor_scalar(ada_acc[:, :], t, c, None, ALU.mult).then_inc(S["ada_step"], 1)
                else:
                    dve.wait_ge(S["ada_step"], m + KB * it)
                    dve.scalar_tensor_tensor(ada_acc[:, :], t, c, ada_acc[:, :], ALU.mult,
                                             ALU.add).then_inc(S["ada_step"], 1)

            def mod_vector(v, it=0):
                dve.wait_ge(S["ada_summed"], v + 1 + it)
                if isinstance(it, int):
                    o, b = modcol[:, v * KB:(v + 1) * KB], cols[:, v * KB:(v + 1) * KB]
                else:
                    o, b = modcol[:, bass.ds(it * KB + v * KB, KB)], cols[:, bass.ds(it * KB + v * KB, KB)]
                dve.tensor_tensor(o, bank(misc, 1)[:, 0:KB], b, ALU.add).then_inc(S["mod_done"], 1)

            def norm(name):
                n = norm_list.index(name)

                def root_taken(t):
                    dve.wait_ge(S["sqrt_done"], NT * n + t + 1)
                    link(dve.reciprocal(rstd[:, t:t + 1], rstd[:, t:t + 1]))

                if name.endswith("x"):
                    dve.wait_ge(S["row_in"], 16 * (out_norms.index(name[:-1]) + 1))
                    for t in range(NT):
                        root_taken(t)
                        xt = x[:, t * D:(t + 1) * D]
                        dve.scalar_tensor_tensor(xt, xt, rstd[:, t:t + 1], out_row, ALU.mult,
                                                 ALU.mult).then_inc(S["x_done"], 1)
                    dve.wait_ge(S["x_done"], x_count(name[:-1]) + 2)
                    return
                f = phases.index(name)
                for t in range(NT):
                    root_taken(t)
                    dve.tensor_scalar(normed[:, t * D:(t + 1) * D], x[:, t * D:(t + 1) * D], rstd[:, t:t + 1],
                                      None, ALU.mult).then_inc(S["normed_ready"], 1)
                if n == 0:
                    split_lo(1)
                v = MODS[name]
                dve.wait_ge(S["mod_done"], v[1] + 1)
                g, l = GAIN[name]
                dve.scalar_tensor_tensor(a_col, modcol[:, v[1] * KB:(v[1] + 1) * KB], 1.0, gain_cols(g, l),
                                         ALU.add, ALU.mult).then_inc(S["shifted_d"], 1)
                dve.wait_ge(S["shifted_d"], 5 * f + 1)
                dve.wait_ge(S["turned"], f + 1)
                for h in range(2):
                    ps = (bank(up, 1), bank(misc, 1))[h]
                    for k in (4 * h + 2, 4 * h + 3):
                        dve.tensor_scalar(op_k(turned32, k), ps[:, (k % 2) * SEQ:(k % 2 + 1) * SEQ],
                                          a_col[:, k:k + 1], modcol[:, v[0] * KB + k:v[0] * KB + k + 1],
                                          ALU.mult, ALU.add).then_inc(S["shifted_d"], 1)
                    for c in (2 * h, 2 * h + 1):
                        dve.wait_ge(S["operand_hi_done"], 4 * f + c + 1)
                        o = slice(c * 512, (c + 1) * 512)
                        dve.tensor_tensor(operand_lo[:, o], turned32[:, o], operand_hi[:, o].bitcast(F32),
                                          ALU.subtract).then_inc(S["operand_ready"], 1)

            def residual(p):
                g = phases.index(p)
                dve.wait_ge(S["gate_done"], g + 1)
                for t in range(NT):
                    if t == 0:
                        dve.wait_ge(S["tile_done"], g + 1)
                    else:
                        dve.wait_ge(slab_used, BASE[p] + SLABS_OF.get(p, FFN_SLABS))
                    o = slice(t * D, (t + 1) * D)
                    link(dve.tensor_tensor(resid_tmp[:, o], dacc[:, o], gate_row[:, :], ALU.mult))
                    dve.tensor_tensor(x[:, o], x[:, o], resid_tmp[:, o], ALU.add).then_inc(S["x_done"], 1)
                dve.wait_ge(S["x_done"], x_count(p))

            def ffn(p):
                b = BASE[p]
                conv = p[0] == "C"

                def product(i, j, it=0):
                    u = count_up(p, i, j)
                    if conv:
                        uc = u - 8 * FI
                        dve.wait_ge(S["tap_a"], uc + 1 + 4 * it)
                        g = bank(up, j)[:, 0:SEQ]
                        dve.scalar_tensor_tensor(silu_sb[j][:, 1:SEQ], g[:, 0:SEQ - 1], tap(p, 1, i, j, it),
                                                 silu_sb[j][:, 1:SEQ], ALU.mult, ALU.add).then_inc(S["tap_d"], 1)
                        dve.wait_ge(S["tap_d"], 2 * uc + 1 + 8 * it)
                        dve.scalar_tensor_tensor(silu_sb[j][:, 2:SEQ], g[:, 0:SEQ - 2], tap(p, 0, i, j, it),
                                                 silu_sb[j][:, 2:SEQ], ALU.mult, ALU.add).then_inc(S["tap_d"], 1)
                    dve.wait_ge(S["silu_done"], u + 1 + 4 * it)
                    if u >= 2:
                        dve.wait_ge(S["actlo_done"], u - 1 + 4 * it)
                    dve.tensor_tensor(act32[j], silu_sb[j], bank(up, j)[:, SEQ:2 * SEQ],
                                      ALU.mult).then_inc(S["prod_done"], 1)

                def hidden_lo(i, j, it=0):
                    dve.wait_ge(S["acthi_done"], count_up(p, i, j) + 1 + 4 * it)
                    o = ((i % 2) * 2 + j) * SEQ
                    dve.tensor_tensor(act_lo[:, o:o + SEQ], act32[j], act_hi[:, o:o + SEQ].bitcast(F32),
                                      ALU.subtract).then_inc(S["actlo_done"], 1)

                def iteration(i, it=0, vec=None, k0=0, count=(0, 2, 2), summed=None):
                    a = b + 3 * i - 1
                    k = k0

                    def some(n, k):
                        for q in range(n if vec is not None else 0):
                            ada_tile(vec, k + q, it)
                        return k + n
                    hidden_lo(i - 1, 1, it)
                    split_lo(a + 2, it)
                    k = some(count[0], k)
                    split_lo(a + 3, it)
                    product(i, 0, it)
                    k = some(count[1], k)
                    split_lo(a + 4, it)
                    product(i, 1, it)
                    hidden_lo(i, 0, it)
                    if summed is not None:
                        mod_vector(summed, it)
                    some(count[2], k)

                v = FIRST_VEC.get(p)
                split_lo(b + 2)
                split_lo(b + 3)
                product(0, 0)
                product(0, 1)
                hidden_lo(0, 0)
                iteration(1, 0, v, 0, (0, 2, 2))
                iteration(2, 0, v, 4, (2, 1, 1))
                with dve.Fori(0, (FI - 3) // 2) as it:
                    iteration(3, it, None if v is None else v + 1, 0, (0, 0, 2), summed=v)
                    iteration(4, it, None if v is None else v + 1, 2, (2, 2, 2))
                hidden_lo(FI - 1, 1)
                if v is not None:
                    mod_vector(v + 4)
                split_lo(b + FFN_SLABS + 1)
                residual(p)

            def head_norm(inst, src, gain, gate=None):
                for c in range(4):
                    o = slice(c * 512, (c + 1) * 512)
                    dve.wait_ge(S["hn_rs"], 4 * inst + c + 1)
                    link(dve.reciprocal(hn_rs_sb[c % 2], hn_rs_sb[c % 2]))
                    ins = dve.scalar_tensor_tensor(src[:, o], src[:, o], gain, hn_rs_sb[c % 2], ALU.mult, ALU.mult)
                    if gate is not None:
                        link(ins)
                        dve.wait_ge(S["silu_g"], 1)
                        ins = dve.tensor_tensor(src[:, o], src[:, o], gate[:, o], ALU.mult)
                    ins.then_inc(S["row_free"], 1)
                    dve.wait_ge(S["hn_hi"], 4 * inst + c + 1)
                    dve.tensor_tensor(operand_lo[:, o], src[:, o], operand_hi[:, o].bitcast(F32),
                                      ALU.subtract).then_inc(S["operand_ready"], 1)

            dve.wait_ge(S["c_ready"], 1)
            for k in range(KB):
                ada_tile(0, k)
            dve.wait_ge(S["cols_psum"], 1)
            for t in range(6):
                r = tile_rows[t]
                ps = bank(up, 0)[:, t * P:t * P + r] if t < 4 else bank(up, 1)[:, (t - 4) * P:(t - 4) * P + r]
                link(dve.tensor_copy(cols[:, t * P:t * P + r], ps))
            link(dve.tensor_copy(qk_gain[:, 1:2], cols[:, 2 * P + 99:2 * P + 100]))
            link(dve.tensor_scalar(head_gain, cols[:, 2 * P + 96:2 * P + 97], 1.0 - LAMBDA_INIT, None, ALU.mult))
            link(dve.tensor_scalar(qk_gain[:, 0:1], cols[:, 2 * P + 98:2 * P + 99], float(NSA_HD) ** -0.5, None,
                                   ALU.mult))
            mod_vector(0)
            for k in range(KB):
                ada_tile(1, k)
            split_lo(0)
            mod_vector(1)
            for p in phases:
                norm(p)
                if p in FFNS:
                    ffn(p)
                else:
                    DVE_MIX[p](dve, link, split_lo, ada_tile, mod_vector, residual, head_norm)
                if p in OUT_ROW:
                    norm(p + "x")


def kernel(**inputs):
    import numpy as _np
    import concourse.bacc as _bacc
    from concourse import mybir as _mybir
    from concourse.bass_utils import run_bass_kernel_spmd as _run

    nc = _bacc.Bacc("TRN2", target_bir_lowering=False, num_devices=1)
    arrays, tensors = {}, {}
    for name, value in inputs.items():
        a = _np.ascontiguousarray(value)
        arrays[f"in_{name}_dram"] = a
        tensors[name] = nc.dram_tensor(f"in_{name}_dram", a.shape, _mybir.dt.from_np(a.dtype),
                                       kind="ExternalInput").ap()
    out = nc.dram_tensor("out_0_dram", (1, SEQ, D), F32, kind="ExternalOutput").ap()
    build(nc, tensors, out)
    r = _run(nc, [arrays], core_ids=[0])
    return r.results[0]["out_0_dram"]
```

```python
import math
from contextlib import ExitStack

import numpy as np
import concourse.bass as bass
from concourse import mybir

F32 = mybir.dt.float32
F32R = mybir.dt.float32r
U32 = mybir.dt.uint32
I32 = mybir.dt.int32
ALU = mybir.AluOpType
ACT = mybir.ActivationFunctionType
AX = mybir.AxisListType.X

P = 128
SEQ = 256
NT = SEQ // P
D = 1024
KB = D // P
DFF = 2816
FI = DFF // 256
EPS = 1e-6
SLAB = 2048
RAW = 6
SPL = 3
WARM = 8
ATILES = 4
N_MOD = 9
N_MOD_2 = 6
HEADS = 8
REL_BUCKETS = 32
REL_MAX_DIST = 128
REL_W = 3 * P
LAMBDA_INIT = 0.8 - 0.6 * math.exp(-0.3 * 0)
NSA_HEADS = 16
NSA_KV = 4
NSA_HPG = NSA_HEADS // NSA_KV
NSA_HD = 64
CMP_LEN = 32
CMP_STRIDE = 16
NC = (SEQ - CMP_LEN) // CMP_STRIDE + 1
FAR = 1e32

FFN_SLABS = 3 * FI
PHASES = ["F0", "A", "F1", "F2", "G", "F3", "H", "C0", "N", "C1"]
SLABS_OF = {"A": 16, "G": 12, "H": 20, "N": 15}
BASE = {}
_n = 0
for _p in PHASES:
    BASE[_p] = _n
    _n += SLABS_OF.get(_p, FFN_SLABS)
FFNS = [p for p in PHASES if p[0] in "FC"]

V2 = 2 * N_MOD
MODS = {"F0": (0, 1, 2), "A": (3, 4, 5), "F1": (6, 7, 8), "F2": (9, 10, 11), "G": (12, 13, 14),
        "F3": (15, 16, 17), "H": (V2, V2 + 1, V2 + 2), "C0": (V2 + 3, V2 + 4, V2 + 5),
        "N": (V2 + 6, V2 + 7, V2 + 8), "C1": (V2 + 9, V2 + 10, V2 + 11)}
NV = V2 + 2 * N_MOD_2
FIRST_VEC = {"F0": 2, "A": 7, "F1": 8, "F2": 13, "F3": 18, "H": 23, "C0": 24, "N": 29}
OPND = {}
for _p in PHASES:
    OPND[_p] = len(OPND)
    if _p in SLABS_OF:
        OPND[_p + "o"] = len(OPND)


def bucket_starts():
    exact = REL_BUCKETS // 2
    n = np.arange(SEQ)
    nf = np.maximum(n, 1).astype(np.float32)
    large = exact + (np.log(nf / np.float32(exact)) / np.float32(math.log(REL_MAX_DIST / exact))
                     * (REL_BUCKETS - exact)).astype(np.int32)
    b = np.where(n < exact, n, np.minimum(large, REL_BUCKETS - 1))
    return [int(np.searchsorted(b, k)) for k in range(REL_BUCKETS)] + [SEQ]


def build(nc, T, out):
    phases = PHASES
    nslabs = sum(SLABS_OF.get(p, FFN_SLABS) for p in phases)
    with ExitStack() as ctx:
        def sb(name, cols, dt=F32):
            return ctx.enter_context(nc.sbuf_tensor(name, [P, cols], dt))

        def sem(name):
            return ctx.enter_context(nc.semaphore(name))

        raw = sb("raw", RAW * SLAB)
        hi = sb("hi", SPL * SLAB, F32R)
        lo = sb("lo", SPL * SLAB, F32R)
        ada = sb("ada", ATILES * D)
        ada_acc = sb("ada_acc", D)
        operand_hi = sb("operand_hi", KB * SEQ, F32R)
        operand_lo = sb("operand_lo", KB * SEQ, F32R)
        x = sb("x", NT * D)
        gate_row = sb("gate_row", D)
        cols = sb("cols", 6 * P)
        modcol = sb("modcol", NV * KB)
        ident = sb("ident", P)
        ones = sb("ones", P)
        pair_ones = sb("pair_ones", P)
        act_hi = sb("act_hi", 2 * 2 * SEQ, F32R)
        act_lo = sb("act_lo", 2 * 2 * SEQ, F32R)
        small = sb("small", 160)
        work = sb("work", 12500)

        def view(a, b):
            return work[:, a:b]

        def slab(t, s, n):
            return t[:, (s % n) * SLAB:(s % n + 1) * SLAB]

        def op_k(t, k):
            return t[:, k * SEQ:(k + 1) * SEQ]

        sumsq = small[:, 0:2]
        rstd = small[:, 2:4]
        eps_col = small[:, 4:5]
        a_col = small[:, 8:16]
        c_col = small[:, 16:32]
        neg_lam = small[:, 32:33]
        lam_s = small[:, 33:37]
        qk_gain = small[:, 38:40]
        head_gain = small[:, 40:41]
        nmax = small[:, 128:140]
        sums = small[:, 140:152]
        coef = small[:, 44:56]
        lb_col = small[:, 68:76]
        oml_col = small[:, 76:84]
        lb_tmp = small[:, 84:108]
        head_ms = small[:, 84:100]
        bn = small[:, 108:120]
        bn_out = small[:, 120:124]
        table_col = small[:, 124:125]

        dacc = ctx.enter_context(nc.psum_tensor("dacc", [P, NT * D], F32))
        up = ctx.enter_context(nc.psum_tensor("up", [P, 2 * 512], F32))
        misc = ctx.enter_context(nc.psum_tensor("misc", [P, 2 * 512], F32))

        def bank(t, j):
            return t[:, j * 512:(j + 1) * 512]

        rel_dram = nc.dram_tensor("rel_scratch", [HEADS, P, REL_W], F32, kind="Internal").ap()

        raw_full = [sem(f"raw_full{i}") for i in range(RAW)]
        ada_full = [sem(f"ada_full{i}") for i in range(ATILES)]
        ada_first = [sem(f"ada_first{i}") for i in range(ATILES)]
        FIRST_ROUNDS = 2 * KB // ATILES
        names = """hi_done lo_done slab_used x_loaded rows_loaded const_done c_in c_psum cols_psum c_ready
            ada_step ada_summed mod_done diag_done gate_psum gate_done sumsq_done sqrt_done normed_ready turned
            shifted_a shifted_d operand_hi_done operand_ready x_done tile_done silu_done prod_done acthi_done
            actlo_done tap_a tap_d sq_done ss_done rs_done qk_done v_done qk_logits biased maxed expd attn_done
            turned_p p_done pv_done o_done lam_in lam_exp lam_done rel_rows rel_out rel_in hn_sq hn_root
            hn_scaled hn_turned hn_hi row_in gelu_done ln_sqrt ln_done ws_in ws_masked ws_turned ws_done mixed
            bs_in ln_stats gated gated_hi level_diff level_exp level_w level_s level_done ho_psum ho_done
            hq_done hk_done sg_done own_done own_kept f_done scanned logf_done lb_a lb_d mask_done g_taken
            hv_done silu_g dist_done nq_done nk_done w1_in hid_pe hid_act kc_pe kc_done nv_done ngate_done
            cl_done cs_done cexp_done cp_done npt_pe npt_done no_done windows_done nqk_pe nb_done nmax_done
            nexp_done nscaled npv_pe no_hi act_chain dve_chain pool_chain stored""".split()
        S = {n: sem(n) for n in names}
        hi_done, lo_done, slab_used = S["hi_done"], S["lo_done"], S["slab_used"]

        block = ctx.enter_context(nc.Block())

        def chain(eng, s):
            count = [0]

            def link(ins):
                count[0] += 1
                ins.then_inc(s, 1)
                eng.wait_ge(s, count[0])
            return link

        col_at = {"ada": 0}
        rows_plan = []
        for li, name in enumerate(["ln_ffn1", "ln_mix", "ln_ffn2", "norm_mix_2", "norm_ffn_2"]):
            rows_plan.append((2, 16 * li, T[name].rearrange("l (k p) -> (l k) p", p=P), 0))
            col_at[name] = 2 * P + 16 * li
        rows_plan += [(2, 80, T["hg_lb_2"].rearrange("l (k p) -> (l k) p", p=P), 0),
                      (2, 96, T["attn_subln"], 0), (2, 97, T["hg_gnorm_2"], 0)]
        for o in (0, 64):
            rows_plan += [(2, 98, T["attn_q_norm"], o), (2, 99, T["attn_k_norm"], o),
                          (3, 0, T["nsa_cmp_pe_2"].rearrange("a b l d -> (a b l) d"), o)]
        rows_plan += [(0, 0, T["ada_b"].rearrange("l (k p) -> (l k) p", p=P)[0:P, :], 0),
                      (1, 0, T["ada_b"].rearrange("l (k p) -> (l k) p", p=P)[P:144, :], 0),
                      (1, 16, T["ada_b_2"].rearrange("l (k p) -> (l k) p", p=P), 0)]
        for l in range(2):
            rows_plan += [(4 + l, 0, T["ffn_conv_w_2"][l].rearrange("w (k p) -> (w k) p", p=P), 0),
                          (4 + l, 66, T["ffn_conv_b_2"][l:l + 1].rearrange("l (k p) -> (l k) p", p=P), 0)]
        tile_rows = [128, 112, 100, 64, 88, 88]

        def gain_cols(name, layer):
            return cols[:, col_at[name] + 8 * layer:col_at[name] + 8 * layer + 8]

        GAIN = {"F0": ("ln_ffn1", 0), "A": ("ln_mix", 0), "F1": ("ln_ffn2", 0), "F2": ("ln_ffn1", 1),
                "G": ("ln_mix", 1), "F3": ("ln_ffn2", 1), "H": ("norm_mix_2", 0), "C0": ("norm_ffn_2", 0),
                "N": ("norm_mix_2", 1), "C1": ("norm_ffn_2", 1)}
        ffn_w = {"F0": ("ffn1_wg", "ffn1_wu", "ffn1_wd", 0), "F1": ("ffn2_wg", "ffn2_wu", "ffn2_wd", 0),
                 "F2": ("ffn1_wg", "ffn1_wu", "ffn1_wd", 1), "F3": ("ffn2_wg", "ffn2_wu", "ffn2_wd", 1)}

        def ffn_sources(p):
            if p in ffn_w:
                g, u, d, l = ffn_w[p]
                return T[g][l], T[u][l], T[d][l]
            l = int(p[1])
            return T["ffn_w_up_2"][l][:, 0:DFF], T["ffn_w_up_2"][l][:, DFF:2 * DFF], T["ffn_w_down_2"][l]

        OUT_ROW = {"F1": T["ln_out"][0:1, :], "F3": T["ln_out"][1:2, :],
                   "C1": T["final_norm_2"].rearrange("(a d) -> a d", a=1)}
        out_norms = [p for p in phases if p in OUT_ROW]
        norm_list = []
        for p in phases:
            norm_list.append(p)
            if p in OUT_ROW:
                norm_list.append(p + "x")

        def x_count(p):
            n = 0
            for q in phases:
                n += 2
                if q == p:
                    return n
                if q in OUT_ROW:
                    n += 2

        def x_before(norm):
            if norm.endswith("x"):
                return x_count(norm[:-1])
            i = phases.index(norm)
            if i == 0:
                return 0
            return x_count(phases[i - 1]) + (2 if phases[i - 1] in OUT_ROW else 0)

        def count_up(p, i):
            return FFNS.index(p) * FI + i

        def tap(p, w, i, j, it=0):
            o = (4 + int(p[1])) * P + 22 * w + 2 * i + j
            return cols[:, o:o + 1] if isinstance(it, int) else cols[:, bass.ds(it * 4 + o, 1)]

        normed = view(0, 2048)
        turned32 = view(2048, 4096)
        silu_sb = view(4096, 4608)
        act32 = view(4608, 5120)
        rows_sb = view(6144, 6144 + 6 * P)
        out_row = view(10900, 11924)
        resid_tmp = view(0, 2048)
        qT = view(0, 2048)
        kT = view(2048, 4096)

        v_sb = view(4096, 6144)
        rel_bias = view(6144, 9216).rearrange("p (h k) -> p h k", h=HEADS)
        sq_sb = [view(9216 + 512 * j, 9728 + 512 * j) for j in range(2)]
        rs_sb = [view(10240 + 512 * j, 10752 + 512 * j) for j in range(2)]
        prob = [view(9216 + 768 * j, 9984 + 768 * j) for j in range(3)]
        attn = [view(11520, 11904), view(11904, 12288), ada_acc[:, 0:3 * P]]
        rel_rows = view(6912, 6912 + REL_W)
        rel_tab = view(7424, 7456)
        lam_in = view(11264, 11520)
        c_rows = view(7712, 7840)
        vg_sb = view(2048, 4096)
        ws_raw = view(4096, 5120)
        ws_t = view(5120, 6144)
        ln_g_row, ln_b_row = view(6144, 7168), view(7168, 8192)
        bs_row = view(8192, 9216)
        b_sb = view(4096, 6144)
        hv_sb = view(6144, 8192)
        wlev = [view(8192, 8704), view(8704, 9216), view(11988, 12500), ada_acc[:, 0:512]]
        pt_sb = [view(9216 + 768 * j, 9984 + 768 * j) for j in range(2)]
        masks = view(10752, 11648)
        restart = view(11648, 11904)
        ks_t, kw_t, kc_t, vc_t = (view(2048 + 512 * j, 2560 + 512 * j) for j in range(4))
        vs_sb, vw_sb = view(4096, 4608), view(4608, 5120)
        w1_sb = [view(5120 + 2048 * j, 7168 + 2048 * j) for j in range(2)]
        w2_sb = [view(9216 + 64 * j, 9280 + 64 * j) for j in range(2)]
        n_prob = [view(5120 + 768 * j, 5888 + 768 * j) for j in range(3)]
        n_pt = [view(7424 + 768 * j, 8192 + 768 * j) for j in range(2)]
        gates = view(9344, 9440)
        kc2 = view(9440, 9500)
        vc_sb = view(9504, 9760)
        hid = [view(9760 + 60 * j, 9820 + 60 * j) for j in range(2)]
        dist = view(9888, 10272)
        cbias = view(10272, 10752)
        windows = [view(10752, 11712), ada_acc[:, 0:960]]
        c_prob = view(10752, 11232)
        c_pt = [view(11232 + 256 * j, 11488 + 256 * j) for j in range(2)]
        n_small = view(11712, 11988)
        diag = [view(11988, 12500), view(5376, 5888)]

        def col_slab(w, c0):
            v = w[:, c0:c0 + 256].rearrange("(k p) n -> p k n", p=P)
            return [(lambda t, a=a: t.rearrange("p (k n) -> p k n", k=KB)[:, 4 * a:4 * a + 4, :],
                     v[:, 4 * a:4 * a + 4, :]) for a in range(2)]

        def row_slab(w, m):
            return [(lambda t, a=a: t[:, a * D:(a + 1) * D], w[(2 * m + a) * P:(2 * m + a + 1) * P, :])
                    for a in range(2)]

        def mixer_slabs(p):
            if p == "A":
                w = T["attn_w_qkv"][0]
                return ([col_slab(w, 256 * m) for m in range(8)] + [row_slab(w[:, 2048:3072], m) for m in range(4)]
                        + [row_slab(T["attn_w_o"][0], m) for m in range(4)])
            if p == "G":
                w = T["sgu_w_in"][0]
                return ([row_slab(w[:, 1024:2048], m) for m in range(4)] + [col_slab(w, 256 * m) for m in range(4)]
                        + [row_slab(T["sgu_w_out"][0], m) for m in range(4)])
            if p == "H":
                w = T["hg_w_in_2"][0]
                return ([col_slab(w, (1024 + 256 * m) % 2048) for m in range(8)]
                        + [row_slab(w[:, 2048:3072], m) for m in range(4)]
                        + [col_slab(w, 3072 + 256 * m) for m in range(4)]
                        + [row_slab(T["hg_w_out_2"][0], m) for m in range(4)])
            w = T["nsa_w_in_2"][0]
            wo = T["nsa_w_out_2"][0]
            res = [col_slab(w, D)]
            for m in range(4):
                src = []
                for g in range(2):
                    c0 = ((m // 2) * 2 * NSA_HPG + g * NSA_HPG + 2 * (m % 2)) * NSA_HD
                    src.append((lambda t, g=g: t.rearrange("p (k n) -> p k n", k=KB)[:, :, g * P:(g + 1) * P],
                                w[:, c0:c0 + P].rearrange("(k p) n -> p k n", p=P)))
                res.append(src)
            for c0 in (1280, 1536, 2048, 1792, 2304, 2608 - 256):
                res.append(col_slab(w, c0))
            for m in range(4):
                src = []
                for g in range(2):
                    r0 = ((m // 2) * 2 * NSA_HPG + g * NSA_HPG + 2 * (m % 2)) * NSA_HD
                    src.append((lambda t, g=g: t[g * 64:(g + 1) * 64, :].rearrange("p (b n) -> p b n", b=2),
                                wo[r0:r0 + P, :].rearrange("(b r) n -> r b n", b=2)))
                res.append(src)
            return res

        def split_views(s):
            if not BASE["N"] < s <= BASE["N"] + 4:
                return [(lambda t: t, lambda t: t)]
            return [(lambda t, c=c: t.rearrange("p (k g n) -> p k g n", k=KB, g=2)[:, :, :, c * 64:(c + 1) * 64],
                     lambda t, c=c: t.rearrange("p (k c g n) -> p k c g n", k=KB, c=2, g=2)[:, :, c]) for c in range(2)]

        PE_MIX, ACT_MIX, DVE_MIX = {}, {}, {}
        ab_banks = [bank(up, 0), bank(up, 1)] + [bank(dacc, j) for j in range(4)]
        sgu_banks = [bank(up, 0), bank(up, 1), bank(dacc, 0), bank(dacc, 1)]
        nsa_banks = [bank(up, 0), bank(up, 1), bank(misc, 0), bank(misc, 1)] + [bank(dacc, j) for j in range(4)]

        def pe_out(p, pe, slab_ready, row_product, operand_stat):
            b = BASE[p] + SLABS_OF[p] - 4
            for m in range(4):
                slab_ready(b + m)
                pe.wait_ge(S["operand_ready"], 4 * OPND[p + "o"] + m + 1)
                row_product(b + m, operand_stat(m), m == 0, m == 3, last_of_phase=(m == 3))

        hn_banks = [bank(up, 0), bank(up, 1), bank(misc, 0), bank(misc, 1)]

        def pe_head_turn(pe, inst, src):
            for c in range(4):
                pe.wait_ge(S["hn_scaled"], 4 * inst + c + 1)
                for j in range(4):
                    last = pe.transpose(hn_banks[c][:, j * P:(j + 1) * P], src[:, (4 * c + j) * P:(4 * c + j + 1) * P],
                                        ident[:, :])
                last.then_inc(S["hn_turned"], 1)

        def act_head_squares(act, inst, first, src):
            for j in range(src.shape[1] // P):
                n = 16 * inst + first + j
                if n >= 4:
                    act.wait_ge(S["hn_sq"], n - 3)
                o = 512 + (n % 4) * P
                act.activation(ada_acc[:, o:o + P], src[:, j * P:(j + 1) * P], ACT.Square,
                               accum_out=head_ms[:, first + j:first + j + 1]).then_inc(S["hn_sq"], 1)

        def pe_attention(pe, slab_ready, col_product, row_product, operand_stat, ada_sum, gate_spread, token_product):
            b = BASE["A"]

            def square_sum(m):
                pe.wait_ge(S["sq_done"], m + 1)
                if m == 0:
                    pe.wait_ge(S["gate_done"], phases.index("A") + 1)
                if m >= 2:
                    pe.wait_ge(S["rs_done"], m - 1)
                pe.matmul(bank(misc, m % 2), pair_ones[:, :], sq_sb[m % 2], start=True, stop=True).then_inc(S["ss_done"], 1)

            for m in range(8):
                slab_ready(b + m)
                if m >= 6:
                    pe.wait_ge(S["qk_done"], m - 5)
                col_product(b + m, ab_banks[m % 6], "A" if m == 0 else None)
                if m == 0:
                    pe.wait_ge(S["operand_ready"], 4 * OPND["A"] + 4)
                    gate_spread("A")
                if m:
                    square_sum(m - 1)
            pe.wait_ge(S["qk_done"], 6)
            for m in range(4):
                slab_ready(b + 8 + m)
                row_product(b + 8 + m, operand_stat(m), m == 0, m == 3)
                if m == 0:
                    square_sum(7)
            pe.wait_ge(S["rs_done"], 8)
            ada_sum(7)

            def logits(h):
                if h >= 2:
                    pe.wait_ge(S["biased"], 2 * (h - 1))
                else:
                    pe.wait_ge(S["qk_done"], 8)
                    pe.wait_ge(S["mod_done"], 8)
                for c in range(2):
                    q = qT[64 * c:64 * c + 64, h * SEQ:(h + 1) * SEQ]
                    k = kT[64 * c:64 * c + 64, h * SEQ:(h + 1) * SEQ]
                    o = bank((up, misc)[c], h % 2)
                    pe.matmul(o[:, 0:SEQ], q[:, P:SEQ], k, start=True, stop=True, skip_group_check=True)
                    last = pe.matmul(o[:, SEQ:3 * P], q[:, 0:P], k[:, 0:P], start=True, stop=True,
                                     skip_group_check=True)
                last.then_inc(S["qk_logits"], 1)

            def turn_probs(h):
                pe.wait_ge(S["attn_done"], h + 1)
                if h == 0:
                    pe.wait_ge(S["v_done"], 1)
                if h >= 2:
                    pe.wait_ge(S["p_done"], h - 1)
                for j in range(3):
                    last = pe.transpose(bank(dacc, h % 2)[:, j * P:(j + 1) * P], attn[h % 3][:, j * P:(j + 1) * P],
                                        ident[:, :])
                last.then_inc(S["turned_p"], 1)

            def values(h):
                pe.wait_ge(S["p_done"], h + 1)
                if h >= 2:
                    pe.wait_ge(S["o_done"], h - 1)
                o = bank(dacc, 2 + h % 2)
                v = [v_sb[:, t * D + h * P:t * D + (h + 1) * P] for t in range(NT)]
                pt = attn[h % 3]
                pe.matmul(o[:, P:SEQ], pt[:, 0:P], v[0], start=True, stop=False, skip_group_check=True)
                pe.matmul(o[:, P:SEQ], pt[:, P:2 * P], v[1], start=False, stop=True, skip_group_check=True)
                pe.matmul(o[:, 0:P], pt[:, 2 * P:3 * P], v[0], start=False, stop=True,
                          skip_group_check=True).then_inc(S["pv_done"], 1)

            for h in range(HEADS + 3):
                if h < HEADS:
                    logits(h)
                if 2 <= h < HEADS + 2:
                    turn_probs(h - 2)
                if h >= 3:
                    values(h - 3)
            pe_head_turn(pe, 0, qT)
            pe_out("A", pe, slab_ready, row_product, operand_stat)

        def act_attention(act, link, split_hi, gate, head_norm):
            b = BASE["A"]
            gate("A")
            split_hi(b + 2)
            act.wait_ge(S["lam_done"], 1)
            act.activation(lam_s[:, 2:4], lam_s[:, 0:2], ACT.Exp).then_inc(S["lam_exp"], 1)

            def square(m):
                act.wait_ge(slab_used, b + m + 1)
                act.activation(sq_sb[m % 2], ab_banks[m % 6], ACT.Square).then_inc(S["sq_done"], 1)

            def root(m):
                act.wait_ge(S["ss_done"], m + 1)
                if m >= 2:
                    act.wait_ge(S["qk_done"], m - 1)
                act.activation(rs_sb[m % 2], bank(misc, m % 2), ACT.Sqrt, scale=1.0 / NSA_HD,
                               bias=eps_col).then_inc(S["rs_done"], 1)

            for m in range(12):
                if m:
                    split_hi(b + m + 2)
                if 1 <= m <= 8:
                    square(m - 1)
                if 2 <= m <= 9:
                    root(m - 2)
            act.wait_ge(slab_used, b + 12)
            act.copy(v_sb, dacc[:, :]).then_inc(S["v_done"], 1)
            split_hi(b + 14)

            def exps(h):
                act.wait_ge(S["maxed"], h + 1)
                for j, (o, n) in enumerate(((0, SEQ), (3 * P, SEQ), (SEQ, P), (3 * P + SEQ, P))):
                    s = prob[h % 3][:, o:o + n]
                    last = act.activation(s, s, ACT.Exp, bias=nmax[:, 4 * (h % 3) + j:4 * (h % 3) + j + 1],
                                          accum_out=sums[:, 4 * (h % 3) + j:4 * (h % 3) + j + 1])
                    last.then_inc(S["expd"], 1)

            def probs_back(h):
                act.wait_ge(S["turned_p"], h + 1)
                act.copy(attn[h % 3], bank(dacc, h % 2)[:, 0:3 * P]).then_inc(S["p_done"], 1)

            def result(h):
                act.wait_ge(S["pv_done"], h + 1)
                act_head_squares(act, 0, 2 * h, bank(dacc, 2 + h % 2)[:, 0:SEQ])
                act.copy(qT[:, h * SEQ:(h + 1) * SEQ], bank(dacc, 2 + h % 2)[:, 0:SEQ]).then_inc(S["o_done"], 1)

            for h in range(HEADS + 3):
                if h < HEADS:
                    exps(h)
                if 2 <= h < HEADS + 2:
                    probs_back(h - 2)
                if h >= 3:
                    result(h - 3)
            head_norm(0, head_gain)
            for m in range(1, 4):
                split_hi(b + 12 + m + 2)

        def dve_attention(dve, link, split_lo, ada_tile, mod_vector, residual, head_norm):
            b = BASE["A"]

            dve.wait_ge(S["lam_in"], 64)
            for i in range(2):
                a = lam_in[:, P * i:P * i + 64]
                link(dve.tensor_tensor(a, a, lam_in[:, P * i + 64:P * i + P], ALU.mult))
                ins = dve.tensor_reduce(lam_s[:, i:i + 1], a, AX, ALU.add)
                if i == 0:
                    link(ins)
            ins.then_inc(S["lam_done"], 1)

            def scale_qk(m):
                dve.wait_ge(S["rs_done"], m + 1)
                link(dve.reciprocal(rs_sb[m % 2], rs_sb[m % 2]))
                dst = (qT, kT)[m // 4][:, (m % 4) * 512:(m % 4 + 1) * 512]
                dve.scalar_tensor_tensor(dst, ab_banks[m % 6], qk_gain[:, m // 4:m // 4 + 1], rs_sb[m % 2],
                                         ALU.mult, ALU.mult).then_inc(S["qk_done"], 1)

            for m in range(12):
                split_lo(b + m + 2)
                if 2 <= m <= 9:
                    scale_qk(m - 2)
                for k in {0: (0, 1), 1: (2, 3), 10: (4, 5), 11: (6, 7)}.get(m, ()):
                    ada_tile(7, k)
            dve.wait_ge(S["lam_exp"], 1)
            link(dve.tensor_tensor(neg_lam, lam_s[:, 3:4], lam_s[:, 2:3], ALU.subtract))
            link(dve.tensor_scalar(neg_lam, neg_lam, -LAMBDA_INIT, None, ALU.add))
            mod_vector(7)
            split_lo(b + 14)
            dve.wait_ge(S["rel_in"], 32)
            dve.wait_ge(S["qk_done"], 8)

            def bias_and_max(h):
                dve.wait_ge(S["qk_logits"], h + 1)
                for c in range(2):
                    dve.tensor_tensor(prob[h % 3][:, c * 3 * P:(c + 1) * 3 * P], bank((up, misc)[c], h % 2)[:, 0:3 * P],
                                      rel_bias[:, h, :], ALU.add).then_inc(S["biased"], 1)
                dve.wait_ge(S["biased"], 2 * h + 2)
                s = prob[h % 3].rearrange("p (c k) -> p c k", c=2)
                link(dve.tensor_reduce(nmax[:, 4 * (h % 3):4 * (h % 3) + 2], s[:, :, 0:SEQ], AX, ALU.max, negate=True))
                dve.tensor_reduce(nmax[:, 4 * (h % 3) + 2:4 * (h % 3) + 4], s[:, :, SEQ:3 * P], AX, ALU.max,
                                  negate=True).then_inc(S["maxed"], 1)

            def combine(h):
                dve.wait_ge(S["expd"], 4 * (h + 1))
                c = coef[:, 4 * (h % 3):4 * (h % 3) + 4]
                link(dve.reciprocal(c, sums[:, 4 * (h % 3):4 * (h % 3) + 4]))
                odd = c.rearrange("p (t c) -> p t c", c=2)[:, :, 1]
                link(dve.tensor_scalar(odd, odd, neg_lam, None, ALU.mult))
                if h >= 3:
                    dve.wait_ge(S["pv_done"], h - 2)
                pr, at = prob[h % 3], attn[h % 3]
                link(dve.tensor_scalar(at[:, 0:SEQ], pr[:, 0:SEQ], c[:, 0:1], None, ALU.mult))
                link(dve.tensor_scalar(at[:, SEQ:3 * P], pr[:, SEQ:3 * P], c[:, 2:3], None, ALU.mult))
                link(dve.scalar_tensor_tensor(at[:, 0:SEQ], pr[:, 3 * P:3 * P + SEQ], c[:, 1:2], at[:, 0:SEQ],
                                              ALU.mult, ALU.add))
                dve.scalar_tensor_tensor(at[:, SEQ:3 * P], pr[:, 3 * P + SEQ:6 * P], c[:, 3:4], at[:, SEQ:3 * P],
                                         ALU.mult, ALU.add).then_inc(S["attn_done"], 1)

            for h in range(HEADS + 1):
                if h < HEADS:
                    bias_and_max(h)
                if h:
                    combine(h - 1)
            dve.wait_ge(S["o_done"], HEADS)
            head_norm(0, qT, head_gain)
            for m in range(1, 4):
                split_lo(b + 12 + m + 2)
            residual("A")

        PE_MIX["A"], ACT_MIX["A"], DVE_MIX["A"] = pe_attention, act_attention, dve_attention

        def pe_gating(pe, slab_ready, col_product, row_product, operand_stat, ada_sum, gate_spread, token_product):
            b = BASE["G"]
            for m in range(4):
                slab_ready(b + m)
                pe.wait_ge(S["operand_ready"], 4 * OPND["G"] + m + 1)
                row_product(b + m, operand_stat(m), m == 0, m == 3)
            gate_spread("G")
            for m in range(4):
                slab_ready(b + 4 + m)
                if m == 2:
                    pe.wait_ge(S["gelu_done"], 1)
                col_product(b + 4 + m, sgu_banks[m])
            pe.wait_ge(S["gate_done"], phases.index("G") + 1)
            pe.wait_ge(S["ws_masked"], 1)
            for g in range(8):
                last = pe.transpose(misc[:, g * P:(g + 1) * P], ws_raw[:, g * P:(g + 1) * P], ident[:, :])
            last.then_inc(S["ws_turned"], 1)
            pe.wait_ge(S["gelu_done"], NT + 4)
            pe.wait_ge(S["bs_in"], 48)
            pe.wait_ge(S["ws_done"], 1)
            pe.wait_ge(S["ln_done"], 2)
            for c in range(4):
                for gg in range(2):
                    g = 2 * c + gg
                    for t in range(NT):
                        o = bank(dacc, c)[:, gg * SEQ + t * P:gg * SEQ + (t + 1) * P]
                        pe.matmul(o, vg_sb[:, t * D + g * P:t * D + (g + 1) * P], ws_t[:, g * P:(g + 1) * P],
                                  start=(gg == 0 and t == 0), stop=False, skip_group_check=True)
                        last = pe.matmul(o, ones[0:1, :], bs_row[0:1, g * P:(g + 1) * P], start=False, stop=True,
                                         skip_group_check=True)
                last.then_inc(S["mixed"], 1)
            pe.wait_ge(S["operand_ready"], 4 * OPND["Go"] + 4)
            pe_out("G", pe, slab_ready, row_product, operand_stat)

        def act_gating(act, link, split_hi, gate, head_norm):
            b = BASE["G"]
            for m in range(9):
                split_hi(b + m + 2)
                if m == 4:
                    act.wait_ge(slab_used, b + 4)
                    for t in range(NT):
                        act.activation(vg_sb[:, t * D:(t + 1) * D], dacc[:, t * D:(t + 1) * D],
                                       ACT.Gelu).then_inc(S["gelu_done"], 1)
                    gate("G")
                if m == 6:
                    act.wait_ge(S["ln_stats"], 1)
                    var = bn_out.rearrange("p (t s) -> p t s", s=2)[:, :, 1]
                    act.activation(var, var, ACT.Sqrt, bias=eps_col).then_inc(S["ln_sqrt"], 1)
                if m >= 5:
                    act.wait_ge(slab_used, b + m)
                    act.activation(qT[:, (m - 5) * 512:(m - 4) * 512], sgu_banks[m - 5],
                                   ACT.Gelu).then_inc(S["gelu_done"], 1)
            for c in range(4):
                act.wait_ge(S["gated"], c + 1)
                act.copy(operand_hi[:, c * 512:(c + 1) * 512], qT[:, c * 512:(c + 1) * 512]).then_inc(S["gated_hi"], 1)
            for m in range(1, 4):
                split_hi(b + 8 + m + 2)

        def dve_gating(dve, link, split_lo, ada_tile, mod_vector, residual, head_norm):
            b = BASE["G"]

            def statistics(t):
                dve.wait_ge(S["gelu_done"], 1 + t)
                for h in range(2):
                    link(dve.bn_stats(bn[:, 6 * h:6 * h + 6], vg_sb[:, t * D + 512 * h:t * D + 512 * (h + 1)]))
                ins = dve.bn_aggr(bn_out[:, 2 * t:2 * t + 2], bn[:, 0:12].rearrange("p (a b) -> p a b", b=6))
                if t == 0:
                    link(ins)
                else:
                    ins.then_inc(S["ln_stats"], 1)

            def normalise(t):
                v = vg_sb[:, t * D:(t + 1) * D]
                link(dve.tensor_scalar(v, v, bn_out[:, 2 * t:2 * t + 1], bn_out[:, 2 * t + 1:2 * t + 2],
                                       ALU.subtract, ALU.mult))
                link(dve.tensor_tensor(v, v, ln_g_row, ALU.mult))
                dve.tensor_tensor(v, v, ln_b_row, ALU.add).then_inc(S["ln_done"], 1)

            for m in range(7):
                split_lo(b + m + 2)
                if m in (4, 5):
                    statistics(m - 4)
            dve.wait_ge(S["ln_sqrt"], 1)
            var = bn_out.rearrange("p (t s) -> p t s", s=2)[:, :, 1]
            link(dve.reciprocal(var, var))
            dve.wait_ge(S["bs_in"], 48)
            for t in range(NT):
                normalise(t)
            dve.wait_ge(S["ws_turned"], 1)
            dve.tensor_copy(ws_t, misc[:, :]).then_inc(S["ws_done"], 1)
            for m in (7, 8):
                split_lo(b + m + 2)
            for c in range(4):
                o = slice(c * 512, (c + 1) * 512)
                dve.wait_ge(S["mixed"], c + 1)
                dve.tensor_tensor(qT[:, o], qT[:, o], bank(dacc, c), ALU.mult).then_inc(S["gated"], 1)
                dve.wait_ge(S["gated_hi"], c + 1)
                dve.tensor_tensor(operand_lo[:, o], qT[:, o], operand_hi[:, o].bitcast(F32),
                                  ALU.subtract).then_inc(S["operand_ready"], 1)
            for m in range(1, 4):
                split_lo(b + 8 + m + 2)
            residual("G")

        PE_MIX["G"], ACT_MIX["G"], DVE_MIX["G"] = pe_gating, act_gating, dve_gating

        LEVELS = [1, 2, 4, 8, 16, 32, 64, P]

        def hgrn_pool_masks(pool, link):
            pool.wait_ge(S["x_done"], x_before("H"))
            link(pool.memset(masks, 0.0))
            for w, m in enumerate(LEVELS[:-1]):
                v = masks[:, w * P:(w + 1) * P].rearrange("p (g h m) -> p g h m", h=2, m=m)[:, :, 1, :]
                n = P // (2 * m)
                link(pool.memset(v, 1.0))
                link(pool.affine_select(out=v, in_=v, compare_op=ALU.is_ge, fill=0.0, base=0,
                                        pattern=[[-2 * m, n], [0, m]], channel_multiplier=1))
                link(pool.affine_select(out=v, in_=v, compare_op=ALU.is_ge, fill=0.0, base=m - 1,
                                        pattern=[[2 * m, n], [0, m]], channel_multiplier=-1))
            link(pool.memset(restart, 1.0))
            pool.memset(restart.rearrange("p (t s) -> p t s", t=NT)[:, :, 0:1], 0.0).then_inc(S["mask_done"], 1)

        def level_halves(n):
            a, w = n // len(LEVELS), n % len(LEVELS)
            m = LEVELS[w]
            f = lambda t, h: t.rearrange("p (g h m) -> p g h m", h=2, m=m)[:, :, h, :]
            return a, w, m, f

        def hgrn_pool_levels(pool):
            for n in range(4 * len(LEVELS)):
                a, w, m, f = level_halves(n)
                o = slice(a * 512, (a + 1) * 512)
                for h, t in ((0, kT), (1, qT)):
                    pool.wait_ge(S["level_exp"], 2 * n + h + 1)
                    pool.tensor_tensor(f(wlev[n % 4], h), f(wlev[n % 4], h), f(t[:, o], h),
                                       ALU.mult).then_inc(S["level_w"], 1)

        def pe_hgrn(pe, slab_ready, col_product, row_product, operand_stat, ada_sum, gate_spread, token_product):
            b = BASE["H"]
            for m in range(8):
                slab_ready(b + m)
                if m >= 6:
                    pe.wait_ge(S["sg_done"], 2 * (m - 5))
                col_product(b + m, ab_banks[m % 6], "H" if m == 0 else None)
                if m == 0:
                    pe.wait_ge(S["operand_ready"], 4 * OPND["H"] + 4)
                    gate_spread("H")
            pe.wait_ge(S["sg_done"], 8)
            pe.wait_ge(S["hq_done"], 4)
            for m in range(4):
                slab_ready(b + 8 + m)
                row_product(b + 8 + m, operand_stat(m), m == 0, m == 3)
            pe.wait_ge(S["gate_done"], phases.index("H") + 1)
            ada_sum(23)

            def own(a):
                if a == 0:
                    pe.wait_ge(S["hv_done"], 1)
                for j in range(4):
                    o = a * 512 + j * P
                    last = pe.matmul(bank(dacc, a % 2)[:, j * P:(j + 1) * P], kT[:, o:o + P], qT[:, o:o + P],
                                     start=True, stop=True, skip_group_check=True)
                last.then_inc(S["own_done"], 1)

            def level(n):
                pe.wait_ge(S["level_w"], 2 * n + 2)
                if n >= 2:
                    pe.wait_ge(S["level_done"], n - 1)
                w = wlev[n % 4]
                cross = n % len(LEVELS) == len(LEVELS) - 1
                for j in range(2 if cross else 4):
                    l = w[:, j * SEQ:j * SEQ + P] if cross else w[:, j * P:(j + 1) * P]
                    r = w[:, j * SEQ + P:(j + 1) * SEQ] if cross else l
                    last = pe.matmul(bank(up, n % 2)[:, j * P:(j + 1) * P], l, r, start=True, stop=True,
                                     skip_group_check=True)
                last.then_inc(S["level_s"], 1)

            def values(a):
                pe.wait_ge(S["level_done"], len(LEVELS) * (a + 1))
                pe.wait_ge(S["own_kept"], a + 1)
                if a >= 2:
                    pe.wait_ge(S["ho_done"], a - 1)
                o = bank(dacc, 2 + a % 2)
                pt = pt_sb[a % 2]
                for j in range(2):
                    v = [hv_sb[:, t * D + (2 * a + j) * P:t * D + (2 * a + j + 1) * P] for t in range(NT)]
                    q = j * SEQ
                    pe.matmul(o[:, q:q + P], pt[:, j * 3 * P:j * 3 * P + P], v[0], start=(j == 0), stop=True,
                              skip_group_check=True)
                    pe.matmul(o[:, q + P:q + SEQ], pt[:, j * 3 * P + P:j * 3 * P + 2 * P], v[1], start=False,
                              stop=False, skip_group_check=True)
                    last = pe.matmul(o[:, q + P:q + SEQ], pt[:, j * 3 * P + 2 * P:j * 3 * P + 3 * P], v[0],
                                     start=False, stop=True, skip_group_check=True)
                last.then_inc(S["ho_psum"], 1)

            def output_gate(c):
                slab_ready(b + 12 + c)
                if c >= 2:
                    pe.wait_ge(S["g_taken"], c - 1)
                token_product(b + 12 + c, bank(misc, c % 2), 0, SEQ)

            pe.wait_ge(S["mod_done"], 24)
            for a in range(4):
                own(a)
                for w in range(len(LEVELS)):
                    level(a * len(LEVELS) + w)
                    if w == 1 and a:
                        values(a - 1)
                    if w == 3 and a:
                        output_gate(a - 1)
            output_gate(3)
            values(3)
            pe_head_turn(pe, 1, qT)
            pe_out("H", pe, slab_ready, row_product, operand_stat)

        def act_hgrn(act, link, split_hi, gate, head_norm):
            b = BASE["H"]
            gate("H")
            act.wait_ge(S["lb_d"], 1)
            act.activation(lb_tmp[:, 0:16], lb_tmp[:, 0:16], ACT.Exp).then_inc(S["lb_a"], 1)

            def take(m):
                act.wait_ge(slab_used, b + m + 1)
                if m >= 4:
                    act.copy(qT[:, (m - 4) * 512:(m - 3) * 512], ab_banks[m % 6]).then_inc(S["hq_done"], 1)
                    return
                if m >= 2:
                    act.wait_ge(S["hk_done"], m - 1)
                act.activation(wlev[m % 2], ab_banks[m % 6], ACT.Sigmoid).then_inc(S["sg_done"], 1)
                act.activation(pt_sb[m % 2][:, 0:512], ab_banks[m % 6], ACT.Sigmoid,
                               scale=-1.0).then_inc(S["sg_done"], 1)

            for m in range(12):
                split_hi(b + m + 2)
                if 1 <= m <= 8:
                    take(m - 1)
                if m == 6:
                    act.wait_ge(S["hk_done"], 4)
                    act.activation(b_sb, b_sb, ACT.Ln).then_inc(S["logf_done"], 1)
            act.wait_ge(slab_used, b + 12)
            act.copy(hv_sb, dacc[:, :]).then_inc(S["hv_done"], 1)
            split_hi(b + 14)

            def result(a):
                act.wait_ge(S["ho_psum"], a + 1)
                act_head_squares(act, 1, 4 * a, bank(dacc, 2 + a % 2))
                act.copy(qT[:, a * 512:(a + 1) * 512], bank(dacc, 2 + a % 2)).then_inc(S["ho_done"], 1)

            def take_gate(c):
                act.wait_ge(slab_used, b + 13 + c)
                act.wait_ge(S["level_w"], 2 * len(LEVELS) * (c + 1))
                act.activation(kT[:, c * 512:(c + 1) * 512].rearrange("p (j t e) -> p j t e", j=2, t=NT),
                               bank(misc, c % 2).rearrange("p (t j e) -> p j t e", t=NT, j=2),
                               ACT.Silu if c == 3 else ACT.Copy).then_inc(S["g_taken"], 1)
                if c < 3:
                    split_hi(b + 15 + c)

            for n in range(4 * len(LEVELS)):
                a, w, m, f = level_halves(n)
                act.wait_ge(S["level_diff"], n + 1)
                t = wlev[n % 4]
                act.activation(f(t, 0), f(t, 0), ACT.Exp, scale=-1.0).then_inc(S["level_exp"], 1)
                src = f(b_sb[:, a * 512:(a + 1) * 512], 1) if m == P else f(t, 1)
                act.activation(f(t, 1), src, ACT.Exp).then_inc(S["level_exp"], 1)
                if w == 4 and a:
                    result(a - 1)
                if w == 6 and a:
                    take_gate(a - 1)
            act.wait_ge(S["g_taken"], 3)
            act.activation(kT[:, 0:1536], kT[:, 0:1536], ACT.Silu).then_inc(S["silu_g"], 1)
            take_gate(3)
            result(3)
            head_norm(1, cols[:, 2 * P + 97:2 * P + 98])
            for m in range(4):
                split_hi(b + 16 + m + 2)

        def dve_hgrn(dve, link, split_lo, ada_tile, mod_vector, residual, head_norm):
            b = BASE["H"]
            l0, l1 = cols[:, 2 * P + 80:2 * P + 88], cols[:, 2 * P + 88:2 * P + 96]
            link(dve.tensor_tensor(lb_tmp[:, 16:24], l0, l1, ALU.max))
            link(dve.tensor_tensor(lb_tmp[:, 0:8], l0, lb_tmp[:, 16:24], ALU.subtract))
            dve.tensor_tensor(lb_tmp[:, 8:16], l1, lb_tmp[:, 16:24], ALU.subtract).then_inc(S["lb_d"], 1)
            dve.wait_ge(S["lb_a"], 1)
            link(dve.tensor_tensor(lb_tmp[:, 16:24], lb_tmp[:, 0:8], lb_tmp[:, 8:16], ALU.add))
            link(dve.reciprocal(lb_tmp[:, 16:24], lb_tmp[:, 16:24]))
            link(dve.tensor_tensor(lb_col, lb_tmp[:, 0:8], lb_tmp[:, 16:24], ALU.mult))
            link(dve.tensor_scalar(oml_col, lb_col, -1.0, 1.0, ALU.mult, ALU.add))

            def forget(c):
                dve.wait_ge(S["sg_done"], 2 * c + 2)
                for j in range(2):
                    h = 2 * c + j
                    o = slice(h * SEQ, (h + 1) * SEQ)
                    dve.tensor_scalar(b_sb[:, o], wlev[c % 2][:, j * SEQ:(j + 1) * SEQ], oml_col[:, h:h + 1],
                                      lb_col[:, h:h + 1], ALU.mult, ALU.add).then_inc(S["f_done"], 1)
                    ins = dve.tensor_scalar(kT[:, o], pt_sb[c % 2][:, j * SEQ:(j + 1) * SEQ], oml_col[:, h:h + 1],
                                            None, ALU.mult)
                    if j == 0:
                        link(ins)
                dve.wait_ge(S["f_done"], 2 * c + 2)
                ins.then_inc(S["hk_done"], 1)

            for m in range(12):
                split_lo(b + m + 2)
                if 1 <= m <= 4:
                    forget(m - 1)
                if m == 7:
                    dve.wait_ge(S["logf_done"], 1)
                    dve.wait_ge(S["mask_done"], 1)
                if 7 <= m <= 10:
                    for h in (2 * m - 14, 2 * m - 13):
                        o = slice(h * SEQ, (h + 1) * SEQ)
                        dve.tensor_tensor_scan(b_sb[:, o], restart, b_sb[:, o], 0.0, ALU.mult,
                                               ALU.add).then_inc(S["scanned"], 1)
                if m < KB:
                    ada_tile(23, m)
            dve.wait_ge(S["scanned"], HEADS)
            mod_vector(23)
            n_levels = 4 * len(LEVELS)

            def difference(n):
                a, w, m, f = level_halves(n)
                if n >= 4:
                    dve.wait_ge(S["level_s"], n - 3)
                src = b_sb[:, a * 512:(a + 1) * 512].rearrange("p (g m) -> p g m", m=2 * m)
                dst = wlev[n % 4].rearrange("p (g m) -> p g m", m=2 * m)
                k = m if m == P else 2 * m
                dve.tensor_tensor(dst[:, :, 0:k], src[:, :, 0:k],
                                  src[:, :, m - 1:m].to_broadcast([P, 512 // (2 * m), k]),
                                  ALU.subtract).then_inc(S["level_diff"], 1)

            def keep(n):
                a, w, m, f = level_halves(n)
                dve.wait_ge(S["level_s"], n + 1)
                pt = pt_sb[a % 2].rearrange("p (h j q) -> p h j q", h=2, j=3)
                sc = bank(up, n % 2)
                if m == P:
                    dve.tensor_copy(pt[:, :, 2, :], sc[:, 0:SEQ].rearrange("p (h q) -> p h q", h=2)).then_inc(S["level_done"], 1)
                    return
                for j in range(2):
                    ins = dve.copy_predicated(pt[:, j, 0:2, :],
                                              masks[:, w * P:(w + 1) * P].bitcast(U32).unsqueeze(1).to_broadcast([P, 2, P]),
                                              sc[:, j * SEQ:(j + 1) * SEQ].rearrange("p (t q) -> p t q", t=2))
                    if j == 0:
                        link(ins)
                    else:
                        ins.then_inc(S["level_done"], 1)

            def keep_own(a):
                if a >= 2:
                    dve.wait_ge(S["ho_psum"], a - 1)
                link(dve.memset(pt_sb[a % 2], 0.0))
                dve.wait_ge(S["own_done"], a + 1)
                pt = pt_sb[a % 2].rearrange("p (h j q) -> p h j q", h=2, j=3)
                for j in range(2):
                    ins = dve.copy_predicated(pt[:, j, 0:2, :], ident[:, :].bitcast(U32).unsqueeze(1).to_broadcast([P, 2, P]),
                                              bank(dacc, a % 2)[:, j * SEQ:(j + 1) * SEQ].rearrange("p (t q) -> p t q", t=2))
                    if j == 0:
                        link(ins)
                ins.then_inc(S["own_kept"], 1)
                dve.wait_ge(S["own_kept"], a + 1)

            for n in range(4):
                difference(n)
            split_lo(b + 14)
            for n in range(n_levels):
                if n % len(LEVELS) == 0:
                    keep_own(n // len(LEVELS))
                if n:
                    dve.wait_ge(S["level_done"], n)
                keep(n)
                if n + 4 < n_levels:
                    difference(n + 4)
                if n % len(LEVELS) == 6 and n > len(LEVELS):
                    split_lo(b + 14 + n // len(LEVELS))
            dve.wait_ge(S["ho_done"], 4)
            head_norm(1, qT, cols[:, 2 * P + 97:2 * P + 98], gate=kT)
            for m in range(4):
                split_lo(b + 16 + m + 2)
            residual("H")

        PE_MIX["H"], ACT_MIX["H"], DVE_MIX["H"] = pe_hgrn, act_hgrn, dve_hgrn

        def nsa_head(n):
            bb, f = n // 2, n % 2
            h = (bb // NSA_HPG) * 2 * NSA_HPG + f * NSA_HPG + bb % NSA_HPG
            return bb, f, bb // NSA_HPG, h, float(np.float32(2.0 ** (-8.0 * (h + 1) / NSA_HEADS)))

        c_max, c_sum = n_small[:, 0:32], n_small[:, 32:64]
        n_nmax, n_sums, n_coef = n_small[:, 64:76], n_small[:, 76:88], n_small[:, 88:100]
        late_row = n_small[:, 100:101]
        c_dist = n_small[:, 104:104 + NT * NC]
        c_prob4 = c_prob.rearrange("p (f t b n) -> p f t b n", f=2, t=NT, n=NC)

        def nsa_pool_tables(pool, link):
            pool.wait_ge(S["x_done"], x_before("N"))
            for o, n, base in ((0, SEQ, P), (SEQ, P, 0)):
                d = dist[:, o:o + n]
                link(pool.iota(d, pattern=[[-1, n]], base=base, channel_multiplier=1,
                               allow_small_or_imprecise_dtypes=True))
                link(pool.affine_select(out=d, in_=d, compare_op=ALU.is_ge, fill=FAR, base=base,
                                        pattern=[[-1, n]], channel_multiplier=1))
            cd = c_dist.rearrange("p (t n) -> p t n", t=NT)
            link(pool.iota(cd, pattern=[[P, NT], [-CMP_STRIDE, NC]], base=0, channel_multiplier=1,
                           allow_small_or_imprecise_dtypes=True))
            link(pool.tensor_scalar(cd, cd, -(CMP_LEN - 1) / 2.0, None, ALU.add))
            link(pool.affine_select(out=cd, in_=cd, compare_op=ALU.is_ge, fill=FAR, base=-(CMP_LEN - 1),
                                    pattern=[[P, NT], [-CMP_STRIDE, NC]], channel_multiplier=1))
            cb = cbias.rearrange("p (f t b n) -> p f t b n", f=2, t=NT, n=NC)
            for n in range(NSA_HEADS):
                bb, f, _, _, slope = nsa_head(n)
                link(pool.tensor_scalar(cb[:, f, :, bb, :], cd, -slope, None, ALU.mult))
            link(pool.memset(late_row, 1.0))
            pool.affine_select(out=late_row, in_=late_row, compare_op=ALU.is_ge, fill=0.0, base=-(CMP_LEN - 1),
                               pattern=[[0, 1]], channel_multiplier=1).then_inc(S["dist_done"], 1)

        def pe_nsa(pe, slab_ready, col_product, row_product, operand_stat, ada_sum, gate_spread, token_product):
            b = BASE["N"]

            for m in range(11):
                slab_ready(b + m)
                if m == 1:
                    pe.wait_ge(S["operand_ready"], 4 * OPND["N"] + 4)
                    gate_spread("N")
                if m == 3:
                    pe.wait_ge(S["gate_done"], phases.index("N") + 1)
                if m < 8:
                    col_product(b + m, nsa_banks[m - 1 if 1 <= m <= 4 else max(m, 4)], "N" if m == 0 else None)
                else:
                    pe.wait_ge(S["nq_done"], m - 7)
                    token_product(b + m, nsa_banks[m - 8], *((0, SEQ) if m < 10 else (SEQ - 3 * NSA_HEADS, 3 * NSA_HEADS)))
            pe.wait_ge(S["nq_done"], 4)
            ada_sum(29)

            pe.wait_ge(S["w1_in"], 96)
            pe.wait_ge(S["nv_done"], 2)
            for a in range(2):
                for q in range(2):
                    pe.wait_ge(S["windows_done"], 2 * a + q + 1)
                    for l in range(CMP_STRIDE):
                        w = (q * CMP_STRIDE + l) * 64
                        last = pe.matmul(bank(up, a)[0:64, 0:NSA_KV * NC], w1_sb[a][:, w:w + 64],
                                         windows[q][:, l * NSA_KV * NC:(l + 1) * NSA_KV * NC],
                                         start=(q == 0 and l == 0), stop=(q == 1 and l == CMP_STRIDE - 1),
                                         skip_group_check=True)
                    last.then_inc(S["hid_pe"], 1)
            pe.wait_ge(S["hid_act"], 1)
            pe.wait_ge(S["nk_done"], 4)
            pe.matmul(bank(dacc, 2)[0:64, 0:NSA_KV * NC], w2_sb[0][0:64, :], hid[0][0:64, :], start=True,
                      stop=True).then_inc(S["kc_pe"], 1)
            pe.wait_ge(S["hid_act"], 2)
            for g in range(NSA_KV):
                last = pe.matmul(bank(dacc, 3)[0:NC, g * 64:(g + 1) * 64], hid[1][0:64, g * NC:(g + 1) * NC],
                                 w2_sb[1][0:64, :], start=True, stop=True, skip_group_check=True)
            last.then_inc(S["kc_pe"], 1)

            def compressed_scores():
                pe.wait_ge(S["kc_done"], 1)
                for t in range(NT):
                    for bb in range(KB):
                        o = (t * KB + bb) * 2 * NC
                        p = bb // NSA_HPG
                        last = pe.matmul(bank(dacc, 0)[:, o:o + 2 * NC], qT[:, bb * SEQ + t * P:bb * SEQ + (t + 1) * P],
                                         kc2[:, p * 2 * NC:(p + 1) * 2 * NC], start=True, stop=True,
                                         skip_group_check=True)
                last.then_inc(S["cs_done"], 1)

            def scores(n):
                bb, f, p, _, _ = nsa_head(n)
                r = slice(64 * f, 64 * f + 64)
                if n >= 2:
                    pe.wait_ge(S["nb_done"], n - 1)
                q = qT[r, bb * SEQ:(bb + 1) * SEQ]
                k = work[r, 2048:3072].rearrange("p (r b s) -> p r b s", r=2, b=2)[:, :, p, :]
                pe.matmul(bank(up, n % 2), q[:, P:SEQ], k, start=True, stop=True, skip_group_check=True)
                pe.matmul(bank(misc, n % 2)[:, 0:SEQ], q[:, 0:P], k[:, :, 0:P], start=True, stop=True,
                          skip_group_check=True).then_inc(S["nqk_pe"], 1)

            def turn_probs(n):
                bb, f, _, _, _ = nsa_head(n)
                pe.wait_ge(S["nscaled"], n + 1)
                if n == 0:
                    pe.wait_ge(S["cp_done"], 1)
                if n:
                    pe.wait_ge(S["npt_done"], n)
                pr = n_prob[n % 3]
                for br in range(2):
                    for j, c in enumerate((512 + br * P, br * SEQ, br * SEQ + P)):
                        w = (br * 3 + j) * P
                        pe.transpose(dacc[:, w:w + P], pr[:, c:c + P], ident[:, :])
                for t in range(NT):
                    w = (6 + t) * P
                    last = pe.transpose(dacc[0:NC, w:w + P], c_prob4[:, f, t, bb, :], ident[:, :])
                last.then_inc(S["npt_pe"], 1)

            def values(n):
                _, _, p, _, _ = nsa_head(n)
                pe.wait_ge(S["npt_done"], n + 1)
                if n >= 2:
                    pe.wait_ge(S["no_done"], n - 1)
                o = bank(dacc, 2 + n % 2)[:, 0:SEQ]
                pe.matmul(o, vc_sb[0:NC, p * P:(p + 1) * P], c_pt[n % 2][0:NC, :], start=True, stop=False,
                          skip_group_check=True)
                for br, v in enumerate((vs_sb, vw_sb)):
                    pt = n_pt[n % 2][:, br * 3 * P:(br + 1) * 3 * P]
                    pe.matmul(o, v[:, p * P:(p + 1) * P], pt[:, 0:SEQ], start=False, stop=False, skip_group_check=True)
                    last = pe.matmul(o[:, P:SEQ], v[:, SEQ + p * P:SEQ + (p + 1) * P], pt[:, SEQ:3 * P], start=False,
                                     stop=(br == 1), skip_group_check=True)
                last.then_inc(S["npv_pe"], 1)

            compressed_scores()
            pe.wait_ge(S["kc_done"], 2)
            pe.wait_ge(S["ngate_done"], 1)
            pe.wait_ge(S["mod_done"], 30)
            for n in range(NSA_HEADS + 3):
                if n < NSA_HEADS:
                    scores(n)
                if 2 <= n < NSA_HEADS + 2:
                    turn_probs(n - 2)
                if n >= 3:
                    values(n - 3)
            pe.wait_ge(S["no_done"], NSA_HEADS)
            pe_out("N", pe, slab_ready, row_product, operand_stat)

        def act_nsa(act, link, split_hi, gate, head_norm):
            b = BASE["N"]
            gate("N")
            for m in range(12):
                split_hi(b + m + 2)
                if 2 <= m <= 5:
                    act.activation(qT[:, (m - 2) * 512:(m - 1) * 512], nsa_banks[m - 2], ACT.Copy,
                                   scale=float(NSA_HD) ** -0.5).then_inc(S["nq_done"], 1)
                elif m == 1 or 6 <= m <= 8:
                    act.copy((kc_t, vc_t, ks_t, kw_t)[max(m - 5, 0)], nsa_banks[max(m - 1, 4)]).then_inc(S["nk_done"], 1)
                elif 9 <= m <= 10:
                    act.copy((vs_sb, vw_sb)[m - 9], nsa_banks[m - 9]).then_inc(S["nv_done"], 1)
            act.activation(gates, bank(misc, 0)[:, 0:NT * 3 * NSA_HEADS], ACT.Sigmoid).then_inc(S["ngate_done"], 1)
            for a in range(2):
                act.wait_ge(S["hid_pe"], 2 * a + 2)
                act.activation(hid[a][0:64, :].rearrange("p (b f n) -> p f b n", f=2, n=NC),
                               bank(up, a)[0:64, 0:NSA_KV * NC].rearrange("p (f b n) -> p f b n", f=2, n=NC),
                               ACT.Silu).then_inc(S["hid_act"], 1)
            act.wait_ge(S["kc_pe"], 1)
            for f in range(2):
                last = act.copy(kc2[64 * f:64 * f + 64, :].rearrange("p (b f n) -> p f b n", f=2, n=NC)[:, f],
                                bank(dacc, 2)[0:64, 0:NSA_KV * NC].rearrange("p (b f n) -> p f b n", f=2, n=NC)[:, f])
            last.then_inc(S["kc_done"], 1)
            act.wait_ge(S["kc_pe"], 2)
            act.copy(vc_sb[0:NC, :], bank(dacc, 3)[0:NC, 0:SEQ]).then_inc(S["kc_done"], 1)

            def exps(n):
                act.wait_ge(S["nmax_done"], n + 1)
                for j, (o, w) in enumerate(((512, P), (512 + P, P), (0, SEQ), (SEQ, SEQ))):
                    s = n_prob[n % 3][:, o:o + w]
                    i = 4 * (n % 3) + j
                    act.activation(s, s, ACT.Exp, bias=n_nmax[:, i:i + 1],
                                   accum_out=n_sums[:, i:i + 1]).then_inc(S["nexp_done"], 1)

            def probs_back(n):
                act.wait_ge(S["npt_pe"], n + 1)
                if n >= 2:
                    act.wait_ge(S["npv_pe"], n - 1)
                act.copy(n_pt[n % 2], dacc[:, 0:768])
                act.copy(c_pt[n % 2][0:NC, :], dacc[0:NC, 768:1024]).then_inc(S["npt_done"], 1)

            def result(n):
                bb, f, _, _, _ = nsa_head(n)
                r = slice(64 * f, 64 * f + 64)
                act.wait_ge(S["npv_pe"], n + 1)
                act.copy(qT[r, bb * SEQ:(bb + 1) * SEQ],
                         bank(dacc, 2 + n % 2)[r, 0:SEQ]).then_inc(S["no_done"], 1)
                if n % 4 == 3:
                    o = slice(n // 4 * 512, (n // 4 + 1) * 512)
                    act.wait_ge(S["no_done"], n + 1)
                    act.copy(operand_hi[:, o], qT[:, o]).then_inc(S["no_hi"], 1)

            act.wait_ge(S["cl_done"], 1)
            act.activation(c_prob, c_prob, ACT.Exp).then_inc(S["cexp_done"], 1)
            for n in range(NSA_HEADS + 3):
                if n < NSA_HEADS:
                    exps(n)
                if 2 <= n < NSA_HEADS + 2:
                    probs_back(n - 2)
                if n >= 3:
                    result(n - 3)
            for m in range(1, 4):
                split_hi(b + 11 + m + 2)

        def dve_nsa(dve, link, split_lo, ada_tile, mod_vector, residual, head_norm):
            b = BASE["N"]

            def make_windows(a, q):
                src = (kc_t, vc_t)[a].rearrange("p (b c s) -> p b c s", b=2, s=CMP_STRIDE)
                w = windows[q].rearrange("p (l f b n) -> p l f b n", f=2, b=2, n=NC)
                o = 3 * P + a * CMP_LEN + q * CMP_STRIDE
                dve.wait_ge(S["nk_done"], a + 1)
                if a:
                    dve.wait_ge(S["hid_pe"], q + 1)
                for f in range(2):
                    r = slice(64 * f, 64 * f + 64)
                    for blk in range(2):
                        ins = dve.tensor_tensor(w[r, :, f, blk, :], src[r, blk, q:q + NC, :].rearrange("p n s -> p s n"),
                                                cols[r, o:o + CMP_STRIDE].unsqueeze(2).to_broadcast([64, CMP_STRIDE, NC]),
                                                ALU.add)
                ins.then_inc(S["windows_done"], 1)

            for m in range(11):
                split_lo(b + m + 2)
                if m < KB:
                    ada_tile(29, m)
                if m == KB:
                    link(dve.memset(windows[0], 0.0))
                    link(dve.memset(kc2, 0.0))
                    make_windows(0, 0)
            mod_vector(29)
            link(dve.memset(windows[1], 0.0))
            make_windows(0, 1)
            make_windows(1, 0)
            make_windows(1, 1)
            split_lo(b + 13)

            dve.wait_ge(S["dist_done"], 1)
            dve.wait_ge(S["cs_done"], 1)
            rows = c_prob.rearrange("p (r n) -> p r n", n=NC)
            link(dve.tensor_tensor(c_prob.rearrange("p (f r n) -> p f r n", f=2, n=NC),
                                   dacc[:, 0:2 * NT * KB * NC].rearrange("p (r f n) -> p f r n", f=2, n=NC),
                                   cbias.rearrange("p (f r n) -> p f r n", f=2, n=NC), ALU.add))
            link(dve.tensor_reduce(c_max, rows, AX, ALU.max))
            dve.tensor_tensor(rows, rows, c_max.unsqueeze(2).to_broadcast([P, 32, NC]),
                              ALU.subtract).then_inc(S["cl_done"], 1)

            def compressed_probs():
                dve.wait_ge(S["cexp_done"], 1)
                link(dve.tensor_reduce(c_sum, rows, AX, ALU.add))
                link(dve.reciprocal(c_sum, c_sum))
                for f in range(2):
                    for t in range(NT):
                        c = c_sum[:, (f * NT + t) * KB:(f * NT + t + 1) * KB].rearrange("p (g h) -> p g h", g=2)
                        g0 = gates.rearrange("p (t g f h r) -> p t g f h r", t=NT, g=2, f=2, r=3)[:, t, :, f, :, 0]
                        link(dve.tensor_tensor(c, c, g0, ALU.mult))
                early = c_sum.rearrange("p (f t b) -> p f t b", f=2, t=NT)[:, :, 0, :]
                link(dve.tensor_scalar(early, early, late_row, None, ALU.mult))
                dve.tensor_tensor(rows, rows, c_sum.unsqueeze(2).to_broadcast([P, 32, NC]),
                                  ALU.mult).then_inc(S["cp_done"], 1)

            def bias_and_max(n):
                _, _, _, _, slope = nsa_head(n)
                dve.wait_ge(S["nqk_pe"], n + 1)
                if n >= 3:
                    dve.wait_ge(S["npt_pe"], n - 2)
                pr = n_prob[n % 3]
                m = n_nmax[:, 4 * (n % 3):4 * (n % 3) + 4]
                late = pr[:, 0:512].rearrange("p (r k) -> p r k", r=2)
                early = pr[:, 512:768].rearrange("p (r k) -> p r k", r=2)
                link(dve.scalar_tensor_tensor(late, dist[:, 0:SEQ].unsqueeze(1).to_broadcast([P, 2, SEQ]), -slope,
                                              bank(up, n % 2).rearrange("p (r k) -> p r k", r=2), ALU.mult, ALU.add))
                dve.scalar_tensor_tensor(early, dist[:, SEQ:3 * P].unsqueeze(1).to_broadcast([P, 2, P]), -slope,
                                         bank(misc, n % 2)[:, 0:SEQ].rearrange("p (r k) -> p r k", r=2), ALU.mult,
                                         ALU.add).then_inc(S["nb_done"], 1)
                dve.wait_ge(S["nb_done"], n + 1)
                link(dve.tensor_reduce(m[:, 0:2], early, AX, ALU.max, negate=True))
                dve.tensor_reduce(m[:, 2:4], late, AX, ALU.max, negate=True).then_inc(S["nmax_done"], 1)

            def scale(n):
                _, _, _, h, _ = nsa_head(n)
                dve.wait_ge(S["nexp_done"], 4 * n + 4)
                i = 4 * (n % 3)
                c = n_coef[:, i:i + 4]
                link(dve.reciprocal(c, n_sums[:, i:i + 4]))
                link(dve.tensor_tensor(c.rearrange("p (t r) -> p t r", t=NT), c.rearrange("p (t r) -> p t r", t=NT),
                                       gates.rearrange("p (t c) -> p t c", t=NT)[:, :, 3 * h + 1:3 * h + 3], ALU.mult))
                pr = n_prob[n % 3]
                late = pr[:, 0:512].rearrange("p (r k) -> p r k", r=2)
                early = pr[:, 512:768].rearrange("p (r k) -> p r k", r=2)
                link(dve.tensor_tensor(late, late, c[:, 2:4].unsqueeze(2).to_broadcast([P, 2, SEQ]), ALU.mult))
                dve.tensor_tensor(early, early, c[:, 0:2].unsqueeze(2).to_broadcast([P, 2, P]),
                                  ALU.mult).then_inc(S["nscaled"], 1)

            def operand_rest(c):
                o = slice(c * 512, (c + 1) * 512)
                dve.wait_ge(S["no_hi"], c + 1)
                dve.tensor_tensor(operand_lo[:, o], qT[:, o], operand_hi[:, o].bitcast(F32),
                                  ALU.subtract).then_inc(S["operand_ready"], 1)

            for n in range(NSA_HEADS + 1):
                if n < NSA_HEADS:
                    bias_and_max(n)
                if n == 0:
                    compressed_probs()
                if n:
                    scale(n - 1)
                if n >= 8 and n % 4 == 0:
                    operand_rest(n // 4 - 2)
            operand_rest(3)
            for m in range(1, 4):
                split_lo(b + 11 + m + 2)
            residual("N")

        PE_MIX["N"], ACT_MIX["N"], DVE_MIX["N"] = pe_nsa, act_nsa, dve_nsa
        def ada_source(v, k):
            if v < V2:
                return T["ada_w"][v // N_MOD][k * P:(k + 1) * P, (v % N_MOD) * D:(v % N_MOD + 1) * D]
            u = v - V2
            return T["ada_w_2"][u // N_MOD_2][k * P:(k + 1) * P, (u % N_MOD_2) * D:(u % N_MOD_2 + 1) * D]

        def ada_load(eng, v, k, it=0, source=None):
            m = v * KB + k
            if m >= ATILES:
                eng.wait_ge(S["ada_step"], m - ATILES + 1 + KB * it)
            eng.dma_start(ada[:, (m % ATILES) * D:(m % ATILES + 1) * D],
                          ada_source(v, k) if source is None else source).then_inc(
                              (ada_first if v < 2 else ada_full)[m % ATILES], 16)

        @block.sync
        def _(sp):
            early_slabs = []
            def load(s, it, sources):
                if s >= RAW:
                    sp.wait_ge(lo_done, s - RAW + 1 + RAW * it)
                for place, src in sources:
                    sp.dma_start(place(slab(raw, s, RAW)), src).then_inc(raw_full[s % RAW], 16)

            def up_src(p, i, j):
                w = ffn_sources(p)[j].rearrange("(k p) n -> p k n", p=P)
                return [(lambda t, a=a: t.rearrange("p (k n) -> p k n", k=KB)[:, 4 * a:4 * a + 4, :],
                         w[:, 4 * a:4 * a + 4, bass.ds(i * 256, 256)]) for a in range(2)]

            def down_src(p, i):
                wd = ffn_sources(p)[2].rearrange("(k p) n -> p k n", p=P)
                return [(lambda t, a=a: t[:, a * D:(a + 1) * D].unsqueeze(1), wd[:, bass.ds(i * 2 + a, 1), :])
                        for a in range(2)]

            def ffn(p):
                b = BASE[p]
                for j in range(2):
                    if b + j not in early_slabs:
                        load(b + j, 0, up_src(p, 0, j))
                for i in (1, 2):
                    for j in range(2):
                        load(b + 3 * i - 1 + j, 0, up_src(p, i, j))
                    load(b + 3 * i + 1, 0, down_src(p, i - 1))
                if p in OUT_ROW:
                    sp.wait_ge(S["x_done"], x_before(p))
                    sp.dma_start(out_row, OUT_ROW[p].to_broadcast([P, D])).then_inc(S["row_in"], 16)
                with sp.Fori(0, (FI - 3) // 2) as it:
                    for i in (3, 4):
                        for j in range(2):
                            load(b + 3 * i - 1 + j, it, up_src(p, it * 2 + i, j))
                        load(b + 3 * i + 1, it, down_src(p, it * 2 + i - 1))
                load(b + FFN_SLABS - 1, 0, down_src(p, FI - 1))

            for r0, name in ((0, "c"), (KB, "c_2")):
                sp.dma_start(c_rows[r0:r0 + KB, :], T[name].rearrange("b (k p) -> (b k) p", p=P)).then_inc(S["c_in"], 16)
            first_tiles = [(v, k) for v in range(2) for k in range(KB)]

            def first_ada():
                v, k = first_tiles.pop(0)
                ada_load(sp, v, k)

            for _ in range(ATILES):
                first_ada()
            sp.dma_start(x[:, :].rearrange("p (t d) -> p t d", t=NT),
                         T["x"][0].rearrange("(t p) d -> p t d", p=P)).then_inc(S["x_loaded"], 16)
            for i, (tile, r0, src, o) in enumerate(rows_plan):
                sp.dma_start(rows_sb[r0:r0 + src.shape[0], tile * P + o:tile * P + o + src.shape[1]],
                             src).then_inc(S["rows_loaded"], 16)
                if i % 4 == 3 and len(first_tiles) > KB + 2:
                    first_ada()
            while first_tiles:
                for _ in range(min(5, len(first_tiles))):
                    first_ada()
                if len(first_tiles) < KB:
                    early_slabs.append(len(early_slabs))
                    load(early_slabs[-1], 0, up_src(phases[0], 0, early_slabs[-1]))
            for i, name in enumerate(("attn_lq1", "attn_lk1", "attn_lq2", "attn_lk2")):
                sp.dma_start(lam_in[:, 64 * i:64 * i + 64], T[name].to_broadcast([P, 64])).then_inc(S["lam_in"], 16)
            sp.dma_start(rel_tab[0:HEADS, :], T["rel_bias"].rearrange("b h -> h b"),
                         allow_slow_non_contiguous=True).then_inc(S["rel_rows"], 16)

            def mixer_parameters(p):
                sp.wait_ge(S["operand_ready"], 4 * OPND[p] + 4)
                sp.wait_ge(S["gate_psum"], 2 * phases.index(p) + 2)
                if p == "A":
                    sp.wait_ge(S["rel_out"], 16)
                    for o, n, dst in ((P - 1, SEQ, rel_bias[:, :, 0:SEQ]), (2 * P - 1, P, rel_bias[:, :, SEQ:3 * P])):
                        sp.dma_start(dst, bass.AP(tensor=rel_dram.tensor, offset=rel_dram.offset + o,
                                                  ap=[[REL_W - 1, P], [P * REL_W, HEADS], [1, n]])).then_inc(S["rel_in"], 16)
                if p == "G":
                    sp.dma_start(ws_raw.rearrange("p (g s) -> p g s", g=8),
                                 T["sgu_w_s"][0].rearrange("g t s -> t g s")).then_inc(S["ws_in"], 16)
                    sp.dma_start(bs_row[0:1, :], T["sgu_b_s"][0:1].rearrange("a g t -> a (g t)")).then_inc(S["bs_in"], 16)
                    for dst, src in ((ln_g_row, T["sgu_ln_g"]), (ln_b_row, T["sgu_ln_b"])):
                        sp.dma_start(dst, src.to_broadcast([P, D])).then_inc(S["bs_in"], 16)
                if p == "N":
                    for a in range(2):
                        for g in range(2):
                            sp.dma_start(w1_sb[a][64 * g:64 * g + 64, :].rearrange("p (l f) -> p l f", f=64),
                                         T["nsa_cmp_w1_2"][0][a].rearrange("(l d) f -> d l f", d=64)).then_inc(S["w1_in"], 16)
                        sp.dma_start(w2_sb[a][0:64, :], T["nsa_cmp_w2_2"][0][a]).then_inc(S["w1_in"], 16)

            for p in phases:
                if p in FFNS:
                    ffn(p)
                    continue
                for m, src in enumerate(mixer_slabs(p)):
                    load(BASE[p] + m, 0, src)
                    if m == RAW - 1:
                        mixer_parameters(p)
            if phases[-1] in FFNS:
                load(nslabs, 0, down_src(phases[-1], FI - 1))
                sp.wait_ge(hi_done, nslabs + 1)
            sp.wait_ge(S["x_done"], x_count(phases[-1]) + (2 if phases[-1] in OUT_ROW else 0))
            sp.dma_start(out[0].rearrange("(t p) d -> p t d", p=P),
                         x[:, :].rearrange("p (t d) -> p t d", t=NT)).then_inc(S["stored"], 16)
            sp.wait_ge(S["stored"], 16)

        @block.gpsimd
        def _(pool):
            link = chain(pool, S["pool_chain"])
            const = S["const_done"]

            link(pool.memset(ones[:, :], 1.0))
            link(pool.memset(ident[:, :], 0.0))
            link(pool.affine_select(out=ident[:, :], in_=ident[:, :], compare_op=ALU.not_equal, fill=1.0, base=0,
                                    pattern=[[-1, P]], channel_multiplier=1))
            link(pool.memset(pair_ones[:, :], 0.0))
            link(pool.memset(pair_ones[0:64, 0:64], 1.0))
            link(pool.memset(pair_ones[64:P, 64:P], 1.0))
            pool.memset(eps_col, EPS).then_inc(const, 1)
            pool.wait_ge(const, 1)

            def gate_diag(p):
                g = phases.index(p)
                v = MODS[p][2]
                pool.wait_ge(S["mod_done"], v + 1)
                if g:
                    pool.wait_ge(S["gate_psum"], 2 * g)
                    pool.wait_ge(S["x_done"], x_before(p))
                for h in range(2):
                    pool.tensor_tensor(diag[h].rearrange("p (b f) -> p b f", b=4),
                                       ident[:, :].unsqueeze(1).to_broadcast([P, 4, P]),
                                       modcol[:, v * KB + 4 * h:v * KB + 4 * h + 4].unsqueeze(2).to_broadcast([P, 4, P]),
                                       ALU.mult).then_inc(S["diag_done"], 1)

            link(pool.memset(rel_rows[0:HEADS, :], -1e30))
            pool.wait_ge(S["rel_rows"], 16)
            starts = bucket_starts()
            for b in range(REL_BUCKETS):
                n = starts[b + 1] - starts[b]
                e = SEQ - starts[b]
                ins = pool.tensor_copy(rel_rows[0:HEADS, e - n:e],
                                       rel_tab[0:HEADS, b:b + 1].to_broadcast([HEADS, n]))
                link(ins)
            pool.dma_start(rel_dram, rel_rows[0:HEADS, :].unsqueeze(1).to_broadcast([HEADS, P, REL_W])).then_inc(S["rel_out"], 16)
            pool.wait_ge(S["rel_out"], 16)

            for p in phases:
                if p in FFNS:
                    if p in FIRST_VEC:
                        v = FIRST_VEC[p]
                        for k in range(KB):
                            ada_load(pool, v, k)
                        w = T["ada_w"] if v + 1 < V2 else T["ada_w_2"]
                        u, n = (v + 1, N_MOD) if v + 1 < V2 else (v + 1 - V2, N_MOD_2)
                        with pool.Fori(0, (FI - 3) // 2) as it:
                            for k in range(KB):
                                ada_load(pool, v + 1, k, it, w[u // n][k * P:(k + 1) * P, bass.ds(it * D + (u % n) * D, D)])
                    gate_diag(p)
                    continue
                gate_diag(p)
                if p in FIRST_VEC:
                    for k in range(KB):
                        ada_load(pool, FIRST_VEC[p], k)
                if p == "H":
                    hgrn_pool_masks(pool, link)
                if p == "N":
                    nsa_pool_tables(pool, link)
                if p == "G":
                    pool.wait_ge(S["ws_in"], 16)
                    v = ws_raw.rearrange("p (g s) -> p g s", g=8)
                    pool.affine_select(out=v, in_=v, compare_op=ALU.is_ge, fill=0.0, base=0,
                                       pattern=[[0, 8], [-1, P]], channel_multiplier=1).then_inc(S["ws_masked"], 1)
                if p == "H":
                    hgrn_pool_levels(pool)

        @block.tensor
        def _(pe):
            def slab_ready(s, it=0):
                pe.wait_ge(lo_done, s + 1 + RAW * it)

            def three(o, stat, mov, start, stop):
                pe.matmul(o, stat[0], mov[0], start=start, stop=False, skip_group_check=True)
                pe.matmul(o, stat[0], mov[1], start=False, stop=False, skip_group_check=True)
                return pe.matmul(o, stat[1], mov[0], start=False, stop=stop, skip_group_check=True)

            def col_product(s, dst, first_of=None):
                sl = (slab(hi, s, SPL), slab(lo, s, SPL))
                for k in range(KB):
                    if first_of is not None and k % 2 == 0:
                        pe.wait_ge(S["operand_ready"], 4 * OPND[first_of] + k // 2 + 1)
                    for b in range(2):
                        last = three(dst[:, b * SEQ:(b + 1) * SEQ], [t[:, k * SEQ + b * P:k * SEQ + (b + 1) * P] for t in sl],
                                     [op_k(t, k) for t in (operand_hi, operand_lo)], k == 0 and b == 0, k == KB - 1)
                last.then_inc(slab_used, 1)

            def token_product(s, dst, c0, w):
                for t in range(NT):
                    for k in range(KB):
                        last = three(dst[:, t * w:(t + 1) * w],
                                     [op_k(o, k)[:, t * P:(t + 1) * P] for o in (operand_hi, operand_lo)],
                                     [slab(o, s, SPL)[:, k * SEQ + c0:k * SEQ + c0 + w] for o in (hi, lo)],
                                     k == 0, k == KB - 1)
                last.then_inc(slab_used, 1)

            def row_product(s, stat, start, stop, last_of_phase=False):
                sl = (slab(hi, s, SPL), slab(lo, s, SPL))
                order = [(kk, t) for kk in range(2) for t in range(NT)]
                if last_of_phase:
                    order = [(kk, t) for t in range(NT) for kk in range(2)]
                for kk, t in order:
                    for part, parts in ((0, (0, 1)), (1, (0,))):
                        for q in parts:
                            for h in range(2):
                                last = pe.matmul(bank(dacc, 2 * t + h), stat(part, kk, t),
                                                 sl[q][:, kk * D + h * 512:kk * D + (h + 1) * 512],
                                                 start=(start and kk == 0 and part == 0 and q == 0),
                                                 stop=(stop and kk == 1 and part == 1), skip_group_check=True)
                    if last_of_phase and (kk, t) == (1, 0):
                        last.then_inc(S["tile_done"], 1)
                last.then_inc(slab_used, 1)

            def operand_stat(m):
                return lambda part, kk, t: op_k((operand_hi, operand_lo)[part], 2 * m + kk)[:, t * P:(t + 1) * P]

            def act_stat(i):
                def f(part, kk, t):
                    o = ((i % 2) * 2 + kk) * SEQ + t * P
                    return (act_hi, act_lo)[part][:, o:o + P]
                return f

            def ada_sum(v, it=0):
                pe.wait_ge(S["ada_step"], KB * (v + 1) + KB * it)
                if v >= 1:
                    pe.wait_ge(S["mod_done"], v + it)
                for k in range(KB):
                    last = pe.matmul(bank(misc, 1)[:, k:k + 1], ada_acc[:, k * P:(k + 1) * P], ones[:, 0:1],
                                     start=True, stop=True, skip_group_check=True)
                last.then_inc(S["ada_summed"], 1)

            def gate_spread(p):
                g = phases.index(p)
                for h in range(2):
                    pe.wait_ge(S["diag_done"], 2 * g + h + 1)
                    pe.matmul(bank(misc, h), ones[:, :], diag[h], start=True, stop=True).then_inc(S["gate_psum"], 1)

            def keep_warm(o, n):
                for _ in range(n):
                    pe.matmul(o[:, 0:P], ones[:, :], ident[:, :], start=True, stop=True, skip_group_check=True)

            def turn(norm):
                n = phases.index(norm)
                for t in range(NT):
                    pe.wait_ge(S["normed_ready"], NT * n + t + 1)
                    for k in range(KB):
                        b = (bank(up, 0), bank(up, 1), bank(misc, 0), bank(misc, 1))[k // 2]
                        o = (k % 2) * SEQ + t * P
                        last = pe.transpose(b[:, o:o + P], normed[:, t * D + k * P:t * D + (k + 1) * P], ident[:, :])
                last.then_inc(S["turned"], 1)

            def ffn(p):
                b = BASE[p]
                def ups(i, it=0):
                    u = count_up(p, i)
                    for j in range(2):
                        s = b + (3 * i - 1 if i else 0) + j
                        slab_ready(s, it)
                        if u:
                            pe.wait_ge(S[("silu_done", "prod_done")[j]], u + 2 * it)
                        col_product(s, bank(up, j), p if (i, j) == (0, 0) else None)

                def down(i, it=0, start=False, stop=False):
                    s = b + (3 * i + 4 if i < FI - 1 else FFN_SLABS - 1)
                    slab_ready(s, it)
                    pe.wait_ge(S["actlo_done"], count_up(p, i) + 1 + 2 * it)
                    row_product(s, act_stat(i), start, stop, last_of_phase=stop)

                v = FIRST_VEC.get(p)
                ups(0)
                ups(1)
                down(0, start=True)
                ups(2)
                down(1)
                with pe.Fori(0, (FI - 3) // 2) as it:
                    for i in (3, 4):
                        ups(i, it)
                        if v is not None and i == 3:
                            ada_sum(v, it)
                        down(i - 1, it)
                if v is not None:
                    pe.wait_ge(S["mod_done"], v + 4)
                gate_spread(p)
                down(FI - 1, stop=True)
                if v is not None:
                    pe.wait_ge(S["gate_done"], phases.index(p) + 1)
                    ada_sum(v + 4)
                    pe.wait_ge(S["mod_done"], v + 5)

            pe.wait_ge(S["c_in"], 32)
            pe.wait_ge(S["const_done"], 1)
            pe.transpose(bank(misc, 0)[:, 0:2 * KB], c_rows[0:2 * KB, :], ident[0:2 * KB, 0:2 * KB]).then_inc(S["c_psum"], 1)
            pe.wait_ge(S["rows_loaded"], 16 * len(rows_plan))
            for n, r in enumerate(tile_rows):
                last = pe.transpose(bank(up, 0)[:, n * P:n * P + r] if n < 4 else bank(up, 1)[:, (n - 4) * P:(n - 4) * P + r],
                                    rows_sb[0:r, n * P:(n + 1) * P], ident[0:r, 0:r])
            last.then_inc(S["cols_psum"], 1)
            for v in range(2):
                ada_sum(v)
            for p in phases:
                if p != phases[0]:
                    keep_warm(bank(up, 0), WARM)
                turn(p)
                keep_warm(bank(dacc, 0), WARM)
                if p in FFNS:
                    ffn(p)
                else:
                    PE_MIX[p](pe, slab_ready, col_product, row_product, operand_stat, ada_sum, gate_spread, token_product)

        @block.scalar
        def _(act):
            link = chain(act, S["act_chain"])

            def split_hi(s, it=0):
                if s >= nslabs:
                    return
                act.wait_ge(raw_full[s % RAW], 32 * (s // RAW + 1) + 32 * it)
                if s >= SPL:
                    act.wait_ge(slab_used, s - SPL + 1 + RAW * it)
                for take, put in split_views(s):
                    last = act.copy(put(slab(hi, s, SPL)), take(slab(raw, s, RAW)))
                last.then_inc(hi_done, 1)

            def norm(name):
                n = norm_list.index(name)
                act.activation(table_col, eps_col, ACT.Sqrt)
                for t in range(NT):
                    if n:
                        act.wait_ge(S["x_done"], x_before(name) - NT + t + 1)
                    elif t == 0:
                        act.wait_ge(S["x_loaded"], 16)
                    act.activation(normed[:, t * D:(t + 1) * D], x[:, t * D:(t + 1) * D], ACT.Square,
                                   accum_out=sumsq[:, t:t + 1]).then_inc(S["sumsq_done"], 1)
                    act.wait_ge(S["sumsq_done"], NT * n + t + 1)
                    act.activation(rstd[:, t:t + 1], sumsq[:, t:t + 1], ACT.Sqrt, scale=1.0 / D,
                                   bias=eps_col).then_inc(S["sqrt_done"], 1)
                if name.endswith("x"):
                    return
                if n == 0:
                    split_hi(0)
                    split_hi(1)
                f = phases.index(name)
                act.wait_ge(S["turned"], f + 1)
                act.wait_ge(S["shifted_d"], 5 * f + 1)
                v = MODS[name]

                def round_chunk(c):
                    act.copy(operand_hi[:, c * 512:(c + 1) * 512],
                             turned32[:, c * 512:(c + 1) * 512]).then_inc(S["operand_hi_done"], 1)

                for h in range(2):
                    ps = (bank(up, 0), bank(misc, 0))[h]
                    for k in (4 * h, 4 * h + 1):
                        act.activation(op_k(turned32, k), ps[:, (k % 2) * SEQ:(k % 2 + 1) * SEQ], ACT.Identity,
                                       scale=a_col[:, k:k + 1],
                                       bias=modcol[:, v[0] * KB + k:v[0] * KB + k + 1]).then_inc(S["shifted_a"], 1)
                    act.wait_ge(S["shifted_a"], 4 * f + 2 * h + 2)
                    round_chunk(2 * h)
                    act.wait_ge(S["shifted_d"], 5 * f + 2 * h + 3)
                    round_chunk(2 * h + 1)

            def gate(p):
                g = phases.index(p)
                act.wait_ge(S["gate_psum"], 2 * g + 2)
                if g:
                    act.wait_ge(S["x_done"], x_count(phases[g - 1]))
                act.activation(gate_row[:, :], misc[:, :], ACT.Copy,
                               scale=0.5 if p[0] == "F" else 1.0).then_inc(S["gate_done"], 1)

            def ffn(p):
                b = BASE[p]
                conv = p[0] == "C"

                def silu(s, i, it=0):
                    u = count_up(p, i)
                    act.wait_ge(slab_used, s + 1 + RAW * it)
                    if u:
                        act.wait_ge(S["prod_done"], u + 2 * it)
                    if not conv:
                        act.activation(silu_sb, bank(up, 0), ACT.Silu).then_inc(S["silu_done"], 1)
                        return
                    for j in range(2):
                        o = slice(j * SEQ, (j + 1) * SEQ)
                        act.activation(silu_sb[:, o], bank(up, 0)[:, o], ACT.Identity, scale=tap(p, 2, i, j, it),
                                       bias=tap(p, 3, i, j, it)).then_inc(S["tap_a"], 1)

                def conv_silu(i, it=0):
                    if conv:
                        act.wait_ge(S["tap_d"], 4 * (count_up(p, i) - 4 * FI) + 4 + 8 * it)
                        act.activation(silu_sb, silu_sb, ACT.Silu).then_inc(S["silu_done"], 1)

                def hidden_hi(i, it=0):
                    act.wait_ge(S["prod_done"], count_up(p, i) + 1 + 2 * it)
                    o = (i % 2) * 2 * SEQ
                    act.copy(act_hi[:, o:o + 2 * SEQ], act32).then_inc(S["acthi_done"], 1)

                def iteration(i, it=0):
                    a = b + 3 * i - 1
                    split_hi(a + 2, it)
                    silu(a, i, it)
                    split_hi(a + 3, it)
                    conv_silu(i, it)
                    split_hi(a + 4, it)
                    hidden_hi(i, it)

                split_hi(b + 2)
                silu(b, 0)
                split_hi(b + 3)
                conv_silu(0)
                hidden_hi(0)
                iteration(1)
                iteration(2)
                with act.Fori(0, (FI - 3) // 2) as it:
                    iteration(3, it)
                    iteration(4, it)
                gate(p)
                split_hi(b + FFN_SLABS + 1)

            def head_norm(inst, gain):
                act.wait_ge(S["hn_sq"], 16 * (inst + 1))
                act.activation(head_ms, head_ms, ACT.Sqrt, scale=1.0 / P, bias=eps_col).then_inc(S["hn_root"], 1)
                for c in range(4):
                    act.wait_ge(S["hn_turned"], 4 * inst + c + 1)
                    act.activation(operand_hi[:, c * 512:(c + 1) * 512], hn_banks[c], ACT.Copy,
                                   scale=gain).then_inc(S["hn_hi"], 1)

            act.wait_ge(S["c_psum"], 1)
            act.activation(c_col, bank(misc, 0)[:, 0:2 * KB], ACT.Silu).then_inc(S["c_ready"], 1)
            for p in phases:
                norm(p)
                if p in FFNS:
                    ffn(p)
                else:
                    ACT_MIX[p](act, link, split_hi, gate, head_norm)
                if p in OUT_ROW:
                    norm(p + "x")

        @block.vector
        def _(dve):
            link = chain(dve, S["dve_chain"])

            def split_lo(s, it=0):
                if s >= nslabs:
                    return
                dve.wait_ge(hi_done, s + 1 + RAW * it)
                for take, put in split_views(s):
                    last = dve.tensor_tensor(put(slab(lo, s, SPL)), take(slab(raw, s, RAW)),
                                             put(slab(hi, s, SPL)).bitcast(F32), ALU.subtract)
                last.then_inc(lo_done, 1)

            def ada_tile(v, k, it=0):
                m = v * KB + k
                t = ada[:, (m % ATILES) * D:(m % ATILES + 1) * D]
                c = c_col[:, (8 if v >= V2 else 0) + k:(8 if v >= V2 else 0) + k + 1]
                if v < 2:
                    dve.wait_ge(ada_first[m % ATILES], 16 * (m // ATILES + 1))
                else:
                    dve.wait_ge(ada_full[m % ATILES], 16 * (m // ATILES + 1 - FIRST_ROUNDS) + 32 * it)
                if k == 0:
                    if v:
                        dve.wait_ge(S["ada_summed"], v + it)
                    dve.tensor_scalar(ada_acc[:, :], t, c, None, ALU.mult).then_inc(S["ada_step"], 1)
                else:
                    dve.wait_ge(S["ada_step"], m + KB * it)
                    dve.scalar_tensor_tensor(ada_acc[:, :], t, c, ada_acc[:, :], ALU.mult,
                                             ALU.add).then_inc(S["ada_step"], 1)

            def mod_vector(v, it=0):
                dve.wait_ge(S["ada_summed"], v + 1 + it)
                if isinstance(it, int):
                    o, b = modcol[:, v * KB:(v + 1) * KB], cols[:, v * KB:(v + 1) * KB]
                else:
                    o, b = modcol[:, bass.ds(it * KB + v * KB, KB)], cols[:, bass.ds(it * KB + v * KB, KB)]
                dve.tensor_tensor(o, bank(misc, 1)[:, 0:KB], b, ALU.add).then_inc(S["mod_done"], 1)

            def norm(name):
                n = norm_list.index(name)

                def root_taken(t):
                    dve.wait_ge(S["sqrt_done"], NT * n + t + 1)
                    link(dve.reciprocal(rstd[:, t:t + 1], rstd[:, t:t + 1]))

                if name.endswith("x"):
                    dve.wait_ge(S["row_in"], 16 * (out_norms.index(name[:-1]) + 1))
                    for t in range(NT):
                        root_taken(t)
                        xt = x[:, t * D:(t + 1) * D]
                        dve.scalar_tensor_tensor(xt, xt, rstd[:, t:t + 1], out_row, ALU.mult,
                                                 ALU.mult).then_inc(S["x_done"], 1)
                    dve.wait_ge(S["x_done"], x_count(name[:-1]) + 2)
                    return
                f = phases.index(name)
                for t in range(NT):
                    root_taken(t)
                    dve.tensor_scalar(normed[:, t * D:(t + 1) * D], x[:, t * D:(t + 1) * D], rstd[:, t:t + 1],
                                      None, ALU.mult).then_inc(S["normed_ready"], 1)
                if n == 0:
                    split_lo(1)
                v = MODS[name]
                dve.wait_ge(S["mod_done"], v[1] + 1)
                g, l = GAIN[name]
                dve.scalar_tensor_tensor(a_col, modcol[:, v[1] * KB:(v[1] + 1) * KB], 1.0, gain_cols(g, l),
                                         ALU.add, ALU.mult).then_inc(S["shifted_d"], 1)
                dve.wait_ge(S["shifted_d"], 5 * f + 1)
                dve.wait_ge(S["turned"], f + 1)
                for h in range(2):
                    ps = (bank(up, 1), bank(misc, 1))[h]
                    for k in (4 * h + 2, 4 * h + 3):
                        dve.tensor_scalar(op_k(turned32, k), ps[:, (k % 2) * SEQ:(k % 2 + 1) * SEQ],
                                          a_col[:, k:k + 1], modcol[:, v[0] * KB + k:v[0] * KB + k + 1],
                                          ALU.mult, ALU.add).then_inc(S["shifted_d"], 1)
                    for c in (2 * h, 2 * h + 1):
                        dve.wait_ge(S["operand_hi_done"], 4 * f + c + 1)
                        o = slice(c * 512, (c + 1) * 512)
                        dve.tensor_tensor(operand_lo[:, o], turned32[:, o], operand_hi[:, o].bitcast(F32),
                                          ALU.subtract).then_inc(S["operand_ready"], 1)

            def residual(p):
                g = phases.index(p)
                dve.wait_ge(S["gate_done"], g + 1)
                for t in range(NT):
                    if t == 0:
                        dve.wait_ge(S["tile_done"], g + 1)
                    else:
                        dve.wait_ge(slab_used, BASE[p] + SLABS_OF.get(p, FFN_SLABS))
                    o = slice(t * D, (t + 1) * D)
                    link(dve.tensor_tensor(resid_tmp[:, o], dacc[:, o], gate_row[:, :], ALU.mult))
                    dve.tensor_tensor(x[:, o], x[:, o], resid_tmp[:, o], ALU.add).then_inc(S["x_done"], 1)
                dve.wait_ge(S["x_done"], x_count(p))

            def ffn(p):
                b = BASE[p]
                conv = p[0] == "C"

                def taps(i, it=0):
                    c = count_up(p, i) - 4 * FI
                    for j in range(2 if conv else 0):
                        dve.wait_ge(S["tap_a"], 2 * c + 2 + 4 * it)
                        g = bank(up, 0)[:, j * SEQ:(j + 1) * SEQ]
                        o = silu_sb[:, j * SEQ:(j + 1) * SEQ]
                        dve.scalar_tensor_tensor(o[:, 1:SEQ], g[:, 0:SEQ - 1], tap(p, 1, i, j, it), o[:, 1:SEQ],
                                                 ALU.mult, ALU.add).then_inc(S["tap_d"], 1)
                        dve.wait_ge(S["tap_d"], 4 * c + 2 * j + 1 + 8 * it)
                        dve.scalar_tensor_tensor(o[:, 2:SEQ], g[:, 0:SEQ - 2], tap(p, 0, i, j, it), o[:, 2:SEQ],
                                                 ALU.mult, ALU.add).then_inc(S["tap_d"], 1)

                def product(s, i, it=0):
                    u = count_up(p, i)
                    dve.wait_ge(slab_used, s + 1 + RAW * it)
                    dve.wait_ge(S["silu_done"], u + 1 + 2 * it)
                    if u:
                        dve.wait_ge(S["actlo_done"], u + 2 * it)
                    dve.tensor_tensor(act32, silu_sb, bank(up, 1), ALU.mult).then_inc(S["prod_done"], 1)

                def hidden_lo(i, it=0):
                    dve.wait_ge(S["acthi_done"], count_up(p, i) + 1 + 2 * it)
                    o = (i % 2) * 2 * SEQ
                    dve.tensor_tensor(act_lo[:, o:o + 2 * SEQ], act32, act_hi[:, o:o + 2 * SEQ].bitcast(F32),
                                      ALU.subtract).then_inc(S["actlo_done"], 1)

                def iteration(i, it=0, vec=None, k0=0, count=(0, 2, 2), summed=None):
                    a = b + 3 * i - 1
                    k = k0

                    def some(n, k):
                        for q in range(n if vec is not None else 0):
                            ada_tile(vec, k + q, it)
                        return k + n
                    split_lo(a + 2, it)
                    taps(i, it)
                    k = some(count[0], k)
                    split_lo(a + 3, it)
                    k = some(count[1], k)
                    product(a + 1, i, it)
                    split_lo(a + 4, it)
                    hidden_lo(i, it)
                    if summed is not None:
                        mod_vector(summed, it)
                    some(count[2], k)

                v = FIRST_VEC.get(p)
                split_lo(b + 2)
                taps(0)
                split_lo(b + 3)
                product(b + 1, 0)
                hidden_lo(0)
                iteration(1, 0, v, 0, (0, 2, 2))
                iteration(2, 0, v, 4, (2, 1, 1))
                with dve.Fori(0, (FI - 3) // 2) as it:
                    iteration(3, it, None if v is None else v + 1, 0, (0, 0, 2), summed=v)
                    iteration(4, it, None if v is None else v + 1, 2, (2, 2, 2))
                split_lo(b + FFN_SLABS + 1)
                residual(p)
                if v is not None:
                    mod_vector(v + 4)

            def head_norm(inst, src, gain, gate=None):
                dve.wait_ge(S["hn_root"], inst + 1)
                link(dve.reciprocal(head_ms, head_ms))
                for c in range(5):
                    if c < 4:
                        o = slice(c * 512, (c + 1) * 512)
                        t = src[:, o].rearrange("p (r e) -> p r e", e=P)
                        ins = dve.tensor_tensor(t, t, head_ms[:, 4 * c:4 * c + 4].unsqueeze(2).to_broadcast([P, 4, P]),
                                                ALU.mult)
                        if gate is not None:
                            link(ins)
                            dve.wait_ge(S["silu_g"], 1)
                            dve.wait_ge(S["g_taken"], 4)
                            ins = dve.tensor_tensor(src[:, o], src[:, o], gate[:, o], ALU.mult)
                        ins.then_inc(S["hn_scaled"], 1)
                    if c:
                        o = slice((c - 1) * 512, c * 512)
                        dve.wait_ge(S["hn_hi"], 4 * inst + c)
                        dve.scalar_tensor_tensor(operand_lo[:, o], hn_banks[c - 1], gain, operand_hi[:, o].bitcast(F32),
                                                 ALU.mult, ALU.subtract).then_inc(S["operand_ready"], 1)

            dve.wait_ge(S["c_ready"], 1)
            for k in range(KB):
                ada_tile(0, k)
            dve.wait_ge(S["cols_psum"], 1)
            for t in range(6):
                r = tile_rows[t]
                ps = bank(up, 0)[:, t * P:t * P + r] if t < 4 else bank(up, 1)[:, (t - 4) * P:(t - 4) * P + r]
                link(dve.tensor_copy(cols[:, t * P:t * P + r], ps))
            link(dve.tensor_copy(qk_gain[:, 1:2], cols[:, 2 * P + 99:2 * P + 100]))
            link(dve.tensor_scalar(head_gain, cols[:, 2 * P + 96:2 * P + 97], 1.0 - LAMBDA_INIT, None, ALU.mult))
            link(dve.tensor_scalar(qk_gain[:, 0:1], cols[:, 2 * P + 98:2 * P + 99], float(NSA_HD) ** -0.5, None,
                                   ALU.mult))
            mod_vector(0)
            for k in range(KB):
                ada_tile(1, k)
            split_lo(0)
            mod_vector(1)
            for p in phases:
                norm(p)
                if p in FFNS:
                    ffn(p)
                else:
                    DVE_MIX[p](dve, link, split_lo, ada_tile, mod_vector, residual, head_norm)
                if p in OUT_ROW:
                    norm(p + "x")


def kernel(**inputs):
    import numpy as _np
    import concourse.bacc as _bacc
    from concourse import mybir as _mybir
    from concourse.bass_utils import run_bass_kernel_spmd as _run

    nc = _bacc.Bacc("TRN2", target_bir_lowering=False, num_devices=1)
    arrays, tensors = {}, {}
    for name, value in inputs.items():
        a = _np.ascontiguousarray(value)
        arrays[f"in_{name}_dram"] = a
        tensors[name] = nc.dram_tensor(f"in_{name}_dram", a.shape, _mybir.dt.from_np(a.dtype),
                                       kind="ExternalInput").ap()
    out = nc.dram_tensor("out_0_dram", (1, SEQ, D), F32, kind="ExternalOutput").ap()
    build(nc, tensors, out)
    r = _run(nc, [arrays], core_ids=[0])
    return r.results[0]["out_0_dram"]
```
